# Optimizing a Trainium2 kernel written in Bass

```python
import math
import jax, jax.numpy as jnp
from jax import lax
import numpy as np

D_MODEL = 1024
BATCH = 1
SEQ = 256
DEPTH = 1

EPS = 1e-5
HYENA_WIDTH = D_MODEL // 2
SHORT_CONV = 3
FILTER_EMB_DIM = 17
FILTER_BANDS = (FILTER_EMB_DIM - 1) // 2
FILTER_HIDDEN = 64
DECAY_TARGET = 1e-2
FAST_DECAY_PCT = 0.3
SLOW_DECAY_PCT = 1.5
ATTN_HEADS = 4
ATTN_HEAD_DIM = 64
ATTN_V_DIM = 2 * ATTN_HEAD_DIM
ATTN_WIDTH = ATTN_HEADS * ATTN_V_DIM
Q_BLOCK = 128
N_BRANCHES = 2
IN_COLS = 3 * HYENA_WIDTH + 3 * ATTN_WIDTH + N_BRANCHES * D_MODEL
N_EXPERTS = 32
TOP_K = 4
D_EXPERT = D_MODEL
SWIGLU_LIMIT = 7.0
SWIGLU_ALPHA = 1.702
EXPERT_BLOCK = 256

kernel_name = "hybrid_hyena_diffattn_moe_adaln"

def rms_norm(x, g):
    xf = x.astype(jnp.float32)
    y = xf * lax.rsqrt(jnp.mean(xf * xf, axis=-1, keepdims=True) + EPS)
    return (y * g.astype(jnp.float32)).astype(x.dtype)

def short_conv(u, w, b):
    L = u.shape[1]
    up = jnp.pad(u, ((0, 0), (1, 1), (0, 0)))
    return up[:, :L] * w[0] + up[:, 1:L + 1] * w[1] + up[:, 2:] * w[2] + b

def implicit_filters(L, w1, b1, w2, b2, w3, b3, w4, freq):
    f32 = jnp.float32
    t = jnp.linspace(0.0, 1.0, L, dtype=f32)[:, None]
    w = 2.0 * math.pi * jnp.arange(L, dtype=f32)[:, None] / L
    fr = jnp.linspace(1e-4, FILTER_BANDS - 1, FILTER_BANDS, dtype=f32)[None, :]
    z = jnp.concatenate([t, jnp.cos(fr * w), -jnp.sin(fr * w)], axis=-1)
    fq = freq.astype(f32)
    h = jnp.sin(fq * (z @ w1.astype(f32) + b1.astype(f32)))
    h = jnp.sin(fq * (h @ w2.astype(f32) + b2.astype(f32)))
    h = jnp.sin(fq * (h @ w3.astype(f32) + b3.astype(f32)))
    k = h @ w4.astype(f32)
    min_decay = math.log(DECAY_TARGET) / SLOW_DECAY_PCT
    max_decay = math.log(DECAY_TARGET) / FAST_DECAY_PCT
    deltas = jnp.linspace(min_decay, max_decay, HYENA_WIDTH, dtype=f32)
    decay = jnp.exp(-t * jnp.abs(deltas))
    k = k.reshape(L, 2, HYENA_WIDTH) * decay[:, None, :]
    return k[:, 0], k[:, 1]

def two_sided_long_conv(v, k_fwd, k_bwd):
    B, L, C = v.shape
    k_full = jnp.concatenate([k_fwd, jnp.zeros((1, C), jnp.float32), k_bwd[1:][::-1]], axis=0)
    kf = jnp.fft.rfft(k_full, n=2 * L, axis=0)
    vf = jnp.fft.rfft(v.astype(jnp.float32), n=2 * L, axis=1)
    y = jnp.fft.irfft(vf * kf[None], n=2 * L, axis=1)[:, :L]
    return y.astype(v.dtype)

def hyena_branch(u3, conv_w, conv_b, k_fwd, k_bwd, d_skip):
    uc = short_conv(u3, conv_w, conv_b)
    x0, x1, v = jnp.split(uc, 3, axis=-1)
    v = v * x1
    y = two_sided_long_conv(v, k_fwd, k_bwd) + v * d_skip
    return y * x0

def diff_attention(q, k, v, lam, lam_init, subln_g):
    B, L = q.shape[0], q.shape[1]
    nb = L // Q_BLOCK
    scale = 1.0 / math.sqrt(ATTN_HEAD_DIM)
    slopes = 2.0 ** (-8.0 * jnp.arange(1, ATTN_HEADS + 1, dtype=jnp.float32) / ATTN_HEADS)
    pos = jnp.arange(L, dtype=jnp.float32)
    kf = k.astype(jnp.float32)
    vf = v.astype(jnp.float32)
    qb = q.astype(jnp.float32).reshape(B, nb, Q_BLOCK, ATTN_HEADS, 2, ATTN_HEAD_DIM).transpose(1, 0, 2, 3, 4, 5)
    qpos = pos.reshape(nb, Q_BLOCK)

    def block(args):
        q_blk, q_pos = args
        s = jnp.einsum('bqhcd,bkhcd->bhcqk', q_blk, kf) * scale
        dist = jnp.abs(q_pos[:, None] - pos[None, :])
        s = s - slopes[None, :, None, None, None] * dist[None, None, None]
        p = jax.nn.softmax(s, axis=-1)
        a = p[:, :, 0] - lam * p[:, :, 1]
        return jnp.einsum('bhqk,bkhe->bqhe', a, vf)

    out = lax.map(block, (qb, qpos))
    out = out.transpose(1, 0, 2, 3, 4).reshape(B, L, ATTN_HEADS, ATTN_V_DIM)
    out = rms_norm(out, subln_g) * (1.0 - lam_init)
    return out.reshape(B, L, ATTN_WIDTH).astype(q.dtype)

def moe_ffn(h, w_router, b_router, w_gate_up, b_gate_up, w_down, b_down):
    B, L, D = h.shape
    T = B * L
    hf = h.reshape(T, D)
    logits = (hf @ w_router + b_router).astype(jnp.float32)
    top_val, top_idx = lax.top_k(logits, TOP_K)
    gates = jax.nn.softmax(top_val, axis=-1)
    P = T * TOP_K
    flat_e = top_idx.reshape(P)
    order = jnp.argsort(flat_e)
    e_sorted = flat_e[order]
    tok_sorted = (order // TOP_K).astype(jnp.int32)
    w_sorted = gates.reshape(P)[order]
    counts = jnp.zeros((N_EXPERTS,), jnp.int32).at[flat_e].add(1)
    padded = ((counts + EXPERT_BLOCK - 1) // EXPERT_BLOCK) * EXPERT_BLOCK
    pad_end = jnp.cumsum(padded)
    pad_start = pad_end - padded
    raw_start = jnp.cumsum(counts) - counts
    rank = jnp.arange(P, dtype=jnp.int32) - raw_start[e_sorted]
    dest = pad_start[e_sorted] + rank
    n_blocks = -(-P // EXPERT_BLOCK) + N_EXPERTS
    n_rows = n_blocks * EXPERT_BLOCK
    row_tok = jnp.zeros((n_rows,), jnp.int32).at[dest].set(tok_sorted)
    row_w = jnp.zeros((n_rows,), jnp.float32).at[dest].set(w_sorted)
    block_start = jnp.arange(n_blocks, dtype=jnp.int32) * EXPERT_BLOCK
    block_expert = jnp.minimum(jnp.searchsorted(pad_end, block_start, side='right'), N_EXPERTS - 1)

    def expert_block(args):
        toks, wts, e = args
        xb = hf[toks]
        gu = xb @ w_gate_up[e] + b_gate_up[e]
        gate, up = gu[:, :D_EXPERT], gu[:, D_EXPERT:]
        gate = jnp.minimum(gate, SWIGLU_LIMIT)
        up = jnp.clip(up, -SWIGLU_LIMIT, SWIGLU_LIMIT)
        glu = gate * jax.nn.sigmoid(SWIGLU_ALPHA * gate)
        y = ((up + 1.0) * glu) @ w_down[e] + b_down[e]
        return y * wts[:, None].astype(y.dtype)

    ys = lax.map(expert_block, (row_tok.reshape(n_blocks, EXPERT_BLOCK),
                                row_w.reshape(n_blocks, EXPERT_BLOCK), block_expert))
    out = jnp.zeros((T, D), h.dtype).at[row_tok].add(ys.reshape(n_rows, D).astype(h.dtype))
    return out.reshape(B, L, D)

def setup_inputs(seed: int = 0) -> dict:
    key = jax.random.key(seed)
    ks = jax.random.split(key, 32)
    f32 = jnp.float32
    D, HW, E, DE, FH = D_MODEL, HYENA_WIDTH, N_EXPERTS, D_EXPERT, FILTER_HIDDEN
    n = lambda k, shape, s: (jax.random.normal(k, shape, f32) * s)
    return {
        "x": n(ks[0], (BATCH, SEQ, D), 1.0),
        "c": n(ks[1], (BATCH, D), 1.0),
        "w_ada": n(ks[2], (DEPTH, D, 6 * D), 0.5 * D ** -0.5),
        "b_ada": n(ks[3], (DEPTH, 6 * D), 0.02),
        "norm_mix_g": 1.0 + n(ks[4], (DEPTH, D), 0.02),
        "w_in": n(ks[5], (DEPTH, D, IN_COLS), D ** -0.5),
        "b_in": n(ks[6], (DEPTH, IN_COLS), 0.02),
        "hy_conv_w": n(ks[7], (DEPTH, SHORT_CONV, 3 * HW), SHORT_CONV ** -0.5),
        "hy_conv_b": n(ks[8], (DEPTH, 3 * HW), 0.02),
        "filt_w1": n(ks[9], (DEPTH, FILTER_EMB_DIM, FH), FILTER_EMB_DIM ** -0.5),
        "filt_b1": n(ks[10], (DEPTH, FH), 0.02),
        "filt_w2": n(ks[11], (DEPTH, FH, FH), FH ** -0.5),
        "filt_b2": n(ks[12], (DEPTH, FH), 0.02),
        "filt_w3": n(ks[13], (DEPTH, FH, FH), FH ** -0.5),
        "filt_b3": n(ks[14], (DEPTH, FH), 0.02),
        "filt_w4": n(ks[15], (DEPTH, FH, 2 * HW), 0.2 * FH ** -0.5),
        "filt_freq": 1.0 + n(ks[16], (DEPTH, FH), 0.02),
        "hy_d_skip": n(ks[17], (DEPTH, HW), 1.0),
        "lambda_qk": n(ks[18], (DEPTH, 4, ATTN_HEAD_DIM), 0.1),
        "attn_subln_g": 1.0 + n(ks[19], (DEPTH, ATTN_V_DIM), 0.02),
        "w_hy_out": n(ks[20], (DEPTH, HW, D), HW ** -0.5),
        "w_attn_out": n(ks[21], (DEPTH, ATTN_WIDTH, D), ATTN_WIDTH ** -0.5),
        "w_mix_out": n(ks[22], (DEPTH, D, D), D ** -0.5),
        "norm_ffn_g": 1.0 + n(ks[23], (DEPTH, D), 0.02),
        "w_router": n(ks[24], (DEPTH, D, E), D ** -0.5),
        "b_router": n(ks[25], (DEPTH, E), 0.01),
        "w_gate_up": n(ks[26], (DEPTH, E, D, 2 * DE), D ** -0.5),
        "b_gate_up": n(ks[27], (DEPTH, E, 2 * DE), 0.01),
        "w_down": n(ks[28], (DEPTH, E, DE, D), DE ** -0.5),
        "b_down": n(ks[29], (DEPTH, E, D), 0.01),
        "final_norm_g": 1.0 + n(ks[30], (D,), 0.02),
    }

def reference(x, c, w_ada, b_ada, norm_mix_g, w_in, b_in, hy_conv_w, hy_conv_b,
              filt_w1, filt_b1, filt_w2, filt_b2, filt_w3, filt_b3, filt_w4, filt_freq,
              hy_d_skip, lambda_qk, attn_subln_g, w_hy_out, w_attn_out, w_mix_out,
              norm_ffn_g, w_router, b_router, w_gate_up, b_gate_up, w_down, b_down,
              final_norm_g):
    B, L, D = x.shape
    split_idx = [3 * HYENA_WIDTH, 3 * HYENA_WIDTH + ATTN_WIDTH,
                 3 * HYENA_WIDTH + 2 * ATTN_WIDTH, 3 * HYENA_WIDTH + 3 * ATTN_WIDTH]
    for l in range(DEPTH):
        lam_init = 0.8 - 0.6 * math.exp(-0.3 * l)
        mod = jax.nn.silu(c) @ w_ada[l] + b_ada[l]
        shift1, scale1, gate1, shift2, scale2, gate2 = jnp.split(mod[:, None, :], 6, axis=-1)

        h = rms_norm(x, norm_mix_g[l]) * (1.0 + scale1) + shift1
        u = h @ w_in[l] + b_in[l]
        u_hy, q, k, v, g = jnp.split(u, split_idx, axis=-1)

        k_fwd, k_bwd = implicit_filters(L, filt_w1[l], filt_b1[l], filt_w2[l], filt_b2[l],
                                        filt_w3[l], filt_b3[l], filt_w4[l], filt_freq[l])
        y_hy = hyena_branch(u_hy, hy_conv_w[l], hy_conv_b[l], k_fwd, k_bwd, hy_d_skip[l])

        lq = lambda_qk[l].astype(jnp.float32)
        lam = jnp.exp(jnp.sum(lq[0] * lq[1])) - jnp.exp(jnp.sum(lq[2] * lq[3])) + lam_init
        q = q.reshape(B, L, ATTN_HEADS, 2, ATTN_HEAD_DIM)
        k = k.reshape(B, L, ATTN_HEADS, 2, ATTN_HEAD_DIM)
        v = v.reshape(B, L, ATTN_HEADS, ATTN_V_DIM)
        y_at = diff_attention(q, k, v, lam, lam_init, attn_subln_g[l])

        gts = jax.nn.sigmoid(g.reshape(B, L, N_BRANCHES, D))
        merged = gts[:, :, 0] * (y_hy @ w_hy_out[l]) + gts[:, :, 1] * (y_at @ w_attn_out[l])
        x = x + gate1 * (merged @ w_mix_out[l])

        h = rms_norm(x, norm_ffn_g[l]) * (1.0 + scale2) + shift2
        x = x + gate2 * moe_ffn(h, w_router[l], b_router[l], w_gate_up[l], b_gate_up[l],
                                w_down[l], b_down[l])
    return rms_norm(x, final_norm_g)


_drawn_inputs = setup_inputs


def setup_inputs(seed=0):
    import zlib

    import numpy as np

    out = dict(_drawn_inputs(seed))
    spreads = {}
    factors = {'norm_mix_g': 4.453,
     'b_in': 3.666,
     'hy_conv_b': 4.988,
     'filt_b1': 6.622,
     'filt_b2': 8.0,
     'filt_b3': 6.251,
     'filt_freq': 6.417,
     'attn_subln_g': 178.699,
     'norm_ffn_g': 29.92,
     'b_router': 35.92,
     'b_gate_up': 183.743,
     'b_down': 200.0,
     'final_norm_g': 21.405,
     'lambda_qk': 4.197}
    for name, (base, spread) in spreads.items():
        noise = np.random.default_rng([zlib.crc32(name.encode()), seed]).standard_normal(out[name].shape)
        drawn = base * np.exp(spread * noise) if base else spread * noise
        out[name] = __import__('jax').numpy.asarray(drawn.astype(out[name].dtype))
    for name, factor in factors.items():
        out[name] = (out[name] * factor).astype(out[name].dtype)
    return out
```

```python
import math
from contextlib import ExitStack

import concourse.bass as bass
from concourse import mybir

F32 = mybir.dt.float32
I32 = mybir.dt.int32
ALU = mybir.AluOpType
ACT = mybir.ActivationFunctionType
AX = mybir.AxisListType

P = 128
D = 1024
L = 256
TT = L // P
KD = D // P
HW = 512
CT = HW // P
HEADS = 4
E = 32
TOPK = 4
FE = 1024
SLOTS = 64
ITEMS = 48
EXTRA = ITEMS - E
EPS = 1e-5
LAM_INIT = 0.2
SLOPES = [2.0 ** (-8.0 * (h + 1) / HEADS) for h in range(HEADS)]
TWO_PI = 2.0 * math.pi

TAB = {}
_at = 0
for _name, _w in (("ident", P), ("tri", P), ("iota", P), ("ones", P), ("lane", 1), ("erev", E), ("odd", 8), ("quad", E),
                  ("item", ITEMS), ("dist", TT * L)):
    TAB[_name] = (_at, _w)
    _at += _w
TABW = _at


def host_tables():
    import numpy as np
    t = np.arange(L)
    f = np.arange(L)
    ang = 2.0 * np.pi * np.outer(t, f) / (2 * L)
    dft = np.concatenate([np.cos(ang), np.sin(ang)], axis=1)
    dft[:, L] = np.cos(np.pi * t)
    wt = np.full(2 * L, 2.0)
    wt[0] = wt[L] = 1.0
    inv = (dft * wt[None, :] / (2 * L)).T
    tl = np.linspace(0.0, 1.0, L, dtype=np.float32)[:, None]
    w = (np.float32(2.0 * math.pi) * np.arange(L, dtype=np.float32)[:, None] / np.float32(L)).astype(np.float32)
    fr = np.linspace(1e-4, 7, 8, dtype=np.float32)[None, :]
    z = np.concatenate([tl, np.cos(fr * w), -np.sin(fr * w)], axis=1)
    deltas = np.linspace(math.log(1e-2) / 1.5, math.log(1e-2) / 0.3, HW, dtype=np.float32)
    decay = np.exp(-tl * np.abs(deltas))
    back = decay.copy()
    back[0] = 0.0
    tab = np.zeros((P, TABW), np.float32)
    put = lambda n, v: tab.__setitem__((slice(None), slice(TAB[n][0], TAB[n][0] + TAB[n][1])), v)
    r = np.arange(P)
    put("ident", np.eye(P))
    put("tri", (r[:, None] < r[None, :]).astype(np.float32))
    put("iota", r[None, :])
    put("ones", 1.0)
    put("lane", r[:, None])
    put("erev", E - np.arange(E)[None, :])
    put("odd", 1 + 2 * np.arange(8)[None, :])
    put("quad", (r[:, None] % E == np.arange(E)[None, :]).astype(np.float32))
    put("item", np.arange(ITEMS)[None, :])
    dist = np.abs(np.arange(L)[:, None] - np.arange(L)[None, :]).reshape(TT, P, L)
    put("dist", dist.transpose(1, 0, 2).reshape(P, TT * L))
    c = lambda a: np.ascontiguousarray(a, np.float32)
    return {"t_small": tab, "t_dft": c(dft), "t_inv": c(inv), "t_z": c(z.T),
            "t_decay": c(np.stack([decay, back]))}


def build(nc, a, out):
    with ExitStack() as ctx:
        regions = {}
        top = [0]

        def region(name, words):
            regions[name] = (top[0], words)
            top[0] += words

        for name, words in (
                ("ring", 24576), ("x", 2048), ("xn", 2048), ("ht", 2048), ("ur", 12 * 258), ("uc", 3072),
                ("kf", 2560), ("dft", 1024), ("inv", 1024), ("qm", 2048), ("kt", 1024), ("ve", 1024),
                ("sc", 1024), ("ab", 512), ("at", 512), ("on", 512), ("adr", 1536),
                ("tab", TABW), ("prm", 128), ("prmT", 128), ("lam", 256), ("bv", 512), ("br", 32),
                ("cs", 256), ("modc", 48), ("tiny", 886)):
            region(name, words)
        arena = ctx.enter_context(nc.sbuf_tensor("arena", [P, top[0]], F32))
        table_i = ctx.enter_context(nc.sbuf_tensor("table_i", [1, 64], I32))
        ps = ctx.enter_context(nc.psum_tensor("ps", [P, 8, 512], F32))

        def at(name, off=0, words=None):
            o, w = regions[name]
            words = w - off if words is None else words
            assert off + words <= w, name
            return arena[:, o + off:o + off + words]

        def tab(name):
            o, w = TAB[name]
            return at("tab", o, w)

        ident, tri, iota, ones, lane = tab("ident"), tab("tri"), tab("iota"), tab("ones"), tab("lane")
        dist = tab("dist").rearrange("p (q k) -> p q k", q=TT)

        ring = [at("ring", 4096 * s, 4096) for s in range(6)]
        gu_slot = [at("ring", 2048 * k, 2048) for k in range(KD)]
        dn_slot = [at("ring", 2048 * (KD + c), 2048).rearrange("p (q n) -> p q n", q=2) for c in range(4)]

        x = at("x").rearrange("p (t d) -> p t d", t=TT)
        xn = at("xn").rearrange("p (t d) -> p t d", t=TT)
        gate_hy = at("xn").rearrange("p (c t) -> p c t", c=KD)
        hT = at("ht").rearrange("p (k t) -> p k t", k=KD)
        uraw = at("ur").rearrange("p (c t) -> p c t", c=12)
        Y = at("ur", 0, 2048).rearrange("p (f c) -> p f c", f=4)
        vtc = at("ur", 2048, 1024).rearrange("p (t c) -> p t c", t=TT)
        merged = at("ur", 0, 2048).rearrange("p (c t) -> p c t", c=KD)
        ucv = at("uc").rearrange("p (c t) -> p c t", c=12)
        x0T, x1T, vT = ucv[:, 0:4], ucv[:, 4:8], ucv[:, 8:12]
        y_hyT, y_atT = x0T, x1T
        gate_at = [ucv[:, 8 + i, :] if i < 4 else at("ur", 2048 + 256 * (i - 4), 256) for i in range(KD)]
        w4 = at("ur", 0, 1024)
        kplus = at("ur", 1024, 1024).rearrange("p (t c) -> p t c", t=TT)
        kback = at("on")
        kminus = at("uc", 2048, 1024).rearrange("p (t c) -> p t c", t=TT)
        decay = at("uc", 0, 2048).rearrange("p (s t c) -> p s t c", s=2, t=TT)
        kA = at("kf", 0, 1024).rearrange("p (f c) -> p f c", f=2)
        kN = at("kf", 1024, 512)
        kB = at("kf", 1536, 1024).rearrange("p (f c) -> p f c", f=2)
        dft = at("dft").rearrange("p (t f) -> p t f", t=TT)
        inv = at("inv").rearrange("p (f t) -> p f t", f=4)
        qm = at("qm").rearrange("p (h c t) -> p h c t", h=HEADS, c=2)
        kT = at("kt").rearrange("p (h t) -> p h t", h=HEADS)
        ve = at("ve").rearrange("p (t e) -> p t e", t=TT)
        sc = [at("sc", 512 * j, 512).rearrange("p (c k) -> p c k", c=2) for j in range(2)]
        flat = [at("sc", 512 * j, 512) for j in range(2)]
        ab = [at("ab", 256 * j, 256) for j in range(2)]
        aT = [at("at", 256 * j, 256).rearrange("p (k q) -> p k q", k=TT) for j in range(2)]
        on = at("on")
        adr = [at("adr", 512 * g, 512) for g in range(3)]
        gain = at("at")
        prm, prmT = at("prm"), at("prmT")
        cs = at("cs").rearrange("p (k r) -> p k r", k=KD)
        wr = at("lam").rearrange("p (k e) -> p k e", k=KD)
        modc = at("modc").rearrange("p (g q j) -> p g q j", g=3, q=4)
        gate1B = at("dft")
        gate2B, fgB = at("qm", 0, 1024), at("qm", 1024, 1024)
        shB, gsB = at("kt"), at("ve")
        sel_bias = at("kf", 0, 2048)
        b_down = at("inv")

        tiny_at = [0]

        def tiny(words):
            o = tiny_at[0]
            tiny_at[0] += words
            return at("tiny", o, words)

        ss, rs = tiny(2), tiny(2)
        lamcol, lam2, negm, sums, rinv, rlam = tiny(1), tiny(2), tiny(4), tiny(4), tiny(4), tiny(2)
        oss, ors, nwt = tiny(4), tiny(4), tiny(8)
        log = tiny(64).rearrange("p (t e) -> p t e", t=TT)
        oh = tiny(256).rearrange("p (k t e) -> p k t e", k=TOPK, t=TT)
        wrk = tiny(64).rearrange("p (t e) -> p t e", t=TT)
        topv = tiny(8).rearrange("p (k t) -> p k t", k=TOPK)
        km = tiny(2)
        gexp = tiny(8).rearrange("p (k t) -> p k t", k=TOPK)
        gsum, gden = tiny(2), tiny(2)
        gk = tiny(8).rearrange("p (k t) -> p k t", k=TOPK)
        pk = tiny(8).rearrange("p (k t) -> p k t", k=TOPK)
        M = tiny(64).rearrange("p (t e) -> p t e", t=TT)
        G = tiny(64).rearrange("p (t e) -> p t e", t=TT)
        nov, exc, inc, tmpe = tiny(32), tiny(48), tiny(32), tiny(32)
        cntT = at("prm")
        ef = tiny(ITEMS)
        ohI = tiny(ITEMS + 2)
        pairs_f = tiny(2)
        
        cmpI = at("ab").rearrange("p (i e) -> p i e", i=EXTRA)
        pos_k = at("sc", 0, 256).rearrange("p (k t e) -> p k t e", k=TOPK, t=TT)
        part = at("sc", 512, 256)
        wrk2 = at("sc", 768, 64).rearrange("p (t e) -> p t e", t=TT)
        cntT2 = at("sc", 256, 128)
        GT = at("at", 0, 256)
        hTp = at("ht", 0, 1024).rearrange("p (k s) -> p k s", k=KD)
        Sel = at("ht", 1024, 256).rearrange("p (t s) -> p t s", t=TT)
        Wt = at("ht", 1280, 256).rearrange("p (t s) -> p t s", t=TT)
        Wtmp = at("ht", 1536, 256).rearrange("p (t s) -> p t s", t=TT)
        Pw = at("ht", 1792, 256).rearrange("p (t q) -> p t q", t=TT)
        y = at("ur", 0, 1024)
        actT = at("ur", 1024, 512).rearrange("p (j s) -> p j s", j=4)
        act_o, g_sb = at("ur", 1536, 512), at("ur", 2048, 512)
        u_sb, s_sb, t_sb = at("uc", 0, 512), at("uc", 512, 512), at("uc", 1024, 512)
        mask = at("cs", 0, 128).rearrange("p (i s) -> p i s", i=2)
        fin = at("xn").rearrange("p (t d) -> p t d", t=TT)

        zT = at("sc", 0, 256)
        w1, w2, w3 = at("sc", 256, 64), at("sc", 320, 64), at("sc", 384, 64)
        hid = at("qm", 0, 256)
        ang, turns = at("kt", 0, 256), at("kt", 256, 256)

        C_C, C_BHY, C_BQ, C_BK, C_BG, C_W, C_CB, C_DS, C_SG, C_F = 0, 8, 20, 24, 28, 44, 80, 92, 96, 97

        def col(c, p0=0, p1=P):
            return prmT[p0:p1, c:c + 1]

        def sem(name):
            return ctx.enter_context(nc.semaphore(name))

        names = """tab_in x_in prm_in filt_in decay_in dft_in inv_in ada_in lam_in bv_in br_in wr_in gain_in
            gub_in bd_in fg_in gub_zero out_done
            prm_zero qm_zero pad_zero prmT_ps prmT_sb sig_c silu_c
            f1_ps f2_ps f3_ps f4_ps ang_1 ang_2 ang_3 hid_1 hid_2 hid_3 filt_sb
            x_sq xn_rdy xT_ps ada_used ada0_sb ada1_sb ada2_sb mc0_ps mc1_ps mc2_ps
            mc0_sb mc1_sb mc2_sb h1_sb kA_ps kN_ps kB0_ps kB1_ps kA_sb kN_sb kB0_sb kf_done
            u_ps u_sb v_sb vT_rdy vt_ps vt_sb V_ps Y_rdy yT_ps yhy_rdy lam_a lam_e
            s_ps s_sb negm_rdy exp_done a_rdy aT_ps aT_sb o_ps o_sq on_rdy oT_ps oT_sb
            g1_ps g1_sb pj_ps pj_sb gat_rdy mix_ps x1_rdy x2_rdy x1_sq xn2_rdy x2T_ps bc_ps bc_sb h2T_sb part_ps part_sb log_ps
            top_rdy top_exp m_rdy rank_ps cnt_sb nov_rdy ex_ps g_all gt_ps gt_sb tables h2_rdy
            gu_used dn_used tr_done sc_done ga_done pt_done
            g_rdy sig_rdy act_rdy actT_rdy y_rdy ga_sb pt_sb sel_rdy wt_rdy mask_rdy
            fin_sq fin_rdy dve_step act_step dve_loop act_end pool_step""".split()
        S = {n: sem(n) for n in names}
        s_front = [sem(f"front_in{j}") for j in range(6)]
        s_gu = [sem(f"gate_up_in{k}") for k in range(KD)]
        s_dn = [sem(f"down_in{c}") for c in range(4)]

        class Steps:

            def __init__(self, eng, s, base=0):
                self.eng, self.s, self.base, self.n = eng, s, base, 0

            def __call__(self, ins):
                ins.then_inc(self.s, 1)
                self.n += 1
                self.eng.wait_ge(self.s, self.base + self.n)

        def sig(eng, ins, name, value):
            ins.then_inc(S[name], 1)
            eng.wait_ge(S[name], value)

        w_ada, w_in = a["w_ada"], a["w_in"]
        blocks = [("ada", 0, j) for j in range(4)]
        for j in range(6):
            blocks += [("in", j, 0)] + ([("ada", 1, j)] if j < 4 else [("ada", 2, 2 * j - 8), ("ada", 2, 2 * j - 7)])
        blocks += [("in", j, 0) for j in range(6, 10)] + [("hy", 0, 0), ("att", 0, 0), ("mix", 0, 0), ("mix", 1, 0)]
        where = {b: n for n, b in enumerate(blocks)}

        def block_source(b):
            kind, i, j = b
            if kind == "ada":
                return w_ada[0, 256 * j:256 * (j + 1), 2048 * i:2048 * (i + 1)].rearrange("(k p) n -> p k n", p=P)
            if kind == "in":
                return w_in[0, :, 512 * i:512 * (i + 1)].rearrange("(k p) n -> p k n", p=P)
            if kind == "hy":
                return a["w_hy_out"][0].rearrange("(k p) n -> p k n", p=P)
            if kind == "att":
                return a["w_attn_out"][0].rearrange("(k p) n -> p k n", p=P)
            return a["w_mix_out"][0, 512 * i:512 * (i + 1), :].rearrange("(k p) n -> p k n", p=P)

        def block_view(b):
            kind = b[0]
            k = {"ada": 2, "in": 8, "hy": 4, "att": 4, "mix": 4}[kind]
            return ring[where[b] % 6].rearrange("p (k n) -> p k n", k=k)

        w_gu, w_dn = a["w_gate_up"], a["w_down"]
        block = ctx.enter_context(nc.Block())

        @block.sync
        def _(sp):
            def wait_used(b):
                kind, i, j = b
                if kind == "ada":
                    sp.wait_ge(S["ada_used"], 4 * i + j + 1)
                elif kind == "in":
                    sp.wait_ge(S["u_ps"], 2 * i + 2)
                elif kind == "mix":
                    sp.wait_ge(S["mix_ps"], i + 2)
                else:
                    sp.wait_ge(S["pj_ps"], KD)

            sp.dma_start(at("tab"), a["t_small"]).then_inc(S["tab_in"], 16)
            sp.wait_ge(S["prm_zero"], 1)
            rows = lambda v: v.rearrange("(r n) -> r n", n=P)
            pieces = [(C_C, 8, rows(a["c"][0])), (C_BHY, 20, rows(a["b_in"][0, 0:2560])),
                      (C_BG, 16, rows(a["b_in"][0, 3072:5120])),
                      (C_W, 12, rows(a["hy_conv_w"][0, 0])), (C_W + 12, 12, rows(a["hy_conv_w"][0, 1])),
                      (C_W + 24, 12, rows(a["hy_conv_w"][0, 2])), (C_CB, 12, rows(a["hy_conv_b"][0])),
                      (C_DS, 4, rows(a["hy_d_skip"][0])), (C_SG, 1, a["attn_subln_g"])]
            for r0, n, src in pieces:
                sp.dma_start(prm[r0:r0 + n, :], src).then_inc(S["prm_in"], 16)
            for r, name in ((C_F, "filt_b1"), (C_F + 1, "filt_b2"), (C_F + 2, "filt_b3"), (C_F + 3, "filt_freq")):
                sp.dma_start(prm[r:r + 1, 0:64], a[name]).then_inc(S["prm_in"], 16)
            for dst, name in ((zT[0:17, :], a["t_z"]), (w1[0:17, :], a["filt_w1"][0]), (w2[0:64, :], a["filt_w2"][0]),
                              (w3[0:64, :], a["filt_w3"][0]), (w4[0:64, :], a["filt_w4"][0])):
                sp.dma_start(dst, name).then_inc(S["filt_in"], 16)
            sp.dma_start(x, a["x"][0].rearrange("(t p) d -> p t d", p=P)).then_inc(S["x_in"], 16)
            for n, b in enumerate(blocks):
                if n >= 6:
                    wait_used(blocks[n - 6])
                sp.dma_start(block_view(b), block_source(b)).then_inc(s_front[n % 6], 16)

            def gate_up(k, expert):
                sp.dma_start(gu_slot[k], w_gu[0, expert, k * P:(k + 1) * P, :]).then_inc(s_gu[k], 16)

            def down(c, expert):
                sp.dma_start(dn_slot[c], w_dn[0, expert, c * 256:(c + 1) * 256, :].rearrange("(q p) n -> p q n", p=P))\
                    .then_inc(s_dn[c], 16)

            def gate_up_dyn(k, e):
                sp.dma_start(gu_slot[k], w_gu[0, bass.ds(e, 1), k * P:(k + 1) * P, :].rearrange("o p n -> p (o n)"))\
                    .then_inc(s_gu[k], 16)

            def down_dyn(c, e):
                sp.dma_start(dn_slot[c], w_dn[0, bass.ds(e, 1), c * 256:(c + 1) * 256, :]
                             .rearrange("o (q p) n -> p (o q) n", p=P)).then_inc(s_dn[c], 16)

            last_use = {n % 6: n for n in range(len(blocks))}
            for f in sorted(range(6), key=lambda s: last_use[s]):
                wait_used(blocks[last_use[f]])
                for k in (2 * f, 2 * f + 1):
                    gate_up(k, 0) if k < KD else down(k - KD, 0)
            for k in range(KD):
                sp.wait_ge(S["gu_used"], k + 1)
                gate_up(k, 1)
            sp.wait_ge(S["tables"], 2)
            n_pairs = sp.value_load(table_i[0:1, 48:49], min_val=E // 2, max_val=ITEMS // 2)
            with sp.Fori(1, n_pairs) as p:
                e_prev = sp.value_load(table_i[0:1, bass.ds(p * 2 - 1, 1)], min_val=0, max_val=E - 1)
                e_a = sp.value_load(table_i[0:1, bass.ds(p * 2, 1)], min_val=0, max_val=E - 1)
                e_b = sp.value_load(table_i[0:1, bass.ds(p * 2 + 1, 1)], min_val=0, max_val=E - 1)
                for k in range(KD):
                    sp.wait_ge(S["gu_used"], p * 16 - 8 + (k + 1))
                    gate_up_dyn(k, e_a)
                for c in range(4):
                    sp.wait_ge(S["dn_used"], p * 8 - 8 + (c + 1))
                    down_dyn(c, e_prev)
                for k in range(KD):
                    sp.wait_ge(S["gu_used"], p * 16 + (k + 1))
                    gate_up_dyn(k, e_b)
                for c in range(4):
                    sp.wait_ge(S["dn_used"], p * 8 - 4 + (c + 1))
                    down_dyn(c, e_a)
            e_last = sp.value_load(table_i[0:1, bass.ds(n_pairs * 2 - 1, 1)], min_val=0, max_val=E - 1)
            last_pair = sp.value_load(table_i[0:1, 49:50], min_val=E // 2 - 1, max_val=ITEMS // 2 - 1)
            for c in range(4):
                sp.wait_ge(S["dn_used"], last_pair * 8 + (c + 1))
                down_dyn(c, e_last)
            for t in range(TT):
                sp.wait_ge(S["fin_rdy"], t + 1)
                sp.dma_start(out[0, t * P:(t + 1) * P, :], fin[:, t, :]).then_inc(S["out_done"], 16)
            sp.wait_ge(S["out_done"], 16 * TT)

        @block.gpsimd
        def _(pool):
            nc.gpsimd.memset(prm, 0.0).then_inc(S["prm_zero"], 1)
            pool.wait_ge(S["filt_sb"], TT)
            nc.gpsimd.memset(at("qm"), 0.0).then_inc(S["qm_zero"], 1)
            pool.wait_ge(S["kB1_ps"], 1)
            nc.gpsimd.memset(uraw[:, :, 0:1], 0.0).then_inc(S["pad_zero"], 1)
            nc.gpsimd.memset(uraw[:, :, 257:258], 0.0).then_inc(S["pad_zero"], 1)
            pool.wait_ge(S["Y_rdy"], 2)
            nc.gpsimd.memset(sel_bias, 0.0).then_inc(S["gub_zero"], 1)
            pool.wait_ge(S["gub_zero"], 1)
            pool.dma_start(sel_bias[0:E, :], a["b_gate_up"][0]).then_inc(S["gub_in"], 16)
            pool.wait_ge(S["yT_ps"], 1)
            pool.dma_start(b_down[0:E, :], a["b_down"][0]).then_inc(S["bd_in"], 16)
            pool.wait_ge(S["s_ps"], 8)
            pool.dma_start(fgB, a["final_norm_g"][:].partition_broadcast(P)).then_inc(S["fg_in"], 16)
            pool.wait_ge(S["bc_sb"], 4)
            for t in range(TT):
                pool.wait_ge(S["x2T_ps"], t + 1)
                nc.gpsimd.tensor_tensor(xn[:, t, :], xn[:, t, :], gsB, ALU.mult).then_inc(S["pool_step"], 1)
                pool.wait_ge(S["pool_step"], t + 1)
                nc.gpsimd.tensor_tensor(xn[:, t, :], xn[:, t, :], shB, ALU.add).then_inc(S["h2_rdy"], 1)

        @block.tensor
        def _(pe):
            mm = pe.matmul

            def bank(b, n=512, o=0):
                return ps[:, b, o:o + n]

            def front_in(b):
                n = where[b]
                pe.wait_ge(s_front[n % 6], 16 * (n // 6 + 1))
                return block_view(b)

            pe.wait_ge(S["tab_in"], 16)
            pe.wait_ge(S["prm_in"], 16 * 13)
            pe.transpose(bank(3, 128), prm, ident).then_inc(S["prmT_ps"], 1)
            pe.wait_ge(S["filt_in"], 16 * 5)
            mm(ps[0:64, 4, 0:256], w1[0:17, :], zT[0:17, :], start=True, stop=True).then_inc(S["f1_ps"], 1)
            pe.wait_ge(S["hid_1"], 1)
            mm(ps[0:64, 5, 0:256], w2[0:64, :], hid[0:64, :], start=True, stop=True).then_inc(S["f2_ps"], 1)
            pe.wait_ge(S["hid_2"], 1)
            mm(ps[0:64, 6, 0:256], w3[0:64, :], hid[0:64, :], start=True, stop=True).then_inc(S["f3_ps"], 1)
            pe.wait_ge(S["hid_3"], 1)
            for s in range(2):
                for t in range(TT):
                    mm(bank(4 + 2 * s + t), hid[0:64, t * P:(t + 1) * P], w4[0:64, s * HW:(s + 1) * HW],
                       start=True, stop=True).then_inc(S["f4_ps"], 1)
            pe.wait_ge(S["xn_rdy"], 1)
            pe.wait_ge(S["prmT_sb"], 1)
            for k in range(KD):
                for t in range(TT):
                    last = pe.transpose(bank(k // 2, 128, (k % 2) * 256 + t * 128), xn[:, t, k * P:(k + 1) * P], ident)
            last.then_inc(S["xT_ps"], 1)

            def ada(g, b, js):
                for j in js:
                    w = front_in(("ada", g, j))
                    for kk in range(2):
                        k = 2 * j + kk
                        for q in range(4):
                            last = mm(ps[32 * q:32 * q + 32, b, :], cs[:, k, :], w[:, kk, q * 512:(q + 1) * 512],
                                      start=(k == 0), stop=(k == KD - 1))
                    last.then_inc(S["ada_used"], 1)

            def ada_cols(g, b):
                for j in range(4):
                    last = pe.transpose(bank(b, 128, j * 128), adr[g][:, j * P:(j + 1) * P], ident)
                return last

            pe.wait_ge(S["silu_c"], 1)
            pe.wait_ge(S["filt_sb"], TT)
            ada(0, 4, range(4))
            pe.wait_ge(S["ada0_sb"], 2)
            ada_cols(0, 5).then_inc(S["mc0_ps"], 1)
            pe.wait_ge(S["dft_in"], 16)

            def spectrum(b, f0, taps):
                for t in range(TT):
                    last = mm(bank(b), dft[:, t, f0:f0 + P], taps[:, t, :], start=(t == 0), stop=(t == TT - 1))
                return last

            spectrum(6, 0, kplus)
            spectrum(7, 128, kplus).then_inc(S["kA_ps"], 1)
            spectrum(4, 256, kplus).then_inc(S["kN_ps"], 1)
            pe.wait_ge(S["mc0_sb"], 1)
            spectrum(5, 256, kminus).then_inc(S["kB0_ps"], 1)
            pe.wait_ge(S["kA_sb"], 1)
            spectrum(6, 384, kminus).then_inc(S["kB1_ps"], 1)

            pe.wait_ge(S["h1_sb"], 1)

            def unit(n):
                blk, half = n // 2, n % 2
                w = front_in(("in", blk, 0))
                if n >= 3:
                    m = n - 3
                    if m in (10, 11):
                        pe.wait_ge(S["v_sb"], m - 9)
                    else:
                        pe.wait_ge(S["u_sb"], m + 1 if m < 10 else m - 1)
                b = n % 3
                if blk == 5:
                    for k in range(KD):
                        last = mm(bank(b), hT[:, k, half * P:(half + 1) * P], w[:, k, :],
                                  start=(k == 0), stop=(k == KD - 1))
                else:
                    for c in range(2):
                        cc = 2 * half + c
                        for k in range(KD):
                            last = mm(bank(b, 256, c * 256), w[:, k, cc * P:(cc + 1) * P], hT[:, k, :],
                                      start=(k == 0), stop=(k == KD - 1))
                last.then_inc(S["u_ps"], 1)

            pe.wait_ge(S["kf_done"], 1)
            for blk in range(6):
                unit(2 * blk)
                unit(2 * blk + 1)
                if blk < 4:
                    ada(1, 6, (blk,))
                else:
                    ada(2, 7, (2 * blk - 8, 2 * blk - 7))
            pe.wait_ge(S["vT_rdy"], 1)
            for t in range(TT):
                for c in range(CT):
                    last = pe.transpose(bank(3 + t, 128, c * 128), vT[:, c, t * P:(t + 1) * P], ident)
                last.then_inc(S["vt_ps"], 1)
            unit(12)
            pe.wait_ge(S["vt_sb"], 2)
            unit(13)
            pe.wait_ge(S["ada1_sb"], 1)
            pe.wait_ge(S["ada2_sb"], 1)
            for f in range(4):
                for t in range(TT):
                    last = mm(bank(4 + f), dft[:, t, f * P:(f + 1) * P], vtc[:, t, :],
                              start=(t == 0), stop=(t == TT - 1))
                last.then_inc(S["V_ps"], 1)
            unit(14)
            unit(15)
            pe.wait_ge(S["Y_rdy"], 2)
            pe.wait_ge(S["inv_in"], 16)
            for c in range(CT):
                for f in range(4):
                    last = mm(bank(6 + c // 2, 256, (c % 2) * 256), Y[:, f, c * P:(c + 1) * P], inv[:, f, :],
                              start=(f == 0), stop=(f == 3))
            last.then_inc(S["yT_ps"], 1)

            def scores(j):
                t, h = j // HEADS, j % HEADS
                if j >= 2:
                    pe.wait_ge(S["s_sb"], j - 1)
                for c in range(2):
                    last = mm(bank(4 + j % 2, 256, c * 256), qm[:, h, c, t * P:(t + 1) * P], kT[:, h, :],
                              start=True, stop=True)
                last.then_inc(S["s_ps"], 1)

            def weights_T(j):
                pe.wait_ge(S["a_rdy"], j + 1)
                if j >= 2:
                    pe.wait_ge(S["aT_sb"], j - 1)
                for k in range(TT):
                    last = pe.transpose(bank(3, 128, (j % 2) * 256 + k * 128), ab[j % 2][:, k * P:(k + 1) * P], ident)
                last.then_inc(S["aT_ps"], 1)

            def values(j):
                t, h = j // HEADS, j % HEADS
                pe.wait_ge(S["aT_sb"], j + 1)
                for k in range(TT):
                    last = mm(bank(6 + t, 128, h * 128), aT[j % 2][:, k, :], ve[:, k, h * P:(h + 1) * P],
                              start=(k == 0), stop=(k == TT - 1))
                last.then_inc(S["o_ps"], 1)

            pe.wait_ge(S["u_sb"], 10)
            pe.wait_ge(S["v_sb"], 2)
            scores(0)
            scores(1)
            pe.wait_ge(S["u_sb"], 14)
            pe.wait_ge(S["ada1_sb"], 1)
            ada_cols(1, 0).then_inc(S["mc1_ps"], 1)
            pe.wait_ge(S["ada2_sb"], 2)
            ada_cols(2, 1).then_inc(S["mc2_ps"], 1)

            def spread(b, g, q):
                return mm(bank(b), ident[:, 32 * q:32 * q + 1].to_broadcast([P, P]), adr[g], start=True, stop=True)

            pe.wait_ge(S["mc1_sb"], 1)
            spread(0, 1, 0).then_inc(S["g1_ps"], 1)
            pe.wait_ge(S["mc2_sb"], 1)
            spread(2, 1, 1).then_inc(S["g1_ps"], 1)

            def attention_gate(i):
                m = i // 2
                if i % 2 == 0:
                    if m == 0:
                        pe.wait_ge(S["g1_sb"], 1)
                    elif m == 2:
                        pe.wait_ge(S["g1_sb"], 2)
                    elif m == 3:
                        pe.wait_ge(S["u_sb"], 15)
                w = front_in(("in", 8 + m // 2, 0))
                cc = i % 4
                for k in range(KD):
                    last = mm(bank(m % 3, 256, (i % 2) * 256), w[:, k, cc * P:(cc + 1) * P], hT[:, k, :],
                              start=(k == 0), stop=(k == KD - 1))
                if i % 2:
                    last.then_inc(S["u_ps"], 1)

            attention_gate(0)
            pe.wait_ge(S["yhy_rdy"], 1)
            for j in range(2 * HEADS + 1):
                if j < 2 * HEADS:
                    weights_T(j)
                    if j + 2 < 2 * HEADS:
                        scores(j + 2)
                if j >= 1:
                    values(j - 1)
                if j + 1 < KD:
                    attention_gate(j + 1)
            for t in range(TT):
                pe.wait_ge(S["on_rdy"], t + 1)
                if t == 0:
                    pe.wait_ge(S["aT_sb"], 2 * HEADS)
                else:
                    pe.wait_ge(S["oT_sb"], t)
                for h in range(HEADS):
                    last = pe.transpose(bank(3, 128, h * 128), on[:, h * P:(h + 1) * P], ident)
                last.then_inc(S["oT_ps"], 1)

            why, wat = front_in(("hy", 0, 0)), front_in(("att", 0, 0))
            pe.wait_ge(S["oT_sb"], TT)
            for i in range(KD):
                if i >= 2:
                    pe.wait_ge(S["pj_sb"], i - 1)
                for src, w, o in ((y_hyT, why, 0), (y_atT, wat, 256)):
                    for k in range(CT):
                        last = mm(bank(4 + i % 2, 256, o), w[:, k, i * P:(i + 1) * P], src[:, k, :],
                                  start=(k == 0), stop=(k == CT - 1))
                last.then_inc(S["pj_ps"], 1)
            pe.wait_ge(S["pj_sb"], KD)
            pe.wait_ge(S["u_sb"], 18)
            for t in range(TT):
                for i in range(2):
                    w = front_in(("mix", i, 0))
                    for kk in range(4):
                        k = 4 * i + kk
                        for h in range(2):
                            last = mm(bank(2 * t + h), merged[:, k, t * P:(t + 1) * P], w[:, kk, h * 512:(h + 1) * 512],
                                      start=(k == 0), stop=(k == KD - 1))
                    if (t, i) != (0, 0):
                        last.then_inc(S["mix_ps"], 1)
            pe.wait_ge(S["x1_rdy"], 2)
            for i, (g, q) in enumerate(((1, 2), (1, 3), (2, 0), (2, 1), (2, 2), (2, 3))):
                if i >= 2:
                    pe.wait_ge(S["bc_sb"], i - 1)
                spread(i % 2, g, q).then_inc(S["bc_ps"], 1)
            for t in range(TT):
                pe.wait_ge(S["xn2_rdy"], t + 1)
                for k in range(KD):
                    last = pe.transpose(bank(4 + 2 * t + k // 4, 128, (k % 4) * 128), xn[:, t, k * P:(k + 1) * P], ident)
                last.then_inc(S["x2T_ps"], 1)
            pe.wait_ge(S["h2T_sb"], TT)
            pe.wait_ge(S["wr_in"], 16)
            for kk in range(2):
                for q in range(4):
                    last = mm(ps[32 * q:32 * q + 32, 2, 0:256], wr[:, 2 * q + kk, :], hT[:, 2 * q + kk, :],
                              start=(kk == 0), stop=(kk == 1))
            last.then_inc(S["part_ps"], 1)
            pe.wait_ge(S["part_sb"], 1)
            for t in range(TT):
                last = mm(bank(3, 32, 32 * t), part[:, t * P:(t + 1) * P], tab("quad"), start=True, stop=True)
            last.then_inc(S["log_ps"], 1)
            pe.wait_ge(S["m_rdy"], 1)
            mm(bank(5, 32, 0), tri, M[:, 0, :], start=True, stop=True)
            mm(bank(5, 32, 32), ones, M[:, 0, :], start=True, stop=False)
            mm(bank(5, 32, 32), tri, M[:, 1, :], start=False, stop=True)
            mm(bank(6, 32, 0), ones, M[:, 0, :], start=True, stop=False)
            mm(bank(6, 32, 0), ones, M[:, 1, :], start=False, stop=True)
            for t in range(TT):
                last = mm(ps[0:32, 7, 0:128], M[:, t, :], ones, start=(t == 0), stop=(t == TT - 1))
            last.then_inc(S["rank_ps"], 1)
            pe.wait_ge(S["cnt_sb"], 2)
            mm(bank(4, 48, 0), cntT2[0:E, :], tri[0:E, 0:48], start=True, stop=True).then_inc(S["ex_ps"], 1)
            def gather(p):
                pe.wait_ge(S["sel_rdy"], p + 1)
                for half in range(2):
                    b = 7 - half
                    for kk in range(4):
                        k = 4 * half + kk
                        for t in range(TT):
                            last = mm(bank(b, 128, kk * 128), xn[:, t, k * P:(k + 1) * P], Sel[:, t, :],
                                      start=(t == 0), stop=(t == TT - 1))
                    last.then_inc(S["ga_done"], 1)

            def gate_up(i, s):
                for b in range(2):
                    for h in range(2):
                        mm(ps[64 * h:64 * h + 64, 4 + b, :], mask[:, s, :],
                           sel_bias[:, b * 1024 + h * 512:b * 1024 + (h + 1) * 512], start=True, stop=False)
                for k in range(KD):
                    pe.wait_ge(s_gu[k], i * 16 + 16)
                    for b in range(2):
                        for h in range(2):
                            last = mm(ps[64 * h:64 * h + 64, 4 + b, :], hTp[:, k, s * 64:(s + 1) * 64],
                                      gu_slot[k][:, b * 1024 + h * 512:b * 1024 + (h + 1) * 512],
                                      start=False, stop=(k == KD - 1))
                    last.then_inc(S["gu_used"], 1)

            def act_transpose():
                for j in range(4):
                    last = pe.transpose(bank(7, 128, j * 128), act_o[:, j * P:(j + 1) * P], ident)
                last.then_inc(S["tr_done"], 1)

            def down(i):
                for c in range(4):
                    pe.wait_ge(s_dn[c], i * 16 + 16)
                    for qq in range(2):
                        q = 2 * c + qq
                        lhs = actT[:, q % 4, (q // 4) * 64:(q // 4) * 64 + 64]
                        for h in range(2):
                            last = mm(ps[64 * h:64 * h + 64, 6, :], lhs, dn_slot[c][:, qq, h * 512:(h + 1) * 512],
                                      start=(q == 0), stop=(q == 7))
                    last.then_inc(S["dn_used"], 1)

            def scatter(stop):
                for t in range(TT):
                    for h in range(2):
                        last = mm(bank(2 * t + h), Pw[:, t, :], y[:, h * 512:(h + 1) * 512],
                                  start=False, stop=stop, skip_group_check=True)
                last.then_inc(S["sc_done"], 1)

            def place_weights():
                for t in range(TT):
                    last = pe.transpose(bank(7, 128, t * 128), Wt[:, t, :], ident)
                last.then_inc(S["pt_done"], 1)

            pe.wait_ge(S["gub_in"], 16)
            pe.wait_ge(S["h2_rdy"], TT)
            gather(0)
            pe.wait_ge(S["mask_rdy"], 1)
            pe.wait_ge(S["ga_sb"], 2)
            gate_up(0, 0)
            pe.wait_ge(S["act_rdy"], 1)
            act_transpose()
            gate_up(1, 1)
            pe.wait_ge(S["actT_rdy"], 1)
            pe.wait_ge(S["g_all"], TOPK)
            for t in range(TT):
                last = pe.transpose(ps[0:32, 7, 128 * t:128 + 128 * t], G[:, t, :], ident)
            last.then_inc(S["gt_ps"], 1)
            down(0)
            pe.wait_ge(S["gt_sb"], 1)
            pe.wait_ge(S["bd_in"], 16)
            pe.wait_ge(S["bc_sb"], 6)
            for t in range(TT):
                for h in range(2):
                    mm(bank(2 * t + h), GT[0:E, t * P:(t + 1) * P], b_down[0:E, h * 512:(h + 1) * 512],
                       start=True, stop=False, skip_group_check=True)
            pe.wait_ge(S["act_rdy"], 2)
            act_transpose()
            pe.wait_ge(S["actT_rdy"], 2)
            pe.wait_ge(S["y_rdy"], 1)
            gather(1)
            pe.wait_ge(S["wt_rdy"], 1)
            pe.wait_ge(S["ga_sb"], 3)
            place_weights()
            pe.wait_ge(S["tables"], 2)
            n_pairs = pe.value_load(table_i[0:1, 48:49], min_val=E // 2, max_val=ITEMS // 2)
            with pe.Fori(1, n_pairs) as p:
                pe.wait_ge(S["mask_rdy"], p + 1)
                pe.wait_ge(S["ga_sb"], p * 2 + 2)
                gate_up(p * 2, 0)
                pe.wait_ge(S["actT_rdy"], p * 2)
                down(p * 2 - 1)
                pe.wait_ge(S["act_rdy"], p * 2 + 1)
                pe.wait_ge(S["pt_sb"], p)
                act_transpose()
                gate_up(p * 2 + 1, 1)
                pe.wait_ge(S["y_rdy"], p * 2)
                scatter(False)
                pe.wait_ge(S["actT_rdy"], p * 2 + 1)
                down(p * 2)
                pe.wait_ge(S["act_rdy"], p * 2 + 2)
                act_transpose()
                pe.wait_ge(S["actT_rdy"], p * 2 + 2)
                pe.wait_ge(S["y_rdy"], p * 2 + 1)
                gather(p + 1)
                pe.wait_ge(S["wt_rdy"], p + 1)
                pe.wait_ge(S["ga_sb"], p * 2 + 3)
                place_weights()
            pe.wait_ge(S["ga_sb"], n_pairs * 2 + 2)
            down(n_pairs * 2 - 1)
            pe.wait_ge(S["y_rdy"], n_pairs * 2)
            pe.wait_ge(S["pt_sb"], n_pairs)
            scatter(True)

        @block.scalar
        def _(act):
            A = nc.scalar.activation
            step = Steps(act, S["act_step"])
            act.dma_start(at("lam"), a["lambda_qk"][0].rearrange("a b -> (a b)").partition_broadcast(P))\
                .then_inc(S["lam_in"], 16)
            act.dma_start(decay, a["t_decay"].rearrange("s (t p) c -> p s t c", p=P)).then_inc(S["decay_in"], 16)
            act.dma_start(dft, a["t_dft"].rearrange("(t p) f -> p t f", p=P)).then_inc(S["dft_in"], 16)
            act.wait_ge(S["prmT_sb"], 1)
            sig(act, A(at("cs", 0, 8), prmT[:, C_C:C_C + 8], ACT.Sigmoid), "sig_c", 1)
            for g in range(3):
                for q in range(4):
                    o = g * 2048 + q * 512
                    act.dma_start(adr[g][32 * q:32 * q + 32, :], a["b_ada"][0, o:o + 512].partition_broadcast(32))\
                        .then_inc(S["ada_in"], 16)
            for r0, name in ((0, "norm_ffn_g"), (64, "norm_mix_g")):
                for h in range(2):
                    act.dma_start(gain[r0 + 32 * h:r0 + 32 * h + 32, :],
                                  a[name][0, 512 * h:512 * (h + 1)].partition_broadcast(32)).then_inc(S["gain_in"], 16)
            act.dma_start(at("bv"), a["b_in"][0, 2560:3072].partition_broadcast(P)).then_inc(S["bv_in"], 16)
            act.dma_start(at("br"), a["b_router"][0].partition_broadcast(P)).then_inc(S["br_in"], 16)
            act.dma_start(inv, a["t_inv"].rearrange("(f p) t -> p f t", p=P)).then_inc(S["inv_in"], 16)
            act.wait_ge(S["x_in"], 16)
            for t in range(TT):
                A(xn[:, t, :], x[:, t, :], ACT.Square, accum_out=ss[:, t:t + 1]).then_inc(S["x_sq"], 1)
            for n in range(1, 4):
                act.wait_ge(S[f"ang_{n}"], 1)
                A(hid[0:64, :], ang[0:64, :], ACT.Sin).then_inc(S[f"hid_{n}"], 1)

            act.wait_ge(S["lam_a"], 1)
            sig(act, A(lam2, lam2, ACT.Exp), "lam_e", 1)
            act.dma_start(wr, a["w_router"][0].rearrange("(k p) e -> p k e", p=P)).then_inc(S["wr_in"], 16)

            def evacuate(n):
                act.wait_ge(S["u_ps"], n + 1)
                for c in range(2):
                    src = ps[:, n % 3, c * 256:(c + 1) * 256]
                    i = 2 * n + c
                    if n < 6:
                        last = A(uraw[:, i, 1:257], src, ACT.Identity, bias=col(C_BHY + i))
                    elif n < 8:
                        h = i - 12
                        for r in range(2):
                            last = A(qm[64 * r:64 * r + 64, h, r, :], src[64 * r:64 * r + 64, :], ACT.Identity,
                                     bias=col(C_BQ + h, 64 * r, 64 * r + 64))
                    elif n < 10:
                        last = A(kT[:, i - 16, :], src, ACT.Identity, bias=col(C_BK + i - 16))
                    else:
                        last = A(gate_hy[:, i - 24, :], src, ACT.Sigmoid, bias=col(C_BG + i - 24))
                last.then_inc(S["u_sb"], 1)

            act.wait_ge(S["qm_zero"], 1)
            act.wait_ge(S["pad_zero"], 2)
            for n in range(10):
                evacuate(n)
            for t in range(TT):
                act.wait_ge(S["vt_ps"], t + 1)
                A(vtc[:, t, :], ps[:, 3 + t, :], ACT.Copy).then_inc(S["vt_sb"], 1)
            for n in range(12, 16):
                evacuate(n)
            for j in range(2 * HEADS):
                act.wait_ge(S["negm_rdy"], j + 1)
                for c in range(2):
                    last = A(sc[j % 2][:, c, :], sc[j % 2][:, c, :], ACT.Exp, scale=0.125,
                             bias=negm[:, 2 * (j % 2) + c:2 * (j % 2) + c + 1],
                             accum_out=sums[:, 2 * (j % 2) + c:2 * (j % 2) + c + 1])
                    if c == 1:
                        last.then_inc(S["exp_done"], 1)
                    else:
                        step(last)
                if j == 0:
                    for h in range(2):
                        act.wait_ge(S["g1_ps"], h + 1)
                        A(gate1B[:, 512 * h:512 * (h + 1)], ps[:, 2 * h, :], ACT.Copy).then_inc(S["g1_sb"], 1)
                if j % 2:
                    m = j // 2
                    act.wait_ge(S["u_ps"], 17 + m)
                    for c in range(2):
                        last = A(gate_at[2 * m + c], ps[:, m % 3, c * 256:(c + 1) * 256], ACT.Identity,
                                 bias=col(C_BG + 8 + 2 * m + c))
                    last.then_inc(S["u_sb"], 1)
                if j in (4, 7):
                    t = j // 4 - (j == 4)
                    act.wait_ge(S["o_ps"], 4 if j == 4 else 8)
                    if t:
                        act.wait_ge(S["on_rdy"], t)
                    A(at("bv"), ps[:, 6 + t, :], ACT.Square).then_inc(S["o_sq"], 1)
            for n, g in enumerate((at("uc", 2048, 1024), at("ur", 2048, 1024))):
                act.wait_ge(S["u_sb"], 16 + 2 * n)
                A(g, g, ACT.Sigmoid).then_inc(S["gat_rdy"], 1)
            act.wait_ge(S["x1_rdy"], 2)
            A(xn[:, 0, :], x[:, 0, :], ACT.Square, accum_out=ss[:, 0:1]).then_inc(S["x1_sq"], 1)
            for i, dst in enumerate((shB[:, 0:512], shB[:, 512:1024], gsB[:, 0:512], gsB[:, 512:1024],
                                     gate2B[:, 0:512], gate2B[:, 512:1024])):
                if i == 3:
                    act.wait_ge(S["x1_rdy"], 4)
                    A(xn[:, 1, :], x[:, 1, :], ACT.Square, accum_out=ss[:, 1:2]).then_inc(S["x1_sq"], 1)
                act.wait_ge(S["bc_ps"], i + 1)
                A(dst, ps[:, i % 2, :], ACT.Copy).then_inc(S["bc_sb"], 1)
            act.wait_ge(S["top_rdy"], 1)
            A(gexp, gexp, ACT.Exp).then_inc(S["top_exp"], 1)

            def sigmoid(i):
                act.wait_ge(S["g_rdy"], i + 1)
                A(s_sb, g_sb, ACT.Sigmoid, scale=1.702).then_inc(S["sig_rdy"], 1)

            def act_copy(i):
                act.wait_ge(S["tr_done"], i + 1)
                A(actT.rearrange("p j s -> p (j s)"), ps[:, 7, :], ACT.Copy).then_inc(S["actT_rdy"], 1)

            def y_copy(i, s):
                act.wait_ge(S["dn_used"], i * 4 + 4)
                for h in range(2):
                    last = A(y[64 * s:64 * s + 64, 512 * h:512 * (h + 1)], ps[64 * h:64 * h + 64, 6, :], ACT.Copy)
                last.then_inc(S["y_rdy"], 1)

            sigmoid(0)
            act_copy(0)
            sigmoid(1)
            act.wait_ge(S["gt_ps"], 1)
            A(GT[0:E, :], ps[0:E, 7, 0:256], ACT.Copy).then_inc(S["gt_sb"], 1)
            y_copy(0, 0)
            act_copy(1)
            act.wait_ge(S["tables"], 2)
            n_pairs = act.value_load(table_i[0:1, 48:49], min_val=E // 2, max_val=ITEMS // 2)
            with act.Fori(1, n_pairs) as p:
                sigmoid(p * 2)
                y_copy(p * 2 - 1, 1)
                act_copy(p * 2)
                sigmoid(p * 2 + 1)
                act.wait_ge(S["sc_done"], p)
                y_copy(p * 2, 0)
                act_copy(p * 2 + 1)
            y_copy(n_pairs * 2 - 1, 1)
            for t in range(TT):
                act.wait_ge(S["x2_rdy"], 2 * t + 2)
                A(fin[:, t, :], x[:, t, :], ACT.Square, accum_out=ss[:, t:t + 1]).then_inc(S["fin_sq"], 1)

        @block.vector
        def _(v):
            V = nc.vector
            step = Steps(v, S["dve_step"])

            def rstd(dst, src, n):
                w = dst.shape[1]
                m, t = nwt[:, 0:w], nwt[:, 4:4 + w]
                step(V.tensor_scalar(m, src, 1.0 / n, EPS, ALU.mult, ALU.add))
                step(V.tensor_scalar(dst.bitcast(I32), m.bitcast(I32), -0.5, float(0x5F3759DF), ALU.mult, ALU.add))
                for _ in range(3):
                    step(V.scalar_tensor_tensor(t, dst, -0.5, dst, ALU.mult, ALU.mult))
                    step(V.tensor_tensor(t, t, m, ALU.mult))
                    step(V.scalar_tensor_tensor(dst, t, 1.5, dst, ALU.add, ALU.mult))

            v.wait_ge(S["prmT_ps"], 1)
            sig(v, V.tensor_copy(prmT, ps[:, 3, 0:128]), "prmT_sb", 1)

            def angle(n, src):
                step(V.tensor_scalar(ang[0:64, :], src, col(C_F + n - 1, 0, 64), col(C_F + 3, 0, 64), ALU.add, ALU.mult))
                magic = 1.5 * 2.0 ** 23
                step(V.tensor_scalar(turns[0:64, :], ang[0:64, :], 1.0 / TWO_PI, magic, ALU.mult, ALU.add))
                step(V.tensor_scalar(turns[0:64, :], turns[0:64, :], -magic, None, ALU.add))
                for part in (6.28125, 0.0019350051879882812, 3.019915981956753e-07):
                    step(V.scalar_tensor_tensor(ang[0:64, :], turns[0:64, :], -part, ang[0:64, :], ALU.mult, ALU.add))
                pi = 3.1415925
                V.tensor_scalar(ang[0:64, :], ang[0:64, :], pi, -pi, ALU.min, ALU.max).then_inc(S[f"ang_{n}"], 1)

            v.wait_ge(S["tab_in"], 16)
            step(V.tensor_copy(ef[:, 0:E], tab("item")[:, 0:E]))
            step(V.tensor_scalar(ohI[:, 0:E], ef[:, 0:E], lane, None, ALU.is_equal))
            v.wait_ge(S["f1_ps"], 1)
            angle(1, ps[0:64, 4, 0:256])
            v.wait_ge(S["sig_c"], 1)
            cb = at("on", 0, 8)
            step(V.tensor_tensor(cb, at("cs", 0, 8), prmT[:, C_C:C_C + 8], ALU.mult))
            sig(v, V.tensor_copy(cs, cb.unsqueeze(2).to_broadcast([P, KD, 32])), "silu_c", 1)
            v.wait_ge(S["lam_in"], 16)
            lam = at("lam").rearrange("p (a b d) -> p a b d", a=2, b=2)
            lprod = at("on", 8, 128).rearrange("p (a d) -> p a d", a=2)
            step(V.tensor_tensor(lprod, lam[:, :, 0, :], lam[:, :, 1, :], ALU.mult))
            sig(v, V.tensor_reduce(lam2, lprod, AX.X, ALU.add), "lam_a", 1)
            v.wait_ge(S["hid_1"], 1)
            v.wait_ge(S["f2_ps"], 1)
            angle(2, ps[0:64, 5, 0:256])
            v.wait_ge(S["x_sq"], TT)
            rstd(rs, ss, D)
            step(V.tensor_scalar(xn[:, 0, :], x[:, 0, :], rs[:, 0:1], None, ALU.mult))
            V.tensor_scalar(xn[:, 1, :], x[:, 1, :], rs[:, 1:2], None, ALU.mult).then_inc(S["xn_rdy"], 1)
            v.wait_ge(S["hid_2"], 1)
            v.wait_ge(S["f3_ps"], 1)
            angle(3, ps[0:64, 6, 0:256])
            v.wait_ge(S["f4_ps"], 4)
            v.wait_ge(S["decay_in"], 16)
            for t in range(TT):
                step(V.tensor_tensor(kminus[:, t, :], ps[:, 4 + t, :], decay[:, 0, t, :], ALU.mult))
                step(V.tensor_tensor(kback, ps[:, 6 + t, :], decay[:, 1, t, :], ALU.mult))
                step(V.tensor_tensor(kplus[:, t, :], kminus[:, t, :], kback, ALU.add))
                sig(v, V.tensor_tensor(kminus[:, t, :], kminus[:, t, :], kback, ALU.subtract), "filt_sb", t + 1)

            def ada_rows(g, b, gains):
                v.wait_ge(S["ada_used"], 4 * g + 4)
                v.wait_ge(S["ada_in"], 16 * 12)
                sig(v, V.tensor_tensor(adr[g], ps[:, b, :], adr[g], ALU.add), f"ada{g}_sb", 1)
                if gains is not None:
                    r = slice(gains, gains + 64)
                    v.wait_ge(S["gain_in"], 16 * 4)
                    sig(v, V.scalar_tensor_tensor(adr[g][r, :], adr[g][r, :], 1.0, gain[r, :], ALU.add, ALU.mult),
                        f"ada{g}_sb", 2)

            def ada_columns(g, b):
                v.wait_ge(S[f"mc{g}_ps"], 1)
                src = ps[:, b, :].rearrange("p (j q r) -> p q j r", j=4, q=4)[:, :, :, 0]
                sig(v, V.tensor_copy(modc[:, g, :, :], src), f"mc{g}_sb", 1)

            def modulated(shift, scale):
                for k in range(KD):
                    last = V.tensor_scalar(hT[:, k, :], ps[:, k // 2, (k % 2) * 256:(k % 2) * 256 + 256],
                                           scale(k), shift(k), ALU.mult, ALU.add)
                return last

            ada_rows(0, 4, 64)
            ada_columns(0, 5)
            v.wait_ge(S["xT_ps"], 1)
            mc = lambda g, i: modc[:, g, i // 4, i % 4:i % 4 + 1]
            modulated(lambda k: mc(0, k), lambda k: mc(0, 8 + k)).then_inc(S["h1_sb"], 1)
            v.wait_ge(S["kA_ps"], 1)
            step(V.tensor_copy(kA[:, 0, :], ps[:, 6, :]))
            step(V.tensor_copy(kN, ps[:, 6, :]))
            sig(v, V.tensor_copy(kA[:, 1, :], ps[:, 7, :]), "kA_sb", 1)
            v.wait_ge(S["kN_ps"], 1)
            step(V.tensor_copy(kN[0:1, :], ps[0:1, 4, :]))
            v.wait_ge(S["kB0_ps"], 1)
            step(V.tensor_copy(kB[:, 0, :], ps[:, 5, :]))
            step(V.memset(kB[0:1, 0, :], 0.0))
            v.wait_ge(S["kB1_ps"], 1)
            sig(v, V.tensor_copy(kB[:, 1, :], ps[:, 6, :]), "kf_done", 1)
            for i in range(12):
                v.wait_ge(S["u_sb"], i // 2 + 1)
                wcol = lambda j: col(C_W + 12 * j + i)
                step(V.tensor_scalar(ucv[:, i, :], uraw[:, i, 1:257], wcol(1), col(C_CB + i), ALU.mult, ALU.add))
                step(V.scalar_tensor_tensor(ucv[:, i, :], uraw[:, i, 0:256], wcol(0), ucv[:, i, :], ALU.mult, ALU.add))
                step(V.scalar_tensor_tensor(ucv[:, i, :], uraw[:, i, 2:258], wcol(2), ucv[:, i, :], ALU.mult, ALU.add))
            sig(v, V.tensor_tensor(vT, vT, x1T, ALU.mult), "vT_rdy", 1)
            ada_rows(1, 6, None)
            v.wait_ge(S["bv_in"], 16)
            for t in range(TT):
                v.wait_ge(S["u_ps"], 11 + t)
                V.tensor_tensor(ve[:, t, :], ps[:, (10 + t) % 3, :], at("bv"), ALU.add).then_inc(S["v_sb"], 1)
            ada_rows(2, 7, 0)
            v.wait_ge(S["V_ps"], 4)
            t0, t1 = flat
            for f in range(2):
                vr, vs = ps[:, 4 + f, :], ps[:, 6 + f, :]
                a2 = kN if f == 0 else kA[:, 1, :]
                step(V.tensor_tensor(t0, vr, kA[:, f, :], ALU.mult))
                step(V.tensor_tensor(t1, vs, kB[:, f, :], ALU.mult))
                step(V.tensor_tensor(Y[:, f, :], t0, t1, ALU.subtract))
                step(V.tensor_tensor(t0, vr, kB[:, f, :], ALU.mult))
                step(V.tensor_tensor(t1, vs, a2, ALU.mult))
                sig(v, V.tensor_tensor(Y[:, 2 + f, :], t0, t1, ALU.add), "Y_rdy", f + 1)
            v.wait_ge(S["yT_ps"], 1)
            for c in range(CT):
                step(V.scalar_tensor_tensor(vT[:, c, :], vT[:, c, :], col(C_DS + c),
                                            ps[:, 6 + c // 2, (c % 2) * 256:(c % 2) * 256 + 256], ALU.mult, ALU.add))
            sig(v, V.tensor_tensor(y_hyT, x0T, vT, ALU.mult), "yhy_rdy", 1)
            ada_columns(1, 0)
            ada_columns(2, 1)

            v.wait_ge(S["lam_e"], 1)
            step(V.tensor_tensor(lamcol, lam2[:, 1:2], lam2[:, 0:1], ALU.subtract))
            step(V.tensor_scalar(lamcol, lamcol, -LAM_INIT, None, ALU.add))

            def logits(j):
                t, h = j // HEADS, j % HEADS
                s = sc[j % 2]
                v.wait_ge(S["s_ps"], j + 1)
                d = dist[:, t, :].unsqueeze(1).to_broadcast([P, 2, L])
                sig(v, V.scalar_tensor_tensor(s, d, -8.0 * SLOPES[h], ps[:, 4 + j % 2, :].rearrange("p (c k) -> p c k", c=2),
                                              ALU.mult, ALU.add), "s_sb", j + 1)
                m = negm[:, 2 * (j % 2):2 * (j % 2) + 2]
                step(V.tensor_reduce(m, s, AX.X, ALU.max))
                V.tensor_scalar(m, m, -0.125, None, ALU.mult).then_inc(S["negm_rdy"], 1)

            def difference(j):
                s, o = sc[j % 2], 2 * (j % 2)
                v.wait_ge(S["exp_done"], j + 1)
                step(V.reciprocal(rinv[:, o:o + 2], sums[:, o:o + 2]))
                step(V.tensor_tensor(rlam[:, j % 2:j % 2 + 1], rinv[:, o + 1:o + 2], lamcol, ALU.mult))
                step(V.tensor_scalar(s[:, 1, :], s[:, 1, :], rlam[:, j % 2:j % 2 + 1], None, ALU.mult))
                if j >= 2:
                    v.wait_ge(S["aT_ps"], j - 1)
                sig(v, V.scalar_tensor_tensor(ab[j % 2], s[:, 0, :], rinv[:, o:o + 1], s[:, 1, :], ALU.mult, ALU.add),
                    "a_rdy", j + 1)

            def turned(j):
                v.wait_ge(S["aT_ps"], j + 1)
                if j >= 2:
                    v.wait_ge(S["o_ps"], j - 1)
                V.tensor_copy(aT[j % 2].rearrange("p k q -> p (k q)"), ps[:, 3, (j % 2) * 256:(j % 2) * 256 + 256])\
                    .then_inc(S["aT_sb"], 1)

            def head_norm(t):
                v.wait_ge(S["o_sq"], t + 1)
                step(V.tensor_reduce(oss, at("bv").rearrange("p (h e) -> p h e", h=HEADS), AX.X, ALU.add))
                rstd(ors, oss, P)
                if t:
                    v.wait_ge(S["oT_ps"], t)
                V.tensor_tensor(on.rearrange("p (h e) -> p h e", h=HEADS),
                                ps[:, 6 + t, :].rearrange("p (h e) -> p h e", h=HEADS),
                                ors.unsqueeze(2).to_broadcast([P, HEADS, P]), ALU.mult).then_inc(S["on_rdy"], 1)

            def head_turned(t):
                v.wait_ge(S["oT_ps"], t + 1)
                V.tensor_scalar(y_atT[:, :, t * P:(t + 1) * P], ps[:, 3, :].rearrange("p (h q) -> p h q", h=HEADS),
                                col(C_SG), 1.0 - LAM_INIT, ALU.mult, ALU.mult).then_inc(S["oT_sb"], 1)

            logits(0)
            for j in range(2 * HEADS):
                if j + 1 < 2 * HEADS:
                    logits(j + 1)
                difference(j)
                turned(j)
                if j == 5:
                    head_norm(0)
            head_turned(0)
            head_norm(1)
            head_turned(1)
            mt = at("ab")
            for i in range(KD):
                v.wait_ge(S["pj_ps"], i + 1)
                v.wait_ge(S["gat_rdy"], i // 4 + 1)
                b = ps[:, 4 + i % 2, :]
                step(V.tensor_tensor(mt[:, 0:256], b[:, 0:256], gate_hy[:, i, :], ALU.mult))
                step(V.tensor_tensor(mt[:, 256:512], b[:, 256:512], gate_at[i], ALU.mult))
                sig(v, V.tensor_tensor(merged[:, i, :], mt[:, 0:256], mt[:, 256:512], ALU.add), "pj_sb", i + 1)
            v.wait_ge(S["g1_sb"], 2)
            for t in range(TT):
                v.wait_ge(S["mix_ps"], 2 * t + 1)
                for h in range(2):
                    step(V.tensor_tensor(flat[0], ps[:, 2 * t + h, :], gate1B[:, 512 * h:512 * (h + 1)], ALU.mult))
                    xs = x[:, t, 512 * h:512 * (h + 1)]
                    sig(v, V.tensor_tensor(xs, xs, flat[0], ALU.add), "x1_rdy", 2 * t + h + 1)
                v.wait_ge(S["x1_sq"], t + 1)
                rstd(rs[:, t:t + 1], ss[:, t:t + 1], D)
                sig(v, V.tensor_scalar(xn[:, t, :], x[:, t, :], rs[:, t:t + 1], None, ALU.mult), "xn2_rdy", t + 1)
            for t in range(TT):
                v.wait_ge(S["x2T_ps"], t + 1)
                for k in range(KD):
                    o = (k % 4) * 128
                    last = V.tensor_scalar(hT[:, k, t * P:(t + 1) * P], ps[:, 4 + 2 * t + k // 4, o:o + 128],
                                           mc(2, k), mc(1, 8 + k), ALU.mult, ALU.add)
                last.then_inc(S["h2T_sb"], 1)
            v.wait_ge(S["part_ps"], 1)
            V.tensor_copy(part, ps[:, 2, 0:256]).then_inc(S["part_sb"], 1)
            v.wait_ge(S["log_ps"], 1)
            v.wait_ge(S["br_in"], 16)
            step(V.tensor_tensor(log, ps[:, 3, 0:64].rearrange("p (t e) -> p t e", t=TT),
                                 at("br").unsqueeze(1).to_broadcast([P, TT, E]), ALU.add))
            erev = tab("erev").unsqueeze(1).to_broadcast([P, TT, E])
            for k in range(TOPK):
                step(V.tensor_reduce(topv[:, k, :], log, AX.X, ALU.max))
                step(V.tensor_tensor(wrk, log, topv[:, k, :].unsqueeze(2).to_broadcast([P, TT, E]), ALU.is_ge))
                step(V.tensor_tensor(wrk, wrk, erev, ALU.mult))
                step(V.tensor_reduce(km, wrk, AX.X, ALU.max))
                step(V.tensor_tensor(oh[:, k, :, :], wrk, km.unsqueeze(2).to_broadcast([P, TT, E]), ALU.is_equal))
                step(V.scalar_tensor_tensor(log, oh[:, k, :, :], -3.0e38, log, ALU.mult, ALU.add))
                if k == 0:
                    step(V.tensor_copy(M, oh[:, 0, :, :]))
                elif k < TOPK - 1:
                    step(V.tensor_tensor(M, M, oh[:, k, :, :], ALU.add))
                else:
                    sig(v, V.tensor_tensor(M, M, oh[:, k, :, :], ALU.add), "m_rdy", 1)
            sig(v, V.tensor_tensor(gexp, topv, topv[:, 0, :].unsqueeze(1).to_broadcast([P, TOPK, TT]), ALU.subtract),
                "top_rdy", 1)
            v.wait_ge(S["rank_ps"], 1)

            def blocks_beyond(dst, cnt, tmp, signal):
                step(V.tensor_scalar(dst, cnt, 64.0, None, ALU.is_gt))
                for n, edge in enumerate((128.0, 192.0)):
                    step(V.tensor_scalar(tmp, cnt, edge, None, ALU.is_gt))
                    sig(v, V.tensor_tensor(dst, dst, tmp, ALU.add), signal, n + 1)

            blocks_beyond(cntT2[0:E, :], ps[0:E, 7, 0:128], cntT[0:E, :], "cnt_sb")
            blocks_beyond(nov, ps[:, 6, 0:32], tmpe, "nov_rdy")
            v.wait_ge(S["ex_ps"], 1)
            step(V.tensor_copy(exc, ps[:, 4, 0:48]))
            step(V.tensor_tensor(inc, exc[:, 0:E], nov, ALU.add))
            step(V.tensor_tensor(tmpe, exc[:, 0:E], tab("item")[:, 0:E], ALU.subtract))
            step(V.tensor_scalar(tmpe, tmpe, 31.0, None, ALU.add))
            rank = ps[:, 5, 0:64].rearrange("p (t e) -> p t e", t=TT)
            wide = lambda c: c.unsqueeze(1).to_broadcast([P, TT, E])
            step(V.tensor_scalar(wrk, rank, 64.0, None, ALU.is_ge))
            step(V.tensor_tensor(wrk, wrk, wide(tmpe), ALU.mult))
            step(V.tensor_tensor(wrk, wrk, wide(tab("item")[:, 0:E]), ALU.add))
            step(V.scalar_tensor_tensor(wrk2, wrk, 64.0, rank, ALU.mult, ALU.add))
            for k in range(TOPK):
                step(V.tensor_tensor(pos_k[:, k, :, :], oh[:, k, :, :], wrk2, ALU.mult))
            step(V.tensor_reduce(pk, pos_k, AX.X, ALU.add))
            def activate(i, st):
                v.wait_ge(S["gu_used"], i * 8 + 8)
                sig(v, V.tensor_scalar(g_sb, ps[:, 4, :], 7.0, None, ALU.min), "g_rdy", i + 1)
                st(V.tensor_scalar(u_sb, ps[:, 5, :], 7.0, -7.0, ALU.min, ALU.max))
                st(V.scalar_tensor_tensor(t_sb, u_sb, 1.0, g_sb, ALU.add, ALU.mult))
                v.wait_ge(S["sig_rdy"], i + 1)
                V.tensor_tensor(act_o, t_sb, s_sb, ALU.mult).then_inc(S["act_rdy"], 1)

            def select(st):
                for k in range(TOPK):
                    for t in range(TT):
                        s = pk[:, k, t:t + 1]
                        if k == 0:
                            ins = V.tensor_scalar(Sel[:, t, :], iota, s, None, ALU.is_equal)
                        else:
                            ins = V.scalar_tensor_tensor(Sel[:, t, :], iota, s, Sel[:, t, :], ALU.is_equal, ALU.add)
                        if k == TOPK - 1 and t == TT - 1:
                            ins.then_inc(S["sel_rdy"], 1)
                        else:
                            st(ins)

            def weigh(st):
                for k in range(TOPK):
                    for t in range(TT):
                        dst = Wt if k == 0 else Wtmp
                        st(V.tensor_scalar(dst[:, t, :], iota, pk[:, k, t:t + 1], gk[:, k, t:t + 1],
                                           ALU.is_equal, ALU.mult))
                    if k == TOPK - 1:
                        V.tensor_tensor(Wt, Wt, Wtmp, ALU.add).then_inc(S["wt_rdy"], 1)
                    elif k:
                        st(V.tensor_tensor(Wt, Wt, Wtmp, ALU.add))

            def advance(st):
                st(V.tensor_scalar(pk, pk, -128.0, None, ALU.add))

            def rows_of(p):
                src = ohI[:, bass.ds(p * 2, 2)] if not isinstance(p, int) else ohI[:, 2 * p:2 * p + 2]
                V.tensor_copy(mask, src.unsqueeze(2).to_broadcast([P, 2, SLOTS])).then_inc(S["mask_rdy"], 1)

            def gathered(p):
                for half in range(2):
                    v.wait_ge(S["ga_done"], p * 2 + (half + 1))
                    V.tensor_copy(hTp[:, 4 * half:4 * half + 4, :].rearrange("p k s -> p (k s)"), ps[:, 7 - half, :])\
                        .then_inc(S["ga_sb"], 1)

            def placed(p):
                v.wait_ge(S["pt_done"], p + 1)
                V.tensor_copy(Pw.rearrange("p t q -> p (t q)"), ps[:, 7, 0:256]).then_inc(S["pt_sb"], 1)

            select(step)
            rows_of(0)
            gathered(0)
            v.wait_ge(S["top_exp"], 1)
            step(V.tensor_tensor(gsum, gexp[:, 0, :], gexp[:, 1, :], ALU.add))
            step(V.tensor_tensor(gsum, gsum, gexp[:, 2, :], ALU.add))
            step(V.tensor_tensor(gsum, gsum, gexp[:, 3, :], ALU.add))
            step(V.reciprocal(gden, gsum))
            step(V.tensor_tensor(gk, gexp, gden.unsqueeze(1).to_broadcast([P, TOPK, TT]), ALU.mult))
            for k in range(TOPK):
                g2 = gk[:, k, :].unsqueeze(2).to_broadcast([P, TT, E])
                if k == 0:
                    sig(v, V.tensor_tensor(G, oh[:, 0, :, :], g2, ALU.mult), "g_all", 1)
                else:
                    step(V.tensor_tensor(wrk, oh[:, k, :, :], g2, ALU.mult))
                    sig(v, V.tensor_tensor(G, G, wrk, ALU.add), "g_all", k + 1)
            step(V.tensor_tensor(cmpI, inc.unsqueeze(1).to_broadcast([P, EXTRA, E]),
                                 tab("item")[:, 0:EXTRA].unsqueeze(2).to_broadcast([P, EXTRA, E]), ALU.is_le))
            step(V.tensor_reduce(ef[:, E:ITEMS], cmpI, AX.X, ALU.add))
            step(V.tensor_scalar(ef[:, E:ITEMS], ef[:, E:ITEMS], float(E - 1), None, ALU.min))
            step(V.memset(ohI[:, ITEMS:ITEMS + 2], 0.0))
            step(V.tensor_scalar(ohI[:, E:ITEMS], ef[:, E:ITEMS], lane, None, ALU.is_equal))
            step(V.tensor_scalar(tmpe[:, 0:8], tab("odd"), exc[:, 40:41], None, ALU.is_le))
            step(V.tensor_reduce(pairs_f[:, 0:1], tmpe[:, 0:8], AX.X, ALU.add))
            step(V.tensor_scalar(pairs_f[:, 0:1], pairs_f[:, 0:1], float(E // 2), None, ALU.add))
            sig(v, V.tensor_copy(table_i[0:1, 0:ITEMS], ef[0:1, :]), "tables", 1)
            step(V.tensor_scalar(pairs_f[:, 1:2], pairs_f[:, 0:1], -1.0, None, ALU.add))
            sig(v, V.tensor_copy(table_i[0:1, 48:50], pairs_f[0:1, 0:2]), "tables", 2)
            activate(0, step)
            weigh(step)
            advance(step)
            v.wait_ge(S["sel_rdy"], 1)
            select(step)
            activate(1, step)
            v.wait_ge(S["gu_used"], 16)
            rows_of(1)
            gathered(1)
            placed(0)
            v.wait_ge(S["tables"], 2)
            n_pairs = v.value_load(table_i[0:1, 48:49], min_val=E // 2, max_val=ITEMS // 2)
            PER = 2 * 2 + (TOPK * TT + TOPK - 2) + 1 + (TOPK * TT - 1)
            with v.Fori(1, n_pairs) as p:
                st = Steps(v, S["dve_loop"], p * PER - PER)
                activate(p * 2, st)
                v.wait_ge(S["pt_done"], p)
                weigh(st)
                v.wait_ge(S["wt_rdy"], p + 1)
                advance(st)
                v.wait_ge(S["ga_done"], p * 2 + 2)
                select(st)
                activate(p * 2 + 1, st)
                rows_of(p + 1)
                gathered(p + 1)
                placed(p)
                assert st.n == PER, (st.n, PER)
            v.wait_ge(S["sc_done"], n_pairs)
            v.wait_ge(S["fg_in"], 16)
            for t in range(TT):
                for h in range(2):
                    step(V.tensor_tensor(u_sb, ps[:, 2 * t + h, :], gate2B[:, 512 * h:512 * (h + 1)], ALU.mult))
                    xs = x[:, t, 512 * h:512 * (h + 1)]
                    sig(v, V.tensor_tensor(xs, xs, u_sb, ALU.add), "x2_rdy", 2 * t + h + 1)
            for t in range(TT):
                v.wait_ge(S["fin_sq"], t + 1)
                rstd(rs[:, t:t + 1], ss[:, t:t + 1], D)
                V.scalar_tensor_tensor(fin[:, t, :], x[:, t, :], rs[:, t:t + 1], fgB, ALU.mult, ALU.mult)\
                    .then_inc(S["fin_rdy"], 1)


def kernel(**inputs):
    import numpy as np
    import concourse.bacc as bacc
    from concourse.bass_utils import run_bass_kernel_spmd

    nc = bacc.Bacc("TRN2", target_bir_lowering=False, num_devices=1)
    arrays, aps = {}, {}
    for name, value in list(inputs.items()) + list(host_tables().items()):
        v = np.ascontiguousarray(value)
        arrays["in_" + name] = v
        aps[name] = nc.dram_tensor("in_" + name, v.shape, mybir.dt.from_np(v.dtype), kind="ExternalInput").ap()
    out = nc.dram_tensor("out_0", (1, L, D), F32, kind="ExternalOutput").ap()
    build(nc, aps, out)
    r = run_bass_kernel_spmd(nc, [arrays], core_ids=[0])
    return r.results[0]["out_0"]
```

```python
import math
from contextlib import ExitStack

import concourse.bass as bass
from concourse import mybir

F32 = mybir.dt.float32
I32 = mybir.dt.int32
ALU = mybir.AluOpType
ACT = mybir.ActivationFunctionType
AX = mybir.AxisListType

P = 128
D = 1024
L = 256
TT = L // P
KD = D // P
HW = 512
CT = HW // P
HEADS = 4
E = 32
TOPK = 4
FE = 1024
SLOTS = 64
ITEMS = 48
EXTRA = ITEMS - E
EPS = 1e-5
LAM_INIT = 0.2
SLOPES = [2.0 ** (-8.0 * (h + 1) / HEADS) for h in range(HEADS)]
TWO_PI = 2.0 * math.pi

TAB = {}
_at = 0
for _name, _w in (("ident", P), ("tri", P), ("iota", P), ("ones", P), ("lane", 1), ("erev", E), ("odd", 8), ("quad", E),
                  ("item", ITEMS), ("dist", TT * L)):
    TAB[_name] = (_at, _w)
    _at += _w
TABW = _at


def host_tables():
    import numpy as np
    t = np.arange(L)
    f = np.arange(L)
    ang = 2.0 * np.pi * np.outer(t, f) / (2 * L)
    dft = np.concatenate([np.cos(ang), np.sin(ang)], axis=1)
    dft[:, L] = np.cos(np.pi * t)
    wt = np.full(2 * L, 2.0)
    wt[0] = wt[L] = 1.0
    inv = (dft * wt[None, :] / (2 * L)).T
    tl = np.linspace(0.0, 1.0, L, dtype=np.float32)[:, None]
    w = (np.float32(2.0 * math.pi) * np.arange(L, dtype=np.float32)[:, None] / np.float32(L)).astype(np.float32)
    fr = np.linspace(1e-4, 7, 8, dtype=np.float32)[None, :]
    z = np.concatenate([tl, np.cos(fr * w), -np.sin(fr * w)], axis=1)
    deltas = np.linspace(math.log(1e-2) / 1.5, math.log(1e-2) / 0.3, HW, dtype=np.float32)
    decay = np.exp(-tl * np.abs(deltas))
    back = decay.copy()
    back[0] = 0.0
    tab = np.zeros((P, TABW), np.float32)
    put = lambda n, v: tab.__setitem__((slice(None), slice(TAB[n][0], TAB[n][0] + TAB[n][1])), v)
    r = np.arange(P)
    put("ident", np.eye(P))
    put("tri", (r[:, None] < r[None, :]).astype(np.float32))
    put("iota", r[None, :])
    put("ones", 1.0)
    put("lane", r[:, None])
    put("erev", E - np.arange(E)[None, :])
    put("odd", 1 + 2 * np.arange(8)[None, :])
    put("quad", (r[:, None] % E == np.arange(E)[None, :]).astype(np.float32))
    put("item", np.arange(ITEMS)[None, :])
    dist = np.abs(np.arange(L)[:, None] - np.arange(L)[None, :]).reshape(TT, P, L)
    put("dist", dist.transpose(1, 0, 2).reshape(P, TT * L))
    c = lambda a: np.ascontiguousarray(a, np.float32)
    return {"t_small": tab, "t_dft": c(dft), "t_inv": c(inv), "t_z": c(z.T),
            "t_decay": c(np.stack([decay, back]))}


def build(nc, a, out):
    with ExitStack() as ctx:
        regions = {}
        top = [0]

        def region(name, words):
            regions[name] = (top[0], words)
            top[0] += words

        for name, words in (
                ("ring", 24576), ("x", 2048), ("xn", 2048), ("ht", 2048), ("ur", 12 * 258), ("uc", 3072),
                ("kf", 2560), ("dft", 1024), ("inv", 1024), ("qm", 2048), ("kt", 1024), ("ve", 1024),
                ("sc", 1024), ("ab", 512), ("at", 512), ("on", 512), ("adr", 1536),
                ("tab", TABW), ("prm", 128), ("prmT", 128), ("lam", 256), ("bv", 512), ("br", 32),
                ("cs", 256), ("modc", 48), ("tiny", 886)):
            region(name, words)
        arena = ctx.enter_context(nc.sbuf_tensor("arena", [P, top[0]], F32))
        table_i = ctx.enter_context(nc.sbuf_tensor("table_i", [1, 64], I32))
        ps = ctx.enter_context(nc.psum_tensor("ps", [P, 8, 512], F32))

        def at(name, off=0, words=None):
            o, w = regions[name]
            words = w - off if words is None else words
            assert off + words <= w, name
            return arena[:, o + off:o + off + words]

        def tab(name):
            o, w = TAB[name]
            return at("tab", o, w)

        def span(name, off, words):
            o = regions[name][0] + off
            return arena[:, o:o + words]

        ident, tri, iota, ones, lane = tab("ident"), tab("tri"), tab("iota"), tab("ones"), tab("lane")
        dist = tab("dist").rearrange("p (q k) -> p q k", q=TT)

        ring = [at("ring", 4096 * s, 4096) for s in range(6)]
        gu_slot = [at("ring", 2048 * k, 2048) for k in range(KD)]
        early_slot = [span("ur", 2048, 2048), span("ur", 4096, 2048), span("on", 0, 2048), span("dft", 0, 2048)]
        b_down = early_slot[0][:, 0:D]
        dn_slot = [at("ring", 2048 * (KD + c), 2048).rearrange("p (q n) -> p q n", q=2) for c in range(4)]

        x = at("x").rearrange("p (t d) -> p t d", t=TT)
        xn = at("xn").rearrange("p (t d) -> p t d", t=TT)
        gate_hy = at("xn").rearrange("p (c t) -> p c t", c=KD)
        hT = at("ht").rearrange("p (k t) -> p k t", k=KD)
        uraw = at("ur").rearrange("p (c t) -> p c t", c=12)
        Y = at("ur", 0, 2048).rearrange("p (f c) -> p f c", f=4)
        vtc = at("ur", 2048, 1024).rearrange("p (t c) -> p t c", t=TT)
        merged = at("ur", 0, 2048).rearrange("p (c t) -> p c t", c=KD)
        ucv = at("uc").rearrange("p (c t) -> p c t", c=12)
        x0T, x1T, vT = ucv[:, 0:4], ucv[:, 4:8], ucv[:, 8:12]
        y_hyT, y_atT = x0T, x1T
        gate_at = [ucv[:, 8 + i, :] if i < 4 else at("ur", 2048 + 256 * (i - 4), 256) for i in range(KD)]
        w4 = at("ur", 0, 1024)
        kplus = at("ur", 1024, 1024).rearrange("p (t c) -> p t c", t=TT)
        kback = at("on")
        kminus = at("uc", 2048, 1024).rearrange("p (t c) -> p t c", t=TT)
        decay = at("uc", 0, 2048).rearrange("p (s t c) -> p s t c", s=2, t=TT)
        kA = at("kf", 0, 1024).rearrange("p (f c) -> p f c", f=2)
        kN = at("kf", 1024, 512)
        kB = at("kf", 1536, 1024).rearrange("p (f c) -> p f c", f=2)
        dft = at("dft").rearrange("p (t f) -> p t f", t=TT)
        inv = at("inv").rearrange("p (f t) -> p f t", f=4)
        qm = at("qm").rearrange("p (h c t) -> p h c t", h=HEADS, c=2)
        kT = at("kt").rearrange("p (h t) -> p h t", h=HEADS)
        ve = at("ve").rearrange("p (t e) -> p t e", t=TT)
        sc = [at("sc", 512 * j, 512).rearrange("p (c k) -> p c k", c=2) for j in range(2)]
        flat = [at("sc", 512 * j, 512) for j in range(2)]
        ab = [at("ab", 256 * j, 256) for j in range(2)]
        aT = [at("at", 256 * j, 256).rearrange("p (k q) -> p k q", k=TT) for j in range(2)]
        on = at("on")
        adr = [at("adr", 512 * g, 512) for g in range(3)]
        gain = at("at")
        prm, prmT = at("prm"), at("prmT")
        cs = at("cs").rearrange("p (k r) -> p k r", k=KD)
        wr = at("lam").rearrange("p (k e) -> p k e", k=KD)
        wr_scaled = at("cs").rearrange("p (k e) -> p k e", k=KD)
        modc = at("modc").rearrange("p (g q j) -> p g q j", g=3, q=4)
        gate1B = at("dft")
        gate2B, fgB = at("qm", 0, 1024), at("qm", 1024, 1024)
        shB, gsB = at("kt"), at("ve")
        sel_bias = at("kf", 0, 2048)

        tiny_at = [0]

        def tiny(words):
            o = tiny_at[0]
            tiny_at[0] += words
            return at("tiny", o, words)

        ss, rs = tiny(2), tiny(2)
        lamcol, lam2, negm, sums, rinv, rlam = tiny(1), tiny(2), tiny(4), tiny(4), tiny(4), tiny(2)
        oss, ors, nwt = tiny(4), tiny(4), tiny(8)
        log = tiny(64).rearrange("p (t e) -> p t e", t=TT)
        oh = tiny(256).rearrange("p (k t e) -> p k t e", k=TOPK, t=TT)
        wrk = tiny(64).rearrange("p (t e) -> p t e", t=TT)
        topv = tiny(8).rearrange("p (k t) -> p k t", k=TOPK)
        km = tiny(2)
        gexp = tiny(8).rearrange("p (k t) -> p k t", k=TOPK)
        gsum, gden = tiny(2), tiny(2)
        gk = tiny(8).rearrange("p (k t) -> p k t", k=TOPK)
        pk = tiny(8).rearrange("p (k t) -> p k t", k=TOPK)
        M = tiny(64).rearrange("p (t e) -> p t e", t=TT)
        G = tiny(64).rearrange("p (t e) -> p t e", t=TT)
        nov, exc, inc, tmpe = tiny(32), tiny(48), tiny(32), tiny(32)
        cntT = at("prm")
        ef = tiny(ITEMS)
        ohI = tiny(ITEMS + 2)
        pairs_f = tiny(2)
        
        cmpI = at("ab").rearrange("p (i e) -> p i e", i=EXTRA)
        pos_k = at("sc", 0, 256).rearrange("p (k t e) -> p k t e", k=TOPK, t=TT)
        part = at("sc", 512, 256)
        wrk2 = at("sc", 768, 64).rearrange("p (t e) -> p t e", t=TT)
        rank = at("sc", 832, 64).rearrange("p (t e) -> p t e", t=TT)
        cntT2 = at("sc", 256, 128)
        GT = at("at", 0, 256)
        hTp = at("ht", 0, 1024).rearrange("p (k s) -> p k s", k=KD)
        Sel = at("ht", 1024, 256).rearrange("p (t s) -> p t s", t=TT)
        Wt = at("ht", 1280, 256).rearrange("p (t s) -> p t s", t=TT)
        Wtmp = at("ht", 1536, 256).rearrange("p (t s) -> p t s", t=TT)
        Pw = at("ht", 1792, 256).rearrange("p (t q) -> p t q", t=TT)
        y = at("ur", 0, 1024)
        actT = at("ur", 1024, 512).rearrange("p (j s) -> p j s", j=4)
        act_o = at("ur", 1536, 512)
        u_sb, s_sb, t_sb, g_sb = at("kt", 0, 512), at("kt", 512, 512), at("ve", 0, 512), at("ve", 512, 512)
        mask = at("cs", 0, 128).rearrange("p (i s) -> p i s", i=2)
        fin = at("xn").rearrange("p (t d) -> p t d", t=TT)

        zT = at("sc", 0, 256)
        w1, w2, w3 = at("sc", 256, 64), at("sc", 320, 64), at("sc", 384, 64)
        hid = at("qm", 0, 256)
        ang, turns = at("kt", 0, 256), at("kt", 256, 256)

        C_C, C_BHY, C_BQ, C_BK, C_BG, C_W, C_CB, C_DS, C_SG, C_F = 0, 8, 20, 24, 28, 44, 80, 92, 96, 97

        def col(c, p0=0, p1=P):
            return prmT[p0:p1, c:c + 1]

        def sem(name):
            return ctx.enter_context(nc.semaphore(name))

        names = """tab_in x_in prm_in filt_in decay_in dft_in inv_in ada_in lam_in bv_in br_in wr_in gain_in
            gub_in bd_in fg_in gub_zero out_done
            prm_zero qm_zero pad_zero prmT_ps prmT_sb sig_c silu_c
            f1_ps f2_ps f3_ps f4_ps ang_1 ang_2 ang_3 hid_1 hid_2 hid_3 filt_sb
            x_sq xn_rdy xT_ps ada_used ada0_sb ada1_sb ada2_sb mc0_ps mc1_ps mc2_ps
            mc0_sb mc1_sb mc2_sb h1_sb kA_ps kN_ps kB_ps kA_sb kf_done
            u_ps u_sb v_sb vT_rdy vt_ps vt_sb V_ps Y_rdy yT_ps yhy_rdy lam_a lam_e
            s_ps s_sb negm_rdy exp_done a_rdy aT_ps aT_sb o_ps o_sq on_rdy oT_ps oT_sb
            g1_ps g1_sb rb_ps rb_sb pj_ps pj_sb gat_rdy mix_ps x1_rdy x2_rdy x1_sq rs_rdy xs_rdy x1T_ps bc_ps bc_sb
            x1T_dve x1T_act part_ps part_sb log_ps top_rdy top_exp m_rdy rank_ps cnt_ps cnt_sb ex_ps g_all gt_ps gt_sb tables h2_rdy
            gu_used dn_used tr_done sc_done ga_done pt_done
            g_rdy sig_rdy act_rdy actT_rdy y_rdy ga_sb pt_sb sel_rdy wt_rdy mask_rdy
            sc_tile fin_sq fin_rdy dve_step act_step dve_loop pool_step""".split()
        S = {n: sem(n) for n in names}
        s_front = [sem(f"front_in{j}") for j in range(6)]
        s_gu = [sem(f"gate_up_in{k}") for k in range(KD)]
        s_early = [sem(f"early_in{k}") for k in range(4)]
        s_dn = [sem(f"down_in{c}") for c in range(4)]

        class Steps:

            def __init__(self, eng, s, base=0):
                self.eng, self.s, self.base, self.n = eng, s, base, 0

            def __call__(self, ins):
                ins.then_inc(self.s, 1)
                self.n += 1
                self.eng.wait_ge(self.s, self.base + self.n)

            def start(self, ins):
                ins.then_inc(self.s, 1)
                self.n += 1

        def sig(eng, ins, name, value):
            ins.then_inc(S[name], 1)
            eng.wait_ge(S[name], value)

        w_ada, w_in = a["w_ada"], a["w_in"]
        blocks = [("ada", 0, j) for j in range(4)]
        for j in range(6):
            blocks += [("in", j, 0)] + ([("ada", 1, j)] if j < 4 else [("ada", 2, 2 * j - 8), ("ada", 2, 2 * j - 7)])
        blocks += [("in", j, 0) for j in range(6, 10)] + [("hy", 0, 0), ("att", 0, 0), ("mix", 0, 0), ("mix", 1, 0)]
        where = {b: n for n, b in enumerate(blocks)}

        def block_source(b):
            kind, i, j = b
            if kind == "ada":
                return w_ada[0, 256 * j:256 * (j + 1), 2048 * i:2048 * (i + 1)].rearrange("(k p) n -> p k n", p=P)
            if kind == "in":
                return w_in[0, :, 512 * i:512 * (i + 1)].rearrange("(k p) n -> p k n", p=P)
            if kind == "hy":
                return a["w_hy_out"][0].rearrange("(k p) n -> p k n", p=P)
            if kind == "att":
                return a["w_attn_out"][0].rearrange("(k p) n -> p k n", p=P)
            return a["w_mix_out"][0, 512 * i:512 * (i + 1), :].rearrange("(k p) n -> p k n", p=P)

        def block_view(b):
            kind = b[0]
            k = {"ada": 2, "in": 8, "hy": 4, "att": 4, "mix": 4}[kind]
            return ring[where[b] % 6].rearrange("p (k n) -> p k n", k=k)

        w_gu, w_dn = a["w_gate_up"], a["w_down"]
        block = ctx.enter_context(nc.Block())

        @block.sync
        def _(sp):
            def wait_used(b):
                kind, i, j = b
                if kind == "ada":
                    sp.wait_ge(S["ada_used"], 4 * i + j + 1)
                elif kind == "in":
                    sp.wait_ge(S["u_ps"], 2 * i + 2)
                elif kind == "mix":
                    sp.wait_ge(S["mix_ps"], i + 3)
                else:
                    sp.wait_ge(S["pj_ps"], KD)

            sp.dma_start(at("tab"), a["t_small"]).then_inc(S["tab_in"], 16)
            sp.wait_ge(S["prm_zero"], 1)
            rows = lambda v: v.rearrange("(r n) -> r n", n=P)
            pieces = [(C_C, 8, rows(a["c"][0])), (C_BHY, 20, rows(a["b_in"][0, 0:2560])),
                      (C_BG, 16, rows(a["b_in"][0, 3072:5120])),
                      (C_W, 12, rows(a["hy_conv_w"][0, 0])), (C_W + 12, 12, rows(a["hy_conv_w"][0, 1])),
                      (C_W + 24, 12, rows(a["hy_conv_w"][0, 2])), (C_CB, 12, rows(a["hy_conv_b"][0])),
                      (C_DS, 4, rows(a["hy_d_skip"][0])), (C_SG, 1, a["attn_subln_g"])]
            for r0, n, src in pieces:
                sp.dma_start(prm[r0:r0 + n, :], src).then_inc(S["prm_in"], 16)
            for r, name in ((C_F, "filt_b1"), (C_F + 1, "filt_b2"), (C_F + 2, "filt_b3"), (C_F + 3, "filt_freq")):
                sp.dma_start(prm[r:r + 1, 0:64], a[name]).then_inc(S["prm_in"], 16)
            for n, b in enumerate(blocks):
                if n >= 6:
                    wait_used(blocks[n - 6])
                sp.dma_start(block_view(b), block_source(b)).then_inc(s_front[n % 6], 16)

            def gate_up(k, expert):
                sp.dma_start(gu_slot[k], w_gu[0, expert, k * P:(k + 1) * P, :]).then_inc(s_gu[k], 16)

            def early(k):
                sp.dma_start(early_slot[k], w_gu[0, 1, k * P:(k + 1) * P, :]).then_inc(s_early[k], 16)

            def down(c, expert):
                sp.dma_start(dn_slot[c], w_dn[0, expert, c * 256:(c + 1) * 256, :].rearrange("(q p) n -> p q n", p=P))\
                    .then_inc(s_dn[c], 16)

            def gate_up_dyn(k, e):
                sp.dma_start(gu_slot[k], w_gu[0, bass.ds(e, 1), k * P:(k + 1) * P, :].rearrange("o p n -> p (o n)"))\
                    .then_inc(s_gu[k], 16)

            def down_dyn(c, e):
                sp.dma_start(dn_slot[c], w_dn[0, bass.ds(e, 1), c * 256:(c + 1) * 256, :]
                             .rearrange("o (q p) n -> p (o q) n", p=P)).then_inc(s_dn[c], 16)

            last_use = {n % 6: n for n in range(len(blocks))}
            for f in sorted(range(6), key=lambda s: last_use[s]):
                if blocks[last_use[f]] == ("mix", 0, 0):
                    sp.wait_ge(S["pj_sb"], KD)
                    early(0)
                    early(1)
                wait_used(blocks[last_use[f]])
                for k in (2 * f, 2 * f + 1):
                    gate_up(k, 0) if k < KD else down(k - KD, 0)
            sp.wait_ge(S["bc_ps"], 6)
            early(2)
            sp.wait_ge(S["x1_rdy"], 4)
            early(3)
            for k in range(4, KD):
                sp.wait_ge(S["gu_used"], k + 1)
                gate_up(k, 1)
            sp.wait_ge(S["tables"], 2)
            n_pairs = sp.value_load(table_i[0:1, 48:49], min_val=E // 2, max_val=ITEMS // 2)
            with sp.Fori(1, n_pairs) as p:
                e_prev = sp.value_load(table_i[0:1, bass.ds(p * 2 - 1, 1)], min_val=0, max_val=E - 1)
                e_a = sp.value_load(table_i[0:1, bass.ds(p * 2, 1)], min_val=0, max_val=E - 1)
                e_b = sp.value_load(table_i[0:1, bass.ds(p * 2 + 1, 1)], min_val=0, max_val=E - 1)
                for k in range(KD):
                    sp.wait_ge(S["gu_used"], p * 16 - 8 + (k + 1))
                    gate_up_dyn(k, e_a)
                for c in range(4):
                    sp.wait_ge(S["dn_used"], p * 8 - 8 + (c + 1))
                    down_dyn(c, e_prev)
                for k in range(KD):
                    sp.wait_ge(S["gu_used"], p * 16 + (k + 1))
                    gate_up_dyn(k, e_b)
                for c in range(4):
                    sp.wait_ge(S["dn_used"], p * 8 - 4 + (c + 1))
                    down_dyn(c, e_a)
            e_last = sp.value_load(table_i[0:1, bass.ds(n_pairs * 2 - 1, 1)], min_val=0, max_val=E - 1)
            last_pair = sp.value_load(table_i[0:1, 49:50], min_val=E // 2 - 1, max_val=ITEMS // 2 - 1)
            for c in range(4):
                sp.wait_ge(S["dn_used"], last_pair * 8 + (c + 1))
                down_dyn(c, e_last)
            for t in range(TT):
                sp.wait_ge(S["fin_rdy"], t + 1)
                sp.dma_start(out[0, t * P:(t + 1) * P, :], fin[:, t, :]).then_inc(S["out_done"], 16)
            sp.wait_ge(S["out_done"], 16 * TT)

        @block.gpsimd
        def _(pool):
            nc.gpsimd.memset(prm, 0.0).then_inc(S["prm_zero"], 1)
            pool.dma_start(at("lam"), a["lambda_qk"][0].rearrange("a b -> (a b)").partition_broadcast(P))\
                .then_inc(S["lam_in"], 16)
            pool.dma_start(decay, a["t_decay"].rearrange("s (t p) c -> p s t c", p=P)).then_inc(S["decay_in"], 16)
            pool.dma_start(dft, a["t_dft"].rearrange("(t p) f -> p t f", p=P)).then_inc(S["dft_in"], 16)
            pool.wait_ge(S["filt_sb"], TT)
            nc.gpsimd.memset(at("qm"), 0.0).then_inc(S["qm_zero"], 1)
            pool.wait_ge(S["kB_ps"], 2)
            nc.gpsimd.memset(uraw[:, :, 0:1], 0.0).then_inc(S["pad_zero"], 1)
            nc.gpsimd.memset(uraw[:, :, 257:258], 0.0).then_inc(S["pad_zero"], 1)
            pool.wait_ge(S["Y_rdy"], 2)
            nc.gpsimd.memset(sel_bias, 0.0).then_inc(S["gub_zero"], 1)
            pool.wait_ge(S["gub_zero"], 1)
            pool.dma_start(sel_bias[0:E, :], a["b_gate_up"][0]).then_inc(S["gub_in"], 16)
            pool.wait_ge(S["s_ps"], 8)
            pool.dma_start(fgB, a["final_norm_g"][:].partition_broadcast(P)).then_inc(S["fg_in"], 16)
            pool.wait_ge(S["bc_sb"], 4)
            for t in range(TT):
                pool.wait_ge(S["xs_rdy"], t + 1)
                nc.gpsimd.tensor_tensor(xn[:, t, :], xn[:, t, :], gsB, ALU.mult).then_inc(S["pool_step"], 1)
                pool.wait_ge(S["pool_step"], t + 1)
                nc.gpsimd.tensor_tensor(xn[:, t, :], xn[:, t, :], shB, ALU.add).then_inc(S["h2_rdy"], 1)
            pool.wait_ge(S["gu_used"], KD + 1)
            pool.dma_start(b_down[0:E, :], a["b_down"][0]).then_inc(S["bd_in"], 16)

        @block.tensor
        def _(pe):
            mm = pe.matmul

            def bank(b, n=512, o=0):
                return ps[:, b, o:o + n]

            def front_in(b):
                n = where[b]
                pe.wait_ge(s_front[n % 6], 16 * (n // 6 + 1))
                return block_view(b)

            pe.wait_ge(S["tab_in"], 16)
            pe.wait_ge(S["prm_in"], 16 * 13)
            pe.transpose(bank(3, 128), prm, ident).then_inc(S["prmT_ps"], 1)
            pe.wait_ge(S["filt_in"], 16 * 5)
            mm(ps[0:64, 0, 0:256], w1[0:17, :], zT[0:17, :], start=True, stop=True).then_inc(S["f1_ps"], 1)
            pe.wait_ge(S["hid_1"], 1)
            mm(ps[0:64, 1, 0:256], w2[0:64, :], hid[0:64, :], start=True, stop=True).then_inc(S["f2_ps"], 1)
            pe.wait_ge(S["hid_2"], 1)
            mm(ps[0:64, 2, 0:256], w3[0:64, :], hid[0:64, :], start=True, stop=True).then_inc(S["f3_ps"], 1)
            def ada(g, b, js):
                for j in js:
                    w = front_in(("ada", g, j))
                    for kk in range(2):
                        k = 2 * j + kk
                        for q in range(4):
                            last = mm(ps[32 * q:32 * q + 32, b, :], cs[:, k, :], w[:, kk, q * 512:(q + 1) * 512],
                                      start=(k == 0), stop=(k == KD - 1))
                    last.then_inc(S["ada_used"], 1)

            def ada_cols(g, b):
                for j in range(4):
                    last = pe.transpose(bank(b, 128, j * 128), adr[g][:, j * P:(j + 1) * P], ident)
                return last

            def rows_turned(ks):
                for k in ks:
                    for t in range(TT):
                        last = pe.transpose(bank(k // 2, 128, (k % 2) * 256 + t * 128), xn[:, t, k * P:(k + 1) * P],
                                            ident)
                return last

            pe.wait_ge(S["silu_c"], 1)
            pe.wait_ge(S["prmT_sb"], 1)
            ada(0, 3, (0,))
            pe.wait_ge(S["hid_3"], 1)
            for s in range(2):
                for t in range(TT):
                    mm(bank(4 + 2 * s + t), hid[0:64, t * P:(t + 1) * P], w4[0:64, s * HW:(s + 1) * HW],
                       start=True, stop=True).then_inc(S["f4_ps"], 1)
            ada(0, 3, (1,))
            pe.wait_ge(S["xn_rdy"], 1)
            rows_turned(range(6))
            ada(0, 3, (2, 3))

            pe.wait_ge(S["dft_in"], 16)
            pe.wait_ge(S["filt_sb"], TT)

            def spectrum(b, f0, taps):
                for t in range(TT):
                    last = mm(bank(b), dft[:, t, f0:f0 + P], taps[:, t, :], start=(t == 0), stop=(t == TT - 1))
                return last

            spectrum(6, 0, kplus)
            spectrum(7, 128, kplus).then_inc(S["kA_ps"], 1)
            pe.wait_ge(S["ada0_sb"], 2)
            ada_cols(0, 5).then_inc(S["mc0_ps"], 1)
            rows_turned((6, 7)).then_inc(S["xT_ps"], 1)
            spectrum(4, 256, kplus).then_inc(S["kN_ps"], 1)
            pe.wait_ge(S["mc0_sb"], 1)
            spectrum(5, 256, kminus).then_inc(S["kB_ps"], 1)
            pe.wait_ge(S["kA_sb"], 1)
            spectrum(6, 384, kminus).then_inc(S["kB_ps"], 1)

            pe.wait_ge(S["h1_sb"], 1)

            def unit(n):
                blk, half = n // 2, n % 2
                w = front_in(("in", blk, 0))
                if n >= 3:
                    m = n - 3
                    if m in (10, 11):
                        pe.wait_ge(S["v_sb"], m - 9)
                    else:
                        pe.wait_ge(S["u_sb"], m + 1 if m < 10 else m - 1)
                b = n % 3
                if blk == 5:
                    for k in range(KD):
                        last = mm(bank(b), hT[:, k, half * P:(half + 1) * P], w[:, k, :],
                                  start=(k == 0), stop=(k == KD - 1))
                else:
                    for c in range(2):
                        cc = 2 * half + c
                        for k in range(KD):
                            last = mm(bank(b, 256, c * 256), w[:, k, cc * P:(cc + 1) * P], hT[:, k, :],
                                      start=(k == 0), stop=(k == KD - 1))
                last.then_inc(S["u_ps"], 1)

            for blk in range(6):
                unit(2 * blk)
                unit(2 * blk + 1)
                if blk == 0:
                    pe.wait_ge(S["kf_done"], 1)
                if blk < 4:
                    ada(1, 6, (blk,))
                else:
                    ada(2, 7, (2 * blk - 8, 2 * blk - 7))
            pe.wait_ge(S["vT_rdy"], 1)
            for t in range(TT):
                for c in range(CT):
                    last = pe.transpose(bank(3 + t, 128, c * 128), vT[:, c, t * P:(t + 1) * P], ident)
                last.then_inc(S["vt_ps"], 1)
            unit(12)
            pe.wait_ge(S["vt_sb"], 2)
            unit(13)
            pe.wait_ge(S["ada1_sb"], 1)
            pe.wait_ge(S["ada2_sb"], 1)
            for f in range(4):
                for t in range(TT):
                    last = mm(bank(4 + f), dft[:, t, f * P:(f + 1) * P], vtc[:, t, :],
                              start=(t == 0), stop=(t == TT - 1))
                last.then_inc(S["V_ps"], 1)
            unit(14)
            unit(15)
            pe.wait_ge(S["Y_rdy"], 2)
            pe.wait_ge(S["inv_in"], 16)
            for c in range(CT):
                for f in range(4):
                    last = mm(bank(6 + c // 2, 256, (c % 2) * 256), Y[:, f, c * P:(c + 1) * P], inv[:, f, :],
                              start=(f == 0), stop=(f == 3))
            last.then_inc(S["yT_ps"], 1)

            def scores(j):
                t, h = j // HEADS, j % HEADS
                if j >= 2:
                    pe.wait_ge(S["s_sb"], j - 1)
                for c in range(2):
                    last = mm(bank(4 + j % 2, 256, c * 256), qm[:, h, c, t * P:(t + 1) * P], kT[:, h, :],
                              start=True, stop=True)
                last.then_inc(S["s_ps"], 1)

            def weights_T(j):
                pe.wait_ge(S["a_rdy"], j + 1)
                if j >= 2:
                    pe.wait_ge(S["aT_sb"], j - 1)
                for k in range(TT):
                    last = pe.transpose(bank(3, 128, (j % 2) * 256 + k * 128), ab[j % 2][:, k * P:(k + 1) * P], ident)
                last.then_inc(S["aT_ps"], 1)

            def values(j):
                t, h = j // HEADS, j % HEADS
                pe.wait_ge(S["aT_sb"], j + 1)
                for k in range(TT):
                    last = mm(bank(6 + t, 128, h * 128), aT[j % 2][:, k, :], ve[:, k, h * P:(h + 1) * P],
                              start=(k == 0), stop=(k == TT - 1))
                last.then_inc(S["o_ps"], 1)

            pe.wait_ge(S["u_sb"], 10)
            pe.wait_ge(S["v_sb"], 2)
            scores(0)
            scores(1)
            pe.wait_ge(S["u_sb"], 14)
            pe.wait_ge(S["ada1_sb"], 1)
            ada_cols(1, 0).then_inc(S["mc1_ps"], 1)
            pe.wait_ge(S["ada2_sb"], 2)
            ada_cols(2, 1).then_inc(S["mc2_ps"], 1)

            def spread(b, g, q):
                return mm(bank(b), ident[:, 32 * q:32 * q + 1].to_broadcast([P, P]), adr[g], start=True, stop=True)

            pe.wait_ge(S["mc1_sb"], 1)
            spread(0, 1, 0).then_inc(S["g1_ps"], 1)
            pe.wait_ge(S["mc2_sb"], 1)
            spread(2, 1, 1).then_inc(S["g1_ps"], 1)
            pe.wait_ge(S["wr_in"], 16)
            for k in range(KD):
                last = mm(bank(1, E), modc[:, 1, 2 + k // 4, k % 4:k % 4 + 1].to_broadcast([P, P]), wr[:, k, :],
                          start=(k == 0), stop=(k == KD - 1))
            last.then_inc(S["rb_ps"], 1)

            def attention_gate(i):
                m = i // 2
                if i % 2 == 0:
                    if m == 0:
                        pe.wait_ge(S["g1_sb"], 1)
                    elif m == 1:
                        pe.wait_ge(S["rb_sb"], 1)
                    elif m == 2:
                        pe.wait_ge(S["g1_sb"], 2)
                    elif m == 3:
                        pe.wait_ge(S["u_sb"], 15)
                w = front_in(("in", 8 + m // 2, 0))
                cc = i % 4
                for k in range(KD):
                    last = mm(bank(m % 3, 256, (i % 2) * 256), w[:, k, cc * P:(cc + 1) * P], hT[:, k, :],
                              start=(k == 0), stop=(k == KD - 1))
                if i % 2:
                    last.then_inc(S["u_ps"], 1)

            attention_gate(0)
            pe.wait_ge(S["yhy_rdy"], 1)
            for j in range(2 * HEADS + 1):
                if j < 2 * HEADS:
                    weights_T(j)
                    if j + 2 < 2 * HEADS:
                        scores(j + 2)
                if j >= 1:
                    values(j - 1)
                if j + 1 < KD:
                    attention_gate(j + 1)
            why, wat = front_in(("hy", 0, 0)), front_in(("att", 0, 0))

            def heads_turned(t):
                pe.wait_ge(S["on_rdy"], t + 1)
                for h in range(HEADS):
                    last = pe.transpose(bank(3, 128, h * 128), on[:, h * P:(h + 1) * P], ident)
                last.then_inc(S["oT_ps"], 1)

            def modulation(i):
                if i < 2:
                    pe.wait_ge(S["u_sb"], 18)
                else:
                    pe.wait_ge(S["bc_sb"], i - 1)
                g, q = ((1, 2), (1, 3), (2, 0), (2, 1), (2, 2), (2, 3))[i]
                spread(i % 2, g, q).then_inc(S["bc_ps"], 1)

            def project(i, src, w, o):
                for k in range(CT):
                    last = mm(bank(4 + i % 2, 256, o), w[:, k, i * P:(i + 1) * P], src[:, k, :],
                              start=(k == 0), stop=(k == CT - 1))
                return last

            pe.wait_ge(S["aT_sb"], 2 * HEADS)
            heads_turned(0)
            modulation(0)
            modulation(1)
            project(0, y_hyT, why, 0)
            modulation(2)
            modulation(3)
            pe.wait_ge(S["oT_sb"], 1)
            heads_turned(1)
            project(1, y_hyT, why, 0)
            pe.wait_ge(S["oT_sb"], TT)
            for i in range(KD):
                if i >= 2:
                    pe.wait_ge(S["pj_sb"], i - 1)
                    project(i, y_hyT, why, 0)
                project(i, y_atT, wat, 256).then_inc(S["pj_ps"], 1)
            pe.wait_ge(S["pj_sb"], KD)
            pe.wait_ge(S["bc_sb"], 4)
            mix = [front_in(("mix", i, 0)) for i in range(2)]

            def mixed(t, h, k):
                return mm(bank(2 * t + h), merged[:, k, t * P:(t + 1) * P], mix[k // 4][:, k % 4, h * 512:(h + 1) * 512],
                          start=(k == 0), stop=(k == KD - 1))

            for k in range(KD):
                for h in range(2):
                    last = mixed(0, h, k)
            last.then_inc(S["mix_ps"], 1)
            for k in range(KD):
                last = mixed(1, 0, k)
            last.then_inc(S["mix_ps"], 1)

            def residual_turned(b, t, half):
                for kk in range(4):
                    k = 4 * half + kk
                    last = pe.transpose(bank(b, 128, kk * 128), x[:, t, k * P:(k + 1) * P], ident)
                return last

            pe.wait_ge(S["x1_rdy"], 2)
            residual_turned(4, 0, 0)
            residual_turned(5, 0, 1).then_inc(S["x1T_ps"], 1)
            for k in range(KD):
                last = mixed(1, 1, k)
                if k % 4 == 3:
                    last.then_inc(S["mix_ps"], 1)
            pe.wait_ge(S["x1_rdy"], 3)
            residual_turned(6, 1, 0).then_inc(S["x1T_ps"], 1)

            def router_parts(t):
                for kk in range(2):
                    for q in range(4):
                        last = mm(ps[32 * q:32 * q + 32, 4, 0:P], wr_scaled[:, 2 * q + kk, :],
                                  hT[:, 2 * q + kk, t * P:(t + 1) * P], start=(kk == 0), stop=(kk == 1))
                last.then_inc(S["part_ps"], 1)

            def router_sum(t):
                pe.wait_ge(S["part_sb"], t + 1)
                return mm(bank(5, E, E * t), part[:, t * P:(t + 1) * P], tab("quad"), start=True, stop=True)

            pe.wait_ge(S["rb_sb"], 2)
            pe.wait_ge(S["x1T_dve"], 1)
            router_parts(0)
            pe.wait_ge(S["x1_rdy"], 4)
            residual_turned(7, 1, 1).then_inc(S["x1T_ps"], 1)
            router_sum(0)
            pe.wait_ge(S["x1T_dve"], 2)
            pe.wait_ge(S["x1T_act"], 1)
            router_parts(1)
            router_sum(1).then_inc(S["log_ps"], 1)
            modulation(4)
            modulation(5)
            pe.wait_ge(S["m_rdy"], 1)
            mm(bank(5, 32, 128), tri, M[:, 0, :], start=True, stop=True)
            mm(bank(5, 32, 160), ones, M[:, 0, :], start=True, stop=False)
            mm(bank(5, 32, 160), tri, M[:, 1, :], start=False, stop=True).then_inc(S["rank_ps"], 1)
            mm(bank(2, 32, 0), ones, M[:, 0, :], start=True, stop=False)
            mm(bank(2, 32, 0), ones, M[:, 1, :], start=False, stop=True)
            for t in range(TT):
                last = mm(ps[0:32, 2, 128:256], M[:, t, :], ones, start=(t == 0), stop=(t == TT - 1))
            last.then_inc(S["cnt_ps"], 1)
            def gather(p):
                pe.wait_ge(S["sel_rdy"], p + 1)
                for half in range(2):
                    b = 7 - half
                    for kk in range(4):
                        k = 4 * half + kk
                        for t in range(TT):
                            last = mm(bank(b, 128, kk * 128), xn[:, t, k * P:(k + 1) * P], Sel[:, t, :],
                                      start=(t == 0), stop=(t == TT - 1))
                    last.then_inc(S["ga_done"], 1)

            def gate_up(i, s):
                for b in range(2):
                    for h in range(2):
                        mm(ps[64 * h:64 * h + 64, 4 + b, :], mask[:, s, :],
                           sel_bias[:, b * 1024 + h * 512:b * 1024 + (h + 1) * 512], start=True, stop=False)
                for k in range(KD):
                    early = k < 4 and isinstance(i, int) and i == 1
                    if early:
                        pe.wait_ge(s_early[k], 16)
                    elif k < 4 and not isinstance(i, int):
                        pe.wait_ge(s_gu[k], i * 16)
                    else:
                        pe.wait_ge(s_gu[k], i * 16 + 16)
                    w = early_slot[k] if early else gu_slot[k]
                    for b in range(2):
                        for h in range(2):
                            last = mm(ps[64 * h:64 * h + 64, 4 + b, :], hTp[:, k, s * 64:(s + 1) * 64],
                                      w[:, b * 1024 + h * 512:b * 1024 + (h + 1) * 512],
                                      start=False, stop=(k == KD - 1))
                    last.then_inc(S["gu_used"], 1)

            def act_transpose():
                for j in range(4):
                    last = pe.transpose(bank(7, 128, j * 128), act_o[:, j * P:(j + 1) * P], ident)
                last.then_inc(S["tr_done"], 1)

            def down(i):
                for c in range(4):
                    pe.wait_ge(s_dn[c], i * 16 + 16)
                    for qq in range(2):
                        q = 2 * c + qq
                        lhs = actT[:, q % 4, (q // 4) * 64:(q // 4) * 64 + 64]
                        for h in range(2):
                            last = mm(ps[64 * h:64 * h + 64, 6, :], lhs, dn_slot[c][:, qq, h * 512:(h + 1) * 512],
                                      start=(q == 0), stop=(q == 7))
                    last.then_inc(S["dn_used"], 1)

            def scatter(stop):
                for t in range(TT):
                    for h in range(2):
                        last = mm(bank(2 * t + h), Pw[:, t, :], y[:, h * 512:(h + 1) * 512],
                                  start=False, stop=stop, skip_group_check=True)
                    if stop and t < TT - 1:
                        last.then_inc(S["sc_tile"], 1)
                last.then_inc(S["sc_done"], 1)

            def place_weights():
                for t in range(TT):
                    last = pe.transpose(bank(7, 128, t * 128), Wt[:, t, :], ident)
                last.then_inc(S["pt_done"], 1)

            pe.wait_ge(S["gub_in"], 16)
            pe.wait_ge(S["h2_rdy"], TT)
            gather(0)
            pe.wait_ge(S["cnt_sb"], 2)
            mm(bank(3, 48, 0), cntT2[0:E, :], tri[0:E, 0:48], start=True, stop=True).then_inc(S["ex_ps"], 1)
            pe.wait_ge(S["mask_rdy"], 1)
            pe.wait_ge(S["ga_sb"], 2)
            gate_up(0, 0)
            pe.wait_ge(S["act_rdy"], 1)
            act_transpose()
            gate_up(1, 1)
            pe.wait_ge(S["actT_rdy"], 1)
            pe.wait_ge(S["g_all"], TOPK)
            for t in range(TT):
                last = pe.transpose(ps[0:32, 7, 128 * t:128 + 128 * t], G[:, t, :], ident)
            last.then_inc(S["gt_ps"], 1)
            down(0)
            pe.wait_ge(S["gt_sb"], 1)
            pe.wait_ge(S["bd_in"], 16)
            pe.wait_ge(S["bc_sb"], 6)
            for t in range(TT):
                for h in range(2):
                    mm(bank(2 * t + h), GT[0:E, t * P:(t + 1) * P], b_down[0:E, h * 512:(h + 1) * 512],
                       start=True, stop=False, skip_group_check=True)
            pe.wait_ge(S["act_rdy"], 2)
            act_transpose()
            pe.wait_ge(S["actT_rdy"], 2)
            pe.wait_ge(S["y_rdy"], 1)
            gather(1)
            pe.wait_ge(S["wt_rdy"], 1)
            pe.wait_ge(S["ga_sb"], 3)
            place_weights()
            pe.wait_ge(S["tables"], 2)
            n_pairs = pe.value_load(table_i[0:1, 48:49], min_val=E // 2, max_val=ITEMS // 2)
            with pe.Fori(1, n_pairs) as p:
                pe.wait_ge(S["mask_rdy"], p + 1)
                pe.wait_ge(S["ga_sb"], p * 2 + 2)
                gate_up(p * 2, 0)
                pe.wait_ge(S["actT_rdy"], p * 2)
                down(p * 2 - 1)
                pe.wait_ge(S["act_rdy"], p * 2 + 1)
                pe.wait_ge(S["pt_sb"], p)
                act_transpose()
                gate_up(p * 2 + 1, 1)
                pe.wait_ge(S["y_rdy"], p * 2)
                scatter(False)
                pe.wait_ge(S["actT_rdy"], p * 2 + 1)
                down(p * 2)
                pe.wait_ge(S["act_rdy"], p * 2 + 2)
                act_transpose()
                pe.wait_ge(S["actT_rdy"], p * 2 + 2)
                pe.wait_ge(S["y_rdy"], p * 2 + 1)
                gather(p + 1)
                pe.wait_ge(S["wt_rdy"], p + 1)
                pe.wait_ge(S["ga_sb"], p * 2 + 3)
                place_weights()
            pe.wait_ge(S["ga_sb"], n_pairs * 2 + 2)
            down(n_pairs * 2 - 1)
            pe.wait_ge(S["y_rdy"], n_pairs * 2)
            pe.wait_ge(S["pt_sb"], n_pairs)
            scatter(True)

        @block.scalar
        def _(act):
            A = nc.scalar.activation
            step = Steps(act, S["act_step"])
            for dst, name in ((zT[0:17, :], a["t_z"]), (w1[0:17, :], a["filt_w1"][0]), (w2[0:64, :], a["filt_w2"][0]),
                              (w3[0:64, :], a["filt_w3"][0]), (w4[0:64, :], a["filt_w4"][0])):
                act.dma_start(dst, name).then_inc(S["filt_in"], 16)
            act.dma_start(x, a["x"][0].rearrange("(t p) d -> p t d", p=P)).then_inc(S["x_in"], 16)

            def bias_rows(g, name):
                for q in range(4):
                    o = g * 2048 + q * 512
                    act.dma_start(adr[g][32 * q:32 * q + 32, :], a["b_ada"][0, o:o + 512].partition_broadcast(32))\
                        .then_inc(S[name], 16)

            bias_rows(0, "gain_in")
            for r0, name in ((0, "norm_ffn_g"), (64, "norm_mix_g")):
                for h in range(2):
                    act.dma_start(gain[r0 + 32 * h:r0 + 32 * h + 32, :],
                                  a[name][0, 512 * h:512 * (h + 1)].partition_broadcast(32)).then_inc(S["gain_in"], 16)
            act.wait_ge(S["prmT_sb"], 1)
            sig(act, A(at("cs", 0, 8), prmT[:, C_C:C_C + 8], ACT.Sigmoid), "sig_c", 1)

            def sine(n):
                act.wait_ge(S[f"ang_{n}"], 1)
                A(hid[0:64, :], ang[0:64, :], ACT.Sin).then_inc(S[f"hid_{n}"], 1)

            for n in range(1, 4):
                sine(n)
            act.wait_ge(S["x_in"], 16)
            for t in range(TT):
                A(xn[:, t, :], x[:, t, :], ACT.Square, accum_out=ss[:, t:t + 1]).then_inc(S["x_sq"], 1)
            bias_rows(1, "ada_in")
            bias_rows(2, "ada_in")
            act.dma_start(at("bv"), a["b_in"][0, 2560:3072].partition_broadcast(P)).then_inc(S["bv_in"], 16)
            act.dma_start(at("br"), a["b_router"][0].partition_broadcast(P)).then_inc(S["br_in"], 16)
            act.dma_start(inv, a["t_inv"].rearrange("(f p) t -> p f t", p=P)).then_inc(S["inv_in"], 16)
            act.wait_ge(S["lam_a"], 1)
            sig(act, A(lam2, lam2, ACT.Exp), "lam_e", 1)
            act.dma_start(wr, a["w_router"][0].rearrange("(k p) e -> p k e", p=P)).then_inc(S["wr_in"], 16)
            act.wait_ge(S["kA_ps"], 1)
            step(A(kA[:, 0, :], ps[:, 6, :], ACT.Copy))
            step(A(kN, ps[:, 6, :], ACT.Copy))
            sig(act, A(kA[:, 1, :], ps[:, 7, :], ACT.Copy), "kA_sb", 1)

            def evacuate(n):
                act.wait_ge(S["u_ps"], n + 1)
                for c in range(2):
                    src = ps[:, n % 3, c * 256:(c + 1) * 256]
                    i = 2 * n + c
                    if n < 6:
                        last = A(uraw[:, i, 1:257], src, ACT.Identity, bias=col(C_BHY + i))
                    elif n < 8:
                        h = i - 12
                        for r in range(2):
                            last = A(qm[64 * r:64 * r + 64, h, r, :], src[64 * r:64 * r + 64, :], ACT.Identity,
                                     bias=col(C_BQ + h, 64 * r, 64 * r + 64))
                    elif n < 10:
                        last = A(kT[:, i - 16, :], src, ACT.Identity, bias=col(C_BK + i - 16))
                    else:
                        last = A(gate_hy[:, i - 24, :], src, ACT.Sigmoid, bias=col(C_BG + i - 24))
                last.then_inc(S["u_sb"], 1)

            act.wait_ge(S["qm_zero"], 1)
            act.wait_ge(S["pad_zero"], 2)
            for n in range(10):
                evacuate(n)
            for t in range(TT):
                act.wait_ge(S["vt_ps"], t + 1)
                A(vtc[:, t, :], ps[:, 3 + t, :], ACT.Copy).then_inc(S["vt_sb"], 1)
            for n in range(12, 16):
                evacuate(n)
            for h in range(2):
                act.wait_ge(S["g1_ps"], h + 1)
                A(gate1B[:, 512 * h:512 * (h + 1)], ps[:, 2 * h, :], ACT.Copy).then_inc(S["g1_sb"], 1)
            for j in range(2 * HEADS):
                act.wait_ge(S["negm_rdy"], j + 1)
                for c in range(2):
                    last = A(sc[j % 2][:, c, :], sc[j % 2][:, c, :], ACT.Exp, scale=0.125,
                             bias=negm[:, 2 * (j % 2) + c:2 * (j % 2) + c + 1],
                             accum_out=sums[:, 2 * (j % 2) + c:2 * (j % 2) + c + 1])
                    if c == 1:
                        last.then_inc(S["exp_done"], 1)
                    else:
                        step(last)
                if j % 2:
                    m = j // 2
                    act.wait_ge(S["u_ps"], 17 + m)
                    for c in range(2):
                        last = A(gate_at[2 * m + c], ps[:, m % 3, c * 256:(c + 1) * 256], ACT.Identity,
                                 bias=col(C_BG + 8 + 2 * m + c))
                    last.then_inc(S["u_sb"], 1)
                if j in (4, 7):
                    t = j // 4 - (j == 4)
                    act.wait_ge(S["o_ps"], 4 if j == 4 else 8)
                    if t:
                        act.wait_ge(S["on_rdy"], t)
                    A(at("bv"), ps[:, 6 + t, :], ACT.Square).then_inc(S["o_sq"], 1)
            def modulation_copy(i):
                act.wait_ge(S["bc_ps"], i + 1)
                dst = (shB, gsB, gate2B)[i // 2]
                A(dst[:, 512 * (i % 2):512 * (i % 2) + 512], ps[:, i % 2, :], ACT.Copy).then_inc(S["bc_sb"], 1)

            for i in range(4):
                modulation_copy(i)
            for n, g in enumerate((at("uc", 2048, 1024), at("ur", 2048, 1024))):
                act.wait_ge(S["u_sb"], 16 + 2 * n)
                A(g, g, ACT.Sigmoid).then_inc(S["gat_rdy"], 1)
            def row_squares(t):
                act.wait_ge(S["x1_rdy"], 2 * t + 2)
                A(xn[:, t, :], x[:, t, :], ACT.Square, accum_out=ss[:, t:t + 1]).then_inc(S["x1_sq"], 1)

            def rows_over_norm(t):
                act.wait_ge(S["rs_rdy"], t + 1)
                A(xn[:, t, :], x[:, t, :], ACT.Copy, scale=rs[:, t:t + 1]).then_inc(S["xs_rdy"], 1)

            def part_copy(t):
                act.wait_ge(S["part_ps"], t + 1)
                A(part[:, t * P:(t + 1) * P], ps[:, 4, 0:P], ACT.Copy).then_inc(S["part_sb"], 1)

            row_squares(0)
            rows_over_norm(0)
            act.wait_ge(S["x1T_ps"], 2)
            A(hT[:, 0:4, P:2 * P], ps[:, 6, :].rearrange("p (k t) -> p k t", k=4), ACT.Copy).then_inc(S["x1T_act"], 1)
            part_copy(0)
            row_squares(1)
            part_copy(1)
            rows_over_norm(1)
            for i in (4, 5):
                modulation_copy(i)
            act.wait_ge(S["top_rdy"], 1)
            A(gexp, gexp, ACT.Exp).then_inc(S["top_exp"], 1)

            def sigmoid(i):
                act.wait_ge(S["g_rdy"], i + 1)
                A(s_sb, g_sb, ACT.Sigmoid, scale=1.702).then_inc(S["sig_rdy"], 1)

            def act_copy(i):
                act.wait_ge(S["tr_done"], i + 1)
                A(actT.rearrange("p j s -> p (j s)"), ps[:, 7, :], ACT.Copy).then_inc(S["actT_rdy"], 1)

            def y_copy(i, s):
                act.wait_ge(S["dn_used"], i * 4 + 4)
                for h in range(2):
                    last = A(y[64 * s:64 * s + 64, 512 * h:512 * (h + 1)], ps[64 * h:64 * h + 64, 6, :], ACT.Copy)
                last.then_inc(S["y_rdy"], 1)

            sigmoid(0)
            act_copy(0)
            sigmoid(1)
            act.wait_ge(S["gt_ps"], 1)
            A(GT[0:E, :], ps[0:E, 7, 0:256], ACT.Copy).then_inc(S["gt_sb"], 1)
            y_copy(0, 0)
            act_copy(1)
            act.wait_ge(S["tables"], 2)
            n_pairs = act.value_load(table_i[0:1, 48:49], min_val=E // 2, max_val=ITEMS // 2)
            with act.Fori(1, n_pairs) as p:
                sigmoid(p * 2)
                y_copy(p * 2 - 1, 1)
                act_copy(p * 2)
                sigmoid(p * 2 + 1)
                act.wait_ge(S["sc_done"], p)
                y_copy(p * 2, 0)
                act_copy(p * 2 + 1)
            y_copy(n_pairs * 2 - 1, 1)
            for t in range(TT):
                act.wait_ge(S["x2_rdy"], 2 * t + 2)
                A(fin[:, t, :], x[:, t, :], ACT.Square, accum_out=ss[:, t:t + 1]).then_inc(S["fin_sq"], 1)

        @block.vector
        def _(v):
            V = nc.vector
            step = Steps(v, S["dve_step"])

            def rstd(dst, src, n, done=None):
                w = dst.shape[1]
                m, t = nwt[:, 0:w], nwt[:, 4:4 + w]
                step(V.tensor_scalar(m, src, 1.0 / n, EPS, ALU.mult, ALU.add))
                step(V.tensor_scalar(dst.bitcast(I32), m.bitcast(I32), -0.5, float(0x5F3759DF), ALU.mult, ALU.add))
                for n in range(3):
                    step(V.scalar_tensor_tensor(t, dst, -0.5, dst, ALU.mult, ALU.mult))
                    step(V.tensor_tensor(t, t, m, ALU.mult))
                    last = V.scalar_tensor_tensor(dst, t, 1.5, dst, ALU.add, ALU.mult)
                    if n < 2 or done is None:
                        step(last)
                last.then_inc(done, 1) if done is not None else None

            v.wait_ge(S["prmT_ps"], 1)
            sig(v, V.tensor_copy(prmT, ps[:, 3, 0:128]), "prmT_sb", 1)

            def angle(n, src):
                step(V.tensor_scalar(ang[0:64, :], src, col(C_F + n - 1, 0, 64), col(C_F + 3, 0, 64), ALU.add, ALU.mult))
                magic = 1.5 * 2.0 ** 23
                step(V.tensor_scalar(turns[0:64, :], ang[0:64, :], 1.0 / TWO_PI, magic, ALU.mult, ALU.add))
                step(V.tensor_scalar(turns[0:64, :], turns[0:64, :], -magic, None, ALU.add))
                for part in (6.28125, 0.0019350051879882812, 3.019915981956753e-07):
                    step(V.scalar_tensor_tensor(ang[0:64, :], turns[0:64, :], -part, ang[0:64, :], ALU.mult, ALU.add))
                pi = 3.1415925
                V.tensor_scalar(ang[0:64, :], ang[0:64, :], pi, -pi, ALU.min, ALU.max).then_inc(S[f"ang_{n}"], 1)

            v.wait_ge(S["tab_in"], 16)
            step(V.tensor_copy(ef[:, 0:E], tab("item")[:, 0:E]))
            step(V.tensor_scalar(ohI[:, 0:E], ef[:, 0:E], lane, None, ALU.is_equal))
            v.wait_ge(S["f1_ps"], 1)
            angle(1, ps[0:64, 0, 0:256])
            v.wait_ge(S["sig_c"], 1)
            cb = at("on", 0, 8)
            step(V.tensor_tensor(cb, at("cs", 0, 8), prmT[:, C_C:C_C + 8], ALU.mult))
            sig(v, V.tensor_copy(cs, cb.unsqueeze(2).to_broadcast([P, KD, 32])), "silu_c", 1)
            v.wait_ge(S["hid_1"], 1)
            v.wait_ge(S["f2_ps"], 1)
            angle(2, ps[0:64, 1, 0:256])
            v.wait_ge(S["hid_2"], 1)
            v.wait_ge(S["f3_ps"], 1)
            angle(3, ps[0:64, 2, 0:256])
            v.wait_ge(S["lam_in"], 16)
            lam = at("lam").rearrange("p (a b d) -> p a b d", a=2, b=2)
            lprod = at("on", 8, 128).rearrange("p (a d) -> p a d", a=2)
            step(V.tensor_tensor(lprod, lam[:, :, 0, :], lam[:, :, 1, :], ALU.mult))
            sig(v, V.tensor_reduce(lam2, lprod, AX.X, ALU.add), "lam_a", 1)
            v.wait_ge(S["x_sq"], TT)
            rstd(rs, ss, D)
            step(V.tensor_scalar(xn[:, 0, :], x[:, 0, :], rs[:, 0:1], None, ALU.mult))
            V.tensor_scalar(xn[:, 1, :], x[:, 1, :], rs[:, 1:2], None, ALU.mult).then_inc(S["xn_rdy"], 1)
            v.wait_ge(S["f4_ps"], 4)
            v.wait_ge(S["decay_in"], 16)
            for t in range(TT):
                step(V.tensor_tensor(kminus[:, t, :], ps[:, 4 + t, :], decay[:, 0, t, :], ALU.mult))
                step(V.tensor_tensor(kback, ps[:, 6 + t, :], decay[:, 1, t, :], ALU.mult))
                step(V.tensor_tensor(kplus[:, t, :], kminus[:, t, :], kback, ALU.add))
                sig(v, V.tensor_tensor(kminus[:, t, :], kminus[:, t, :], kback, ALU.subtract), "filt_sb", t + 1)

            def ada_rows(g, b, gains):
                v.wait_ge(S["ada_used"], 4 * g + 4)
                v.wait_ge(*((S["gain_in"], 16 * 8) if g == 0 else (S["ada_in"], 16 * 8)))
                sig(v, V.tensor_tensor(adr[g], ps[:, b, :], adr[g], ALU.add), f"ada{g}_sb", 1)
                if gains is not None:
                    r = slice(gains, gains + 64)
                    v.wait_ge(S["gain_in"], 16 * 8)
                    sig(v, V.scalar_tensor_tensor(adr[g][r, :], adr[g][r, :], 1.0, gain[r, :], ALU.add, ALU.mult),
                        f"ada{g}_sb", 2)

            def ada_columns(g, b):
                v.wait_ge(S[f"mc{g}_ps"], 1)
                src = ps[:, b, :].rearrange("p (j q r) -> p q j r", j=4, q=4)[:, :, :, 0]
                sig(v, V.tensor_copy(modc[:, g, :, :], src), f"mc{g}_sb", 1)

            def modulated(shift, scale):
                for k in range(KD):
                    last = V.tensor_scalar(hT[:, k, :], ps[:, k // 2, (k % 2) * 256:(k % 2) * 256 + 256],
                                           scale(k), shift(k), ALU.mult, ALU.add)
                return last

            ada_rows(0, 3, 64)
            ada_columns(0, 5)
            v.wait_ge(S["xT_ps"], 1)
            mc = lambda g, i: modc[:, g, i // 4, i % 4:i % 4 + 1]
            modulated(lambda k: mc(0, k), lambda k: mc(0, 8 + k)).then_inc(S["h1_sb"], 1)
            v.wait_ge(S["kA_sb"], 1)
            v.wait_ge(S["kN_ps"], 1)
            step(V.tensor_copy(kN[0:1, :], ps[0:1, 4, :]))
            v.wait_ge(S["kB_ps"], 1)
            step(V.tensor_copy(kB[:, 0, :], ps[:, 5, :]))
            step(V.memset(kB[0:1, 0, :], 0.0))
            v.wait_ge(S["kB_ps"], 2)
            sig(v, V.tensor_copy(kB[:, 1, :], ps[:, 6, :]), "kf_done", 1)
            for i in range(12):
                v.wait_ge(S["u_sb"], i // 2 + 1)
                wcol = lambda j: col(C_W + 12 * j + i)
                step(V.tensor_scalar(ucv[:, i, :], uraw[:, i, 1:257], wcol(1), col(C_CB + i), ALU.mult, ALU.add))
                step(V.scalar_tensor_tensor(ucv[:, i, :], uraw[:, i, 0:256], wcol(0), ucv[:, i, :], ALU.mult, ALU.add))
                step(V.scalar_tensor_tensor(ucv[:, i, :], uraw[:, i, 2:258], wcol(2), ucv[:, i, :], ALU.mult, ALU.add))
            sig(v, V.tensor_tensor(vT, vT, x1T, ALU.mult), "vT_rdy", 1)
            ada_rows(1, 6, None)
            v.wait_ge(S["bv_in"], 16)
            for t in range(TT):
                v.wait_ge(S["u_ps"], 11 + t)
                V.tensor_tensor(ve[:, t, :], ps[:, (10 + t) % 3, :], at("bv"), ALU.add).then_inc(S["v_sb"], 1)
            ada_rows(2, 7, 0)
            v.wait_ge(S["V_ps"], 4)
            t0, t1 = flat
            for f in range(2):
                vr, vs = ps[:, 4 + f, :], ps[:, 6 + f, :]
                a2 = kN if f == 0 else kA[:, 1, :]
                step(V.tensor_tensor(t0, vr, kA[:, f, :], ALU.mult))
                step(V.tensor_tensor(t1, vs, kB[:, f, :], ALU.mult))
                step(V.tensor_tensor(Y[:, f, :], t0, t1, ALU.subtract))
                step(V.tensor_tensor(t0, vr, kB[:, f, :], ALU.mult))
                step(V.tensor_tensor(t1, vs, a2, ALU.mult))
                sig(v, V.tensor_tensor(Y[:, 2 + f, :], t0, t1, ALU.add), "Y_rdy", f + 1)
            v.wait_ge(S["yT_ps"], 1)
            for c in range(CT):
                step(V.scalar_tensor_tensor(vT[:, c, :], vT[:, c, :], col(C_DS + c),
                                            ps[:, 6 + c // 2, (c % 2) * 256:(c % 2) * 256 + 256], ALU.mult, ALU.add))
            sig(v, V.tensor_tensor(y_hyT, x0T, vT, ALU.mult), "yhy_rdy", 1)
            ada_columns(1, 0)
            ada_columns(2, 1)
            gs_cols = at("modc", 32, KD).unsqueeze(2).to_broadcast([P, KD, E])
            v.wait_ge(S["rb_ps"], 1)
            v.wait_ge(S["br_in"], 16)
            sig(v, V.tensor_tensor(at("br"), at("br"), ps[:, 1, 0:E], ALU.add), "rb_sb", 1)
            sig(v, V.tensor_tensor(wr_scaled, wr, gs_cols, ALU.mult), "rb_sb", 2)

            v.wait_ge(S["lam_e"], 1)
            step(V.tensor_tensor(lamcol, lam2[:, 1:2], lam2[:, 0:1], ALU.subtract))
            step(V.tensor_scalar(lamcol, lamcol, -LAM_INIT, None, ALU.add))

            def logits(j):
                t, h = j // HEADS, j % HEADS
                s = sc[j % 2]
                v.wait_ge(S["s_ps"], j + 1)
                d = dist[:, t, :].unsqueeze(1).to_broadcast([P, 2, L])
                sig(v, V.scalar_tensor_tensor(s, d, -8.0 * SLOPES[h], ps[:, 4 + j % 2, :].rearrange("p (c k) -> p c k", c=2),
                                              ALU.mult, ALU.add), "s_sb", j + 1)
                m = negm[:, 2 * (j % 2):2 * (j % 2) + 2]
                step(V.tensor_reduce(m, s, AX.X, ALU.max))
                V.tensor_scalar(m, m, -0.125, None, ALU.mult).then_inc(S["negm_rdy"], 1)

            def difference(j):
                s, o = sc[j % 2], 2 * (j % 2)
                v.wait_ge(S["exp_done"], j + 1)
                step(V.reciprocal(rinv[:, o:o + 2], sums[:, o:o + 2]))
                step(V.tensor_tensor(rlam[:, j % 2:j % 2 + 1], rinv[:, o + 1:o + 2], lamcol, ALU.mult))
                step(V.tensor_scalar(s[:, 1, :], s[:, 1, :], rlam[:, j % 2:j % 2 + 1], None, ALU.mult))
                if j >= 2:
                    v.wait_ge(S["aT_ps"], j - 1)
                sig(v, V.scalar_tensor_tensor(ab[j % 2], s[:, 0, :], rinv[:, o:o + 1], s[:, 1, :], ALU.mult, ALU.add),
                    "a_rdy", j + 1)

            def turned(j):
                v.wait_ge(S["aT_ps"], j + 1)
                if j >= 2:
                    v.wait_ge(S["o_ps"], j - 1)
                V.tensor_copy(aT[j % 2].rearrange("p k q -> p (k q)"), ps[:, 3, (j % 2) * 256:(j % 2) * 256 + 256])\
                    .then_inc(S["aT_sb"], 1)

            def head_norm(t):
                v.wait_ge(S["o_sq"], t + 1)
                step(V.tensor_reduce(oss, at("bv").rearrange("p (h e) -> p h e", h=HEADS), AX.X, ALU.add))
                rstd(ors, oss, P)
                if t:
                    v.wait_ge(S["oT_ps"], t)
                V.tensor_tensor(on.rearrange("p (h e) -> p h e", h=HEADS),
                                ps[:, 6 + t, :].rearrange("p (h e) -> p h e", h=HEADS),
                                ors.unsqueeze(2).to_broadcast([P, HEADS, P]), ALU.mult).then_inc(S["on_rdy"], 1)

            def head_turned(t):
                v.wait_ge(S["oT_ps"], t + 1)
                V.tensor_scalar(y_atT[:, :, t * P:(t + 1) * P], ps[:, 3, :].rearrange("p (h q) -> p h q", h=HEADS),
                                col(C_SG), 1.0 - LAM_INIT, ALU.mult, ALU.mult).then_inc(S["oT_sb"], 1)

            logits(0)
            for j in range(2 * HEADS):
                if j + 1 < 2 * HEADS:
                    logits(j + 1)
                difference(j)
                turned(j)
                if j == 5:
                    head_norm(0)
            head_turned(0)
            head_norm(1)
            head_turned(1)
            mt = at("ab")
            for i in range(KD):
                v.wait_ge(S["pj_ps"], i + 1)
                v.wait_ge(S["gat_rdy"], i // 4 + 1)
                b = ps[:, 4 + i % 2, :]
                step(V.tensor_tensor(mt[:, 0:256], b[:, 0:256], gate_hy[:, i, :], ALU.mult))
                step(V.tensor_tensor(mt[:, 256:512], b[:, 256:512], gate_at[i], ALU.mult))
                sig(v, V.tensor_tensor(merged[:, i, :], mt[:, 0:256], mt[:, 256:512], ALU.add), "pj_sb", i + 1)
            v.wait_ge(S["g1_sb"], 2)
            for t in range(TT):
                for h in range(2):
                    v.wait_ge(S["mix_ps"], 1 if t == 0 else 2 + 2 * h)
                    step(V.tensor_tensor(flat[0], ps[:, 2 * t + h, :], gate1B[:, 512 * h:512 * (h + 1)], ALU.mult))
                    xs = x[:, t, 512 * h:512 * (h + 1)]
                    sig(v, V.tensor_tensor(xs, xs, flat[0], ALU.add), "x1_rdy", 2 * t + h + 1)
                v.wait_ge(S["x1T_ps"], 2 * t + 1)
                if t == 0:
                    step(V.tensor_copy(hT[:, 0:4, 0:P], ps[:, 4, :].rearrange("p (k t) -> p k t", k=4)))
                V.tensor_copy(hT[:, 4:8, t * P:(t + 1) * P], ps[:, 5 + 2 * t, :].rearrange("p (k t) -> p k t", k=4))\
                    .then_inc(S["x1T_dve"], 1)
                v.wait_ge(S["x1_sq"], t + 1)
                rstd(rs[:, t:t + 1], ss[:, t:t + 1], D, S["rs_rdy"])
            v.wait_ge(S["log_ps"], 1)
            v.wait_ge(S["rs_rdy"], TT)
            for t in range(TT):
                step(V.scalar_tensor_tensor(log[:, t, :], ps[:, 5, E * t:E * t + E], rs[:, t:t + 1], at("br"),
                                            ALU.mult, ALU.add))
            for k in range(TOPK):
                step(V.tensor_reduce(topv[:, k, :], log, AX.X, ALU.max))
                for t in range(TT):
                    ins = V.scalar_tensor_tensor(wrk[:, t, :], log[:, t, :], topv[:, k, t:t + 1], tab("erev"),
                                                 ALU.is_ge, ALU.mult)
                    step.start(ins) if t == 0 else step(ins)
                step(V.tensor_reduce(km, wrk, AX.X, ALU.max))
                step(V.tensor_tensor(oh[:, k, :, :], wrk, km.unsqueeze(2).to_broadcast([P, TT, E]), ALU.is_equal))
                if k < TOPK - 1:
                    step(V.scalar_tensor_tensor(log, oh[:, k, :, :], -3.0e38, log, ALU.mult, ALU.add))
            sig(v, V.tensor_reduce(M, oh.rearrange("p k t e -> p t e k"), AX.X, ALU.add), "m_rdy", 1)
            sig(v, V.tensor_tensor(gexp, topv, topv[:, 0, :].unsqueeze(1).to_broadcast([P, TOPK, TT]), ALU.subtract),
                "top_rdy", 1)
            v.wait_ge(S["rank_ps"], 1)
            step(V.tensor_copy(rank, ps[:, 5, 128:192].rearrange("p (t e) -> p t e", t=TT)))
            for t in range(TT):
                for e in range(2):
                    last = V.tensor_scalar(Sel[:, t, e * SLOTS:(e + 1) * SLOTS], iota[:, 0:SLOTS],
                                           rank[:, t, e:e + 1], M[:, t, e:e + 1], ALU.is_equal, ALU.mult)
                    if (t, e) == (TT - 1, 1):
                        v.wait_ge(S["dve_step"], step.n)
                        last.then_inc(S["sel_rdy"], 1)
                    else:
                        step.start(last)

            def rows_of(p):
                src = ohI[:, bass.ds(p * 2, 2)] if not isinstance(p, int) else ohI[:, 2 * p:2 * p + 2]
                V.tensor_copy(mask, src.unsqueeze(2).to_broadcast([P, 2, SLOTS])).then_inc(S["mask_rdy"], 1)

            rows_of(0)

            def blocks_beyond(dst, cnt, tmp, signal=None):
                step(V.tensor_scalar(dst, cnt, 64.0, None, ALU.is_gt))
                for n, edge in enumerate((128.0, 192.0)):
                    step(V.tensor_scalar(tmp, cnt, edge, None, ALU.is_gt))
                    ins = V.tensor_tensor(dst, dst, tmp, ALU.add)
                    sig(v, ins, signal, n + 1) if signal else step(ins)

            v.wait_ge(S["cnt_ps"], 1)
            blocks_beyond(cntT2[0:E, :], ps[0:E, 2, 128:256], cntT[0:E, :], "cnt_sb")
            blocks_beyond(nov, ps[:, 2, 0:32], tmpe)

            def positions():
                v.wait_ge(S["ex_ps"], 1)
                step(V.tensor_copy(exc, ps[:, 3, 0:48]))
                step(V.tensor_tensor(inc, exc[:, 0:E], nov, ALU.add))
                step(V.tensor_tensor(tmpe, exc[:, 0:E], tab("item")[:, 0:E], ALU.subtract))
                step(V.tensor_scalar(tmpe, tmpe, 31.0, None, ALU.add))
                wide = lambda c: c.unsqueeze(1).to_broadcast([P, TT, E])
                step(V.tensor_scalar(wrk, rank, 64.0, None, ALU.is_ge))
                step(V.tensor_tensor(wrk, wrk, wide(tmpe), ALU.mult))
                step(V.tensor_tensor(wrk, wrk, wide(tab("item")[:, 0:E]), ALU.add))
                step(V.scalar_tensor_tensor(wrk2, wrk, 64.0, rank, ALU.mult, ALU.add))
                for k in range(TOPK):
                    step(V.tensor_tensor(pos_k[:, k, :, :], oh[:, k, :, :], wrk2, ALU.mult))
                step(V.tensor_reduce(pk, pos_k, AX.X, ALU.add))

            def activate(i, st):
                v.wait_ge(S["gu_used"], i * 8 + 8)
                sig(v, V.tensor_scalar(g_sb, ps[:, 4, :], 7.0, None, ALU.min), "g_rdy", i + 1)
                st(V.tensor_scalar(u_sb, ps[:, 5, :], 7.0, -7.0, ALU.min, ALU.max))
                st(V.scalar_tensor_tensor(t_sb, u_sb, 1.0, g_sb, ALU.add, ALU.mult))
                v.wait_ge(S["sig_rdy"], i + 1)
                V.tensor_tensor(act_o, t_sb, s_sb, ALU.mult).then_inc(S["act_rdy"], 1)

            def select(st):
                for k in range(TOPK):
                    for t in range(TT):
                        s = pk[:, k, t:t + 1]
                        if k == 0:
                            ins = V.tensor_scalar(Sel[:, t, :], iota, s, None, ALU.is_equal)
                        else:
                            ins = V.scalar_tensor_tensor(Sel[:, t, :], iota, s, Sel[:, t, :], ALU.is_equal, ALU.add)
                        if k == TOPK - 1 and t == TT - 1:
                            ins.then_inc(S["sel_rdy"], 1)
                        else:
                            st(ins)

            def weigh(st):
                for k in range(TOPK):
                    for t in range(TT):
                        dst = Wt if k == 0 else Wtmp
                        st(V.tensor_scalar(dst[:, t, :], iota, pk[:, k, t:t + 1], gk[:, k, t:t + 1],
                                           ALU.is_equal, ALU.mult))
                    if k == TOPK - 1:
                        V.tensor_tensor(Wt, Wt, Wtmp, ALU.add).then_inc(S["wt_rdy"], 1)
                    elif k:
                        st(V.tensor_tensor(Wt, Wt, Wtmp, ALU.add))

            def advance(st):
                st(V.tensor_scalar(pk, pk, -128.0, None, ALU.add))

            def gathered(p):
                for half in range(2):
                    v.wait_ge(S["ga_done"], p * 2 + (half + 1))
                    V.tensor_copy(hTp[:, 4 * half:4 * half + 4, :].rearrange("p k s -> p (k s)"), ps[:, 7 - half, :])\
                        .then_inc(S["ga_sb"], 1)

            def placed(p):
                v.wait_ge(S["pt_done"], p + 1)
                V.tensor_copy(Pw.rearrange("p t q -> p (t q)"), ps[:, 7, 0:256]).then_inc(S["pt_sb"], 1)

            gathered(0)
            positions()
            v.wait_ge(S["top_exp"], 1)
            step(V.tensor_tensor(gsum, gexp[:, 0, :], gexp[:, 1, :], ALU.add))
            step(V.tensor_tensor(gsum, gsum, gexp[:, 2, :], ALU.add))
            step(V.tensor_tensor(gsum, gsum, gexp[:, 3, :], ALU.add))
            step(V.reciprocal(gden, gsum))
            step(V.tensor_tensor(gk, gexp, gden.unsqueeze(1).to_broadcast([P, TOPK, TT]), ALU.mult))
            for k in range(TOPK):
                g2 = gk[:, k, :].unsqueeze(2).to_broadcast([P, TT, E])
                if k == 0:
                    sig(v, V.tensor_tensor(G, oh[:, 0, :, :], g2, ALU.mult), "g_all", 1)
                else:
                    step(V.tensor_tensor(wrk, oh[:, k, :, :], g2, ALU.mult))
                    sig(v, V.tensor_tensor(G, G, wrk, ALU.add), "g_all", k + 1)
            step(V.tensor_tensor(cmpI, inc.unsqueeze(1).to_broadcast([P, EXTRA, E]),
                                 tab("item")[:, 0:EXTRA].unsqueeze(2).to_broadcast([P, EXTRA, E]), ALU.is_le))
            step(V.tensor_reduce(ef[:, E:ITEMS], cmpI, AX.X, ALU.add))
            step(V.tensor_scalar(ef[:, E:ITEMS], ef[:, E:ITEMS], float(E - 1), None, ALU.min))
            step(V.memset(ohI[:, ITEMS:ITEMS + 2], 0.0))
            step(V.tensor_scalar(ohI[:, E:ITEMS], ef[:, E:ITEMS], lane, None, ALU.is_equal))
            step(V.tensor_scalar(tmpe[:, 0:8], tab("odd"), exc[:, 40:41], None, ALU.is_le))
            step(V.tensor_reduce(pairs_f[:, 0:1], tmpe[:, 0:8], AX.X, ALU.add))
            step(V.tensor_scalar(pairs_f[:, 0:1], pairs_f[:, 0:1], float(E // 2), None, ALU.add))
            sig(v, V.tensor_copy(table_i[0:1, 0:ITEMS], ef[0:1, :]), "tables", 1)
            step(V.tensor_scalar(pairs_f[:, 1:2], pairs_f[:, 0:1], -1.0, None, ALU.add))
            sig(v, V.tensor_copy(table_i[0:1, 48:50], pairs_f[0:1, 0:2]), "tables", 2)
            activate(0, step)
            weigh(step)
            advance(step)
            v.wait_ge(S["sel_rdy"], 1)
            select(step)
            activate(1, step)
            v.wait_ge(S["gu_used"], 16)
            rows_of(1)
            gathered(1)
            placed(0)
            v.wait_ge(S["tables"], 2)
            n_pairs = v.value_load(table_i[0:1, 48:49], min_val=E // 2, max_val=ITEMS // 2)
            PER = 2 * 2 + (TOPK * TT + TOPK - 2) + 1 + (TOPK * TT - 1)
            with v.Fori(1, n_pairs) as p:
                st = Steps(v, S["dve_loop"], p * PER - PER)
                activate(p * 2, st)
                v.wait_ge(S["pt_done"], p)
                weigh(st)
                v.wait_ge(S["wt_rdy"], p + 1)
                advance(st)
                v.wait_ge(S["ga_done"], p * 2 + 2)
                select(st)
                activate(p * 2 + 1, st)
                rows_of(p + 1)
                gathered(p + 1)
                placed(p)
                assert st.n == PER, (st.n, PER)
            v.wait_ge(S["fg_in"], 16)
            for t in range(TT):
                if t < TT - 1:
                    v.wait_ge(S["sc_tile"], t + 1)
                else:
                    v.wait_ge(S["sc_done"], n_pairs)
                for h in range(2):
                    step(V.tensor_tensor(u_sb, ps[:, 2 * t + h, :], gate2B[:, 512 * h:512 * (h + 1)], ALU.mult))
                    xs = x[:, t, 512 * h:512 * (h + 1)]
                    sig(v, V.tensor_tensor(xs, xs, u_sb, ALU.add), "x2_rdy", 2 * t + h + 1)
            v.wait_ge(S["fin_sq"], TT)
            rstd(rs, ss, D)
            for t in range(TT):
                V.scalar_tensor_tensor(fin[:, t, :], x[:, t, :], rs[:, t:t + 1], fgB, ALU.mult, ALU.mult)\
                    .then_inc(S["fin_rdy"], 1)


def kernel(**inputs):
    import numpy as np
    import concourse.bacc as bacc
    from concourse.bass_utils import run_bass_kernel_spmd

    nc = bacc.Bacc("TRN2", target_bir_lowering=False, num_devices=1)
    arrays, aps = {}, {}
    for name, value in list(inputs.items()) + list(host_tables().items()):
        v = np.ascontiguousarray(value)
        arrays["in_" + name] = v
        aps[name] = nc.dram_tensor("in_" + name, v.shape, mybir.dt.from_np(v.dtype), kind="ExternalInput").ap()
    out = nc.dram_tensor("out_0", (1, L, D), F32, kind="ExternalOutput").ap()
    build(nc, aps, out)
    r = run_bass_kernel_spmd(nc, [arrays], core_ids=[0])
    return r.results[0]["out_0"]
```

```python
import math
from contextlib import ExitStack

import concourse.bass as bass
from concourse import mybir

F32 = mybir.dt.float32
I32 = mybir.dt.int32
ALU = mybir.AluOpType
ACT = mybir.ActivationFunctionType
AX = mybir.AxisListType

P = 128
D = 1024
L = 256
TT = L // P
KD = D // P
HW = 512
CT = HW // P
HEADS = 4
E = 32
TOPK = 4
FE = 1024
SLOTS = 64
ITEMS = 48
EXTRA = ITEMS - E
EPS = 1e-5
LAM_INIT = 0.2
SLOPES = [2.0 ** (-8.0 * (h + 1) / HEADS) for h in range(HEADS)]
TWO_PI = 2.0 * math.pi

TAB = {}
_at = 0
for _name, _w in (("ident", P), ("tri", P), ("iota", P), ("ones", P), ("lane", 1), ("erev", E), ("odd", 8), ("quad", E),
                  ("item", ITEMS), ("dist", TT * L)):
    TAB[_name] = (_at, _w)
    _at += _w
TABW = _at


def host_tables():
    import numpy as np
    t = np.arange(L)
    f = np.arange(L)
    ang = 2.0 * np.pi * np.outer(t, f) / (2 * L)
    dft = np.concatenate([np.cos(ang), np.sin(ang)], axis=1)
    dft[:, L] = np.cos(np.pi * t)
    wt = np.full(2 * L, 2.0)
    wt[0] = wt[L] = 1.0
    inv = (dft * wt[None, :] / (2 * L)).T
    tl = np.linspace(0.0, 1.0, L, dtype=np.float32)[:, None]
    w = (np.float32(2.0 * math.pi) * np.arange(L, dtype=np.float32)[:, None] / np.float32(L)).astype(np.float32)
    fr = np.linspace(1e-4, 7, 8, dtype=np.float32)[None, :]
    z = np.concatenate([tl, np.cos(fr * w), -np.sin(fr * w)], axis=1)
    deltas = np.linspace(math.log(1e-2) / 1.5, math.log(1e-2) / 0.3, HW, dtype=np.float32)
    decay = np.exp(-tl * np.abs(deltas))
    back = decay.copy()
    back[0] = 0.0
    tab = np.zeros((P, TABW), np.float32)
    put = lambda n, v: tab.__setitem__((slice(None), slice(TAB[n][0], TAB[n][0] + TAB[n][1])), v)
    r = np.arange(P)
    put("ident", np.eye(P))
    put("tri", (r[:, None] < r[None, :]).astype(np.float32))
    put("iota", r[None, :])
    put("ones", 1.0)
    put("lane", r[:, None])
    put("erev", E - np.arange(E)[None, :])
    put("odd", 1 + 2 * np.arange(8)[None, :])
    put("quad", (r[:, None] % E == np.arange(E)[None, :]).astype(np.float32))
    put("item", np.arange(ITEMS)[None, :])
    dist = np.abs(np.arange(L)[:, None] - np.arange(L)[None, :]).reshape(TT, P, L)
    put("dist", dist.transpose(1, 0, 2).reshape(P, TT * L))
    c = lambda a: np.ascontiguousarray(a, np.float32)
    return {"t_small": tab, "t_dft": c(dft), "t_inv": c(inv), "t_z": c(z.T),
            "t_decay": c(np.stack([decay, back]))}


def build(nc, a, out):
    with ExitStack() as ctx:
        regions = {}
        top = [0]

        def region(name, words):
            regions[name] = (top[0], words)
            top[0] += words

        for name, words in (
                ("ring", 24576), ("x", 2048), ("xn", 2048), ("ht", 2048), ("ur", 12 * 258), ("uc", 3072),
                ("kf", 2560), ("dft", 1024), ("inv", 1024), ("qm", 2048), ("kt", 1024), ("ve", 1024),
                ("sc", 1024), ("at", 512), ("ab", 512), ("on", 512), ("adr", 1536),
                ("tab", TABW), ("prm", 128), ("prmT", 128), ("lam", 256), ("bv", 512), ("br", 32),
                ("cs", 256), ("modc", 48), ("tiny", 886)):
            region(name, words)
        arena = ctx.enter_context(nc.sbuf_tensor("arena", [P, top[0]], F32))
        table_i = ctx.enter_context(nc.sbuf_tensor("table_i", [1, 64], I32))
        ps = ctx.enter_context(nc.psum_tensor("ps", [P, 8, 512], F32))

        def at(name, off=0, words=None):
            o, w = regions[name]
            words = w - off if words is None else words
            assert off + words <= w, name
            return arena[:, o + off:o + off + words]

        def tab(name):
            o, w = TAB[name]
            return at("tab", o, w)

        def span(name, off, words):
            o = regions[name][0] + off
            return arena[:, o:o + words]

        ident, tri, iota, ones, lane = tab("ident"), tab("tri"), tab("iota"), tab("ones"), tab("lane")
        dist = tab("dist").rearrange("p (q k) -> p q k", q=TT)

        ring = [at("ring", 4096 * s, 4096) for s in range(6)]
        gu_slot = [at("ring", 2048 * k, 2048) for k in range(KD)]
        odd_slot = [span("ur", 2048, 2048), span("ur", 4096, 2048), span("ab", 0, 2048), span("dft", 0, 2048),
                    span("qm", 0, 2048), span("ur", 0, 2048)]
        OWN = len(odd_slot)
        y = b_down = span("prm", 0, D)
        dn_slot = [at("ring", 2048 * (KD + c), 2048).rearrange("p (q n) -> p q n", q=2) for c in range(4)]
        last_down = [g.rearrange("p (q n) -> p q n", q=2) for g in gu_slot[:4]]

        x = at("x").rearrange("p (t d) -> p t d", t=TT)
        xn = at("xn").rearrange("p (t d) -> p t d", t=TT)
        gate_hy = at("xn").rearrange("p (c t) -> p c t", c=KD)
        hT = at("ht").rearrange("p (k t) -> p k t", k=KD)
        uraw = at("ur").rearrange("p (c t) -> p c t", c=12)
        Y = at("ur", 0, 2048).rearrange("p (f c) -> p f c", f=4)
        vtc = at("ur", 2048, 1024).rearrange("p (t c) -> p t c", t=TT)
        merged = at("ur", 0, 2048).rearrange("p (c t) -> p c t", c=KD)
        ucv = at("uc").rearrange("p (c t) -> p c t", c=12)
        x0T, x1T, vT = ucv[:, 0:4], ucv[:, 4:8], ucv[:, 8:12]
        y_hyT, y_atT = x0T, x1T
        gate_at = [ucv[:, 8 + i, :] if i < 4 else at("ur", 2048 + 256 * (i - 4), 256) for i in range(KD)]
        w4 = at("ur", 0, 1024)
        kplus = at("ur", 1024, 1024).rearrange("p (t c) -> p t c", t=TT)
        kback = at("on")
        kminus = at("uc", 2048, 1024).rearrange("p (t c) -> p t c", t=TT)
        decay = at("uc", 0, 2048).rearrange("p (s t c) -> p s t c", s=2, t=TT)
        kA = at("kf", 0, 1024).rearrange("p (f c) -> p f c", f=2)
        kN = at("kf", 1024, 512)
        kB = at("kf", 1536, 1024).rearrange("p (f c) -> p f c", f=2)
        dft = at("dft").rearrange("p (t f) -> p t f", t=TT)
        inv = at("inv").rearrange("p (f t) -> p f t", f=4)
        qm = at("qm").rearrange("p (h c t) -> p h c t", h=HEADS, c=2)
        kT = at("kt").rearrange("p (h t) -> p h t", h=HEADS)
        ve = at("ve").rearrange("p (t e) -> p t e", t=TT)
        sc = [at("sc", 512 * j, 512).rearrange("p (c k) -> p c k", c=2) for j in range(2)]
        flat = [at("sc", 512 * j, 512) for j in range(2)]
        ab = [at("ab", 256 * j, 256) for j in range(2)]
        aT = [at("at", 256 * j, 256).rearrange("p (k q) -> p k q", k=TT) for j in range(2)]
        on = at("on")
        adr = [at("adr", 512 * g, 512) for g in range(3)]
        gain = at("at")
        prm, prmT = at("prm"), at("prmT")
        cs = at("cs").rearrange("p (k r) -> p k r", k=KD)
        wr = at("lam").rearrange("p (k e) -> p k e", k=KD)
        wr_scaled = at("cs").rearrange("p (k e) -> p k e", k=KD)
        modc = at("modc").rearrange("p (g q j) -> p g q j", g=3, q=4)
        gate1B = at("dft")
        gate2B, fgB = at("dft"), at("inv")
        shB, gsB = at("kt"), at("ve")
        sel_bias = at("kf", 0, 2048)

        tiny_at = [0]

        def tiny(words):
            o = tiny_at[0]
            tiny_at[0] += words
            return at("tiny", o, words)

        ss, rs = tiny(2), tiny(2)
        lamcol, lam2, negm, sums, rinv, rlam = tiny(1), tiny(2), tiny(4), tiny(4), tiny(4), tiny(2)
        oss, ors, nwt = tiny(4), tiny(4), tiny(8)
        log = tiny(64).rearrange("p (t e) -> p t e", t=TT)
        oh = tiny(256).rearrange("p (k t e) -> p k t e", k=TOPK, t=TT)
        wrk = tiny(64).rearrange("p (t e) -> p t e", t=TT)
        topv = tiny(8).rearrange("p (k t) -> p k t", k=TOPK)
        km = tiny(2)
        gexp = tiny(8).rearrange("p (k t) -> p k t", k=TOPK)
        gsum, gden = tiny(2), tiny(2)
        gk = tiny(8).rearrange("p (k t) -> p k t", k=TOPK)
        pk = tiny(8).rearrange("p (k t) -> p k t", k=TOPK)
        M = tiny(64).rearrange("p (t e) -> p t e", t=TT)
        G = tiny(64).rearrange("p (t e) -> p t e", t=TT)
        nov, exc, inc, tmpe = tiny(32), tiny(48), tiny(32), tiny(32)
        cntT = at("sc", 384, 128)
        ef = tiny(ITEMS)
        ohI = tiny(ITEMS + 2)
        pairs_f = tiny(3)

        cmpI = at("kt", 0, 512).rearrange("p (i e) -> p i e", i=EXTRA)
        pos_k = at("sc", 0, 256).rearrange("p (k t e) -> p k t e", k=TOPK, t=TT)
        part = at("sc", 512, 256)
        wrk2 = at("sc", 768, 64).rearrange("p (t e) -> p t e", t=TT)
        rank = at("sc", 832, 64).rearrange("p (t e) -> p t e", t=TT)
        cntT2 = at("sc", 256, 128)
        GT = at("at", 0, 256)
        hTp = at("ht", 0, 1024).rearrange("p (k s) -> p k s", k=KD)
        Sel = at("ht", 1024, 256).rearrange("p (t s) -> p t s", t=TT)
        Wt = at("ht", 1280, 256).rearrange("p (t s) -> p t s", t=TT)
        Wtmp = at("ht", 1536, 256).rearrange("p (t s) -> p t s", t=TT)
        Pw = at("ht", 1792, 256).rearrange("p (t q) -> p t q", t=TT)
        actT = at("sc", 512, 512).rearrange("p (j s) -> p j s", j=4)
        act_o = at("sc", 0, 512)
        u_sb, s_sb, t_sb, g_sb = at("kt", 0, 512), at("kt", 512, 512), at("ve", 0, 512), at("ve", 512, 512)
        mask = at("cs", 0, 128).rearrange("p (i s) -> p i s", i=2)
        fin = at("xn").rearrange("p (t d) -> p t d", t=TT)

        zT = at("sc", 0, 256)
        w1, w2, w3 = at("sc", 256, 64), at("sc", 320, 64), at("sc", 384, 64)
        hid = at("qm", 0, 256)
        ang, turns = at("kt", 0, 256), at("kt", 256, 256)

        C_C, C_BHY, C_BQ, C_BK, C_BG, C_W, C_CB, C_DS, C_SG, C_F = 0, 8, 20, 24, 28, 44, 80, 92, 96, 97

        def col(c, p0=0, p1=P):
            return prmT[p0:p1, c:c + 1]

        def sem(name):
            return ctx.enter_context(nc.semaphore(name))

        names = """tab_in x_in prm_in filt_in decay_in dft_in inv_in ada_in lam_in bv_in br_in wr_in gain_in
            gub_in bd_in fg_in gub_zero out_done
            prm_zero qm_zero pad_zero prmT_ps prmT_sb sig_c silu_c
            f1_ps f2_ps f3_ps f4_ps ang_1 ang_2 ang_3 hid_1 hid_2 hid_3 filt_sb
            weighted x_sq xn_rdy xT_ps ada_used ada0_sb ada1_sb ada2_sb mc_ps
            mc_sb h1_sb h1_act kA_ps kN_ps kB_ps kA_sb kf_done
            u_ps u_sb v_sb vT_rdy vt_ps vt_sb V_ps Y_rdy yT_ps yhy_rdy lam_a lam_e
            s_ps s_sb negm_rdy exp_done a_rdy aT_ps aT_sb o_ps o_sq on_rdy oT_ps oT_sb
            rb_ps rb_sb pj_ps pj_sb gat_rdy mix_ps x1_rdy x2_rdy x1_sq rs_rdy xs_rdy x1T_ps bc_sb
            x1T_dve x1T_act part_ps part_sb log_ps top_rdy top_exp m_rdy rank_ps cnt_ps cnt_sb ex_ps g_all gt_ps gt_sb tables h2_rdy
            gu_used dn_used tr_done sc_done ga_done pt_done
            g_rdy sig_rdy act_rdy actT_rdy y_rdy ga_sb pt_sb sel_rdy wt_rdy mask_rdy
            sc_tile fin_sq fin_rdy dve_step act_step dve_loop pool_step""".split()
        S = {n: sem(n) for n in names}
        s_front = [sem(f"front_in{j}") for j in range(6)]
        s_gu = [sem(f"gate_up_in{k}") for k in range(KD)]
        s_odd = [sem(f"odd_gate_up_in{k}") for k in range(OWN)]
        s_dn = [sem(f"down_in{c}") for c in range(4)]

        pj_bank = (0, 1, 4, 5)

        class Steps:

            def __init__(self, eng, s, base=0):
                self.eng, self.s, self.base, self.n = eng, s, base, 0

            def __call__(self, ins):
                ins.then_inc(self.s, 1)
                self.n += 1
                self.eng.wait_ge(self.s, self.base + self.n)

            def start(self, ins):
                ins.then_inc(self.s, 1)
                self.n += 1

        def sig(eng, ins, name, value):
            ins.then_inc(S[name], 1)
            eng.wait_ge(S[name], value)

        w_ada, w_in = a["w_ada"], a["w_in"]
        ada_after = {1: (1, 0), 3: (1, 1), 4: (2, 0), 5: (2, 1)}
        blocks = [("ada", 0, j) for j in range(4)]
        for j in range(6):
            blocks.append(("in", j, 0))
            if j in ada_after:
                g, pair = ada_after[j]
                blocks += [("ada", g, 2 * pair), ("ada", g, 2 * pair + 1)]
        blocks += [("in", j, 0) for j in range(6, 10)] + [("hy", 0, 0), ("att", 0, 0), ("mix", 0, 0), ("mix", 1, 0)]
        where = {b: n for n, b in enumerate(blocks)}

        def block_source(b):
            kind, i, j = b
            if kind == "ada":
                return w_ada[0, 256 * j:256 * (j + 1), 2048 * i:2048 * (i + 1)].rearrange("(k p) n -> p k n", p=P)
            if kind == "in":
                return w_in[0, :, 512 * i:512 * (i + 1)].rearrange("(k p) n -> p k n", p=P)
            if kind == "hy":
                return a["w_hy_out"][0].rearrange("(k p) n -> p k n", p=P)
            if kind == "att":
                return a["w_attn_out"][0].rearrange("(k p) n -> p k n", p=P)
            return a["w_mix_out"][0, 512 * i:512 * (i + 1), :].rearrange("(k p) n -> p k n", p=P)

        def block_view(b):
            kind = b[0]
            k = {"ada": 2, "in": 8, "hy": 4, "att": 4, "mix": 4}[kind]
            return ring[where[b] % 6].rearrange("p (k n) -> p k n", k=k)

        w_gu, w_dn = a["w_gate_up"], a["w_down"]
        block = ctx.enter_context(nc.Block())

        @block.sync
        def _(sp):
            def wait_used(b):
                kind, i, j = b
                if kind == "ada":
                    sp.wait_ge(S["ada_used"], 4 * i + j + 1)
                elif kind == "in":
                    sp.wait_ge(S["u_ps"], 2 * i + 2)
                elif kind == "mix":
                    sp.wait_ge(S["mix_ps"], i + 3)
                else:
                    sp.wait_ge(S["pj_ps"], KD)

            sp.dma_start(at("tab"), a["t_small"]).then_inc(S["tab_in"], 16)
            sp.wait_ge(S["prm_zero"], 1)
            rows = lambda v: v.rearrange("(r n) -> r n", n=P)
            pieces = [(C_C, 8, rows(a["c"][0])), (C_BHY, 20, rows(a["b_in"][0, 0:2560])),
                      (C_BG, 16, rows(a["b_in"][0, 3072:5120])),
                      (C_W, 36, a["hy_conv_w"][0].rearrange("j (r n) -> (j r) n", n=P)), (C_CB, 12, rows(a["hy_conv_b"][0])),
                      (C_DS, 4, rows(a["hy_d_skip"][0])), (C_SG, 1, a["attn_subln_g"])]
            for r0, n, src in pieces:
                sp.dma_start(prm[r0:r0 + n, :], src).then_inc(S["prm_in"], 16)
            for r, name in ((C_F, "filt_b1"), (C_F + 1, "filt_b2"), (C_F + 2, "filt_b3"), (C_F + 3, "filt_freq")):
                sp.dma_start(prm[r:r + 1, 0:64], a[name]).then_inc(S["prm_in"], 16)
            for n, b in enumerate(blocks):
                if n >= 6:
                    wait_used(blocks[n - 6])
                sp.dma_start(block_view(b), block_source(b)).then_inc(s_front[n % 6], 16)
                if n == 0:
                    sp.dma_start(decay, a["t_decay"].rearrange("s (t p) c -> p s t c", p=P)).then_inc(S["decay_in"], 16)
                elif n == 2:
                    sp.dma_start(dft, a["t_dft"].rearrange("(t p) f -> p t f", p=P)).then_inc(S["dft_in"], 16)

            def gate_up(k, item):
                dst, s = (odd_slot[k], s_odd[k]) if item == 1 and k < OWN else (gu_slot[k], s_gu[k])
                sp.dma_start(dst, w_gu[0, item, k * P:(k + 1) * P, :]).then_inc(s, 16)

            def down(c, item):
                sp.dma_start(dn_slot[c], w_dn[0, item, c * 256:(c + 1) * 256, :].rearrange("(q p) n -> p q n", p=P))\
                    .then_inc(s_dn[c], 16)

            last_use = {n % 6: n for n in range(len(blocks))}
            for f in sorted(range(6), key=lambda s: last_use[s]):
                if blocks[last_use[f]] == ("mix", 0, 0):
                    sp.wait_ge(S["pj_sb"], KD)
                    gate_up(0, 1)
                    gate_up(1, 1)
                    sp.wait_ge(S["s_ps"], 2 * HEADS)
                    gate_up(4, 1)
                    sp.wait_ge(S["bc_sb"], 6)
                    gate_up(2, 1)
                wait_used(blocks[last_use[f]])
                for k in (2 * f, 2 * f + 1):
                    gate_up(k, 0) if k < KD else down(k - KD, 0)
            sp.wait_ge(S["x1_rdy"], 4)
            gate_up(3, 1)
            gate_up(5, 1)
            for k in range(OWN):
                sp.wait_ge(S["gu_used"], k + 1)
                gate_up(k, 2)
            for k in range(OWN, KD):
                sp.wait_ge(S["gu_used"], k + 1)
                gate_up(k, 1)

            def stream(pair, expert, ks, odd, used):
                for k in ks:
                    dst, s = (odd_slot[k], s_odd[k]) if odd and k < OWN else (gu_slot[k], s_gu[k])
                    sp.wait_ge(S["gu_used"], pair * 16 + (used + k + 1))
                    sp.dma_start(dst, w_gu[0, bass.ds(expert, 1), k * P:(k + 1) * P, :]
                                 .rearrange("o p n -> p (o n)")).then_inc(s, 16)

            def stream_down(pair, expert, used):
                for c in range(4):
                    sp.wait_ge(S["dn_used"], pair * 8 + (used + c + 1))
                    sp.dma_start(dn_slot[c], w_dn[0, bass.ds(expert, 1), c * 256:(c + 1) * 256, :]
                                 .rearrange("o (q p) n -> p (o q) n", p=P)).then_inc(s_dn[c], 16)

            def expert_of(index):
                return sp.value_load(table_i[0:1, bass.ds(index, 1)], min_val=0, max_val=E - 1)

            own, rest = range(OWN), range(OWN, KD)
            stream(1, 3, own, True, -8)
            stream(1, 2, rest, False, -8)
            stream_down(1, 1, -8)
            stream(1, 4, own, False, 0)
            stream(1, 3, rest, True, 0)
            stream_down(1, 2, -4)
            sp.wait_ge(S["tables"], 2)
            last_pair = sp.value_load(table_i[0:1, 49:50], min_val=E // 2 - 1, max_val=ITEMS // 2 - 1)
            with sp.Fori(2, last_pair) as p:
                e_prev, e_a, e_b = expert_of(p * 2 - 1), expert_of(p * 2), expert_of(p * 2 + 1)
                stream(p, e_b, own, True, -8)
                stream(p, e_a, rest, False, -8)
                stream_down(p, e_prev, -8)
                stream(p, e_b, rest, True, 0)
                stream_down(p, e_a, -4)
                e_next = expert_of(p * 2 + 2)
                stream(p, e_next, own, False, 0)
            q = sp.value_load(table_i[0:1, 50:51], min_val=E // 2 - 2, max_val=ITEMS // 2 - 2)
            e_prev, e_a, e_b = expert_of(q * 2 + 1), expert_of(q * 2 + 2), expert_of(q * 2 + 3)
            stream(q, e_a, rest, False, 8)
            stream_down(q, e_prev, 0)
            stream(q, e_b, own, True, 8)
            stream(q, e_b, rest, True, 16)
            stream_down(q, e_a, 4)
            for c in range(4):
                sp.wait_ge(S["gu_used"], q * 16 + (16 + c + 1))
                sp.dma_start(last_down[c], w_dn[0, bass.ds(e_b, 1), c * 256:(c + 1) * 256, :]
                             .rearrange("o (q p) n -> p (o q) n", p=P)).then_inc(s_gu[c], 16)
            sp.wait_ge(S["gu_used"], q * 16 + 32)
            sp.dma_start(fgB, a["final_norm_g"][:].partition_broadcast(P)).then_inc(S["fg_in"], 16)
            for t in range(TT):
                sp.wait_ge(S["fin_rdy"], t + 1)
                sp.dma_start(out[0, t * P:(t + 1) * P, :], fin[:, t, :]).then_inc(S["out_done"], 16)
            sp.wait_ge(S["out_done"], 16 * TT)

        @block.gpsimd
        def _(pool):
            nc.gpsimd.memset(prm, 0.0).then_inc(S["prm_zero"], 1)
            for q in range(4):
                pool.dma_start(adr[0][32 * q:32 * q + 32, :], a["b_ada"][0, 512 * q:512 * (q + 1)].partition_broadcast(32))\
                    .then_inc(S["gain_in"], 16)
            for r0, name in ((0, "norm_ffn_g"), (64, "norm_mix_g")):
                for h in range(2):
                    pool.dma_start(gain[r0 + 32 * h:r0 + 32 * h + 32, :],
                                   a[name][0, 512 * h:512 * (h + 1)].partition_broadcast(32)).then_inc(S["gain_in"], 16)
            pool.dma_start(at("lam"), a["lambda_qk"][0].rearrange("a b -> (a b)").partition_broadcast(P))\
                .then_inc(S["lam_in"], 16)
            pool.wait_ge(S["filt_sb"], TT)
            nc.gpsimd.memset(at("qm"), 0.0).then_inc(S["qm_zero"], 1)
            pool.wait_ge(S["kB_ps"], 2)
            nc.gpsimd.memset(uraw[:, :, 0:1], 0.0).then_inc(S["pad_zero"], 1)
            nc.gpsimd.memset(uraw[:, :, 257:258], 0.0).then_inc(S["pad_zero"], 1)
            pool.wait_ge(S["Y_rdy"], 2)
            nc.gpsimd.memset(sel_bias, 0.0).then_inc(S["gub_zero"], 1)
            pool.wait_ge(S["gub_zero"], 1)
            pool.dma_start(sel_bias[0:E, :], a["b_gate_up"][0]).then_inc(S["gub_in"], 16)
            pool.wait_ge(S["pj_sb"], KD)
            pool.dma_start(b_down[0:E, :], a["b_down"][0]).then_inc(S["bd_in"], 16)
            pool.wait_ge(S["bc_sb"], 6)
            for t in range(TT):
                pool.wait_ge(S["xs_rdy"], t + 1)
                nc.gpsimd.tensor_tensor(xn[:, t, :], xn[:, t, :], gsB, ALU.mult).then_inc(S["pool_step"], 1)
                pool.wait_ge(S["pool_step"], t + 1)
                nc.gpsimd.tensor_tensor(xn[:, t, :], xn[:, t, :], shB, ALU.add).then_inc(S["h2_rdy"], 1)

        @block.tensor
        def _(pe):
            mm = pe.matmul

            def bank(b, n=512, o=0):
                return ps[:, b, o:o + n]

            def front_in(b):
                n = where[b]
                pe.wait_ge(s_front[n % 6], 16 * (n // 6 + 1))
                return block_view(b)

            pe.wait_ge(S["tab_in"], 16)
            pe.wait_ge(S["prm_in"], 16 * 11)
            pe.transpose(bank(3, 128), prm, ident).then_inc(S["prmT_ps"], 1)
            pe.wait_ge(S["filt_in"], 16 * 5)
            mm(ps[0:64, 0, 0:256], w1[0:17, :], zT[0:17, :], start=True, stop=True).then_inc(S["f1_ps"], 1)
            pe.wait_ge(S["hid_1"], 1)
            mm(ps[0:64, 1, 0:256], w2[0:64, :], hid[0:64, :], start=True, stop=True).then_inc(S["f2_ps"], 1)
            pe.wait_ge(S["hid_2"], 1)
            mm(ps[0:64, 2, 0:256], w3[0:64, :], hid[0:64, :], start=True, stop=True).then_inc(S["f3_ps"], 1)
            def ada_first(b, js):
                for j in js:
                    w = front_in(("ada", 0, j))
                    for kk in range(2):
                        k = 2 * j + kk
                        for q in range(4):
                            last = mm(ps[32 * q:32 * q + 32, b, :], cs[:, k, :], w[:, kk, q * 512:(q + 1) * 512],
                                      start=(k == 0), stop=(k == KD - 1))
                    last.then_inc(S["ada_used"], 1)

            def ada_pair(g, b, pair):
                pe.wait_ge(S["weighted"], 2 * (g - 1) + pair + 1)
                w = block_view(("ada", g, 2 * pair))
                for q in range(4):
                    last = mm(ps[32 * q:32 * q + 32, b, :], ones[:, 0:32], w[:, 0, q * 512:(q + 1) * 512],
                              start=(pair == 0), stop=(pair == 1))
                last.then_inc(S["ada_used"], 2)

            def ada_cols(g, b):
                for j in range(4):
                    last = pe.transpose(bank(b, 128, j * 128), adr[g][:, j * P:(j + 1) * P], ident)
                return last

            def rows_turned(ks):
                for k in ks:
                    for t in range(TT):
                        last = pe.transpose(bank(k // 2, 128, (k % 2) * 256 + t * 128), xn[:, t, k * P:(k + 1) * P],
                                            ident)
                return last

            pe.wait_ge(S["silu_c"], 1)
            pe.wait_ge(S["prmT_sb"], 1)
            ada_first(3, (0,))
            pe.wait_ge(S["hid_3"], 1)
            for s in range(2):
                for t in range(TT):
                    mm(bank(4 + 2 * s + t), hid[0:64, t * P:(t + 1) * P], w4[0:64, s * HW:(s + 1) * HW],
                       start=True, stop=True).then_inc(S["f4_ps"], 1)
            ada_first(3, (1,))
            pe.wait_ge(S["xn_rdy"], 1)
            rows_turned(range(6))
            ada_first(3, (2,))

            pe.wait_ge(S["dft_in"], 16)
            pe.wait_ge(S["filt_sb"], TT)

            def spectrum(b, f0, taps):
                for t in range(TT):
                    last = mm(bank(b), dft[:, t, f0:f0 + P], taps[:, t, :], start=(t == 0), stop=(t == TT - 1))
                return last

            spectrum(6, 0, kplus)
            spectrum(7, 128, kplus).then_inc(S["kA_ps"], 1)
            ada_first(3, (3,))
            spectrum(4, 256, kplus).then_inc(S["kN_ps"], 1)
            pe.wait_ge(S["ada0_sb"], 2)
            ada_cols(0, 5).then_inc(S["mc_ps"], 1)
            rows_turned((6, 7)).then_inc(S["xT_ps"], 1)
            pe.wait_ge(S["mc_sb"], 1)
            spectrum(5, 256, kminus).then_inc(S["kB_ps"], 1)
            pe.wait_ge(S["kA_sb"], 1)
            spectrum(6, 384, kminus).then_inc(S["kB_ps"], 1)

            pe.wait_ge(S["h1_sb"], 1)
            pe.wait_ge(S["h1_act"], 1)

            def unit(n):
                blk, half = n // 2, n % 2
                w = front_in(("in", blk, 0))
                if n >= 3:
                    m = n - 3
                    if m in (10, 11):
                        pe.wait_ge(S["v_sb"], m - 9)
                    else:
                        pe.wait_ge(S["u_sb"], m + 1 if m < 10 else m - 1)
                b = n % 3
                if blk == 5:
                    for k in range(KD):
                        last = mm(bank(b), hT[:, k, half * P:(half + 1) * P], w[:, k, :],
                                  start=(k == 0), stop=(k == KD - 1))
                else:
                    for c in range(2):
                        cc = 2 * half + c
                        for k in range(KD):
                            last = mm(bank(b, 256, c * 256), w[:, k, cc * P:(cc + 1) * P], hT[:, k, :],
                                      start=(k == 0), stop=(k == KD - 1))
                last.then_inc(S["u_ps"], 1)

            for blk in range(6):
                unit(2 * blk)
                unit(2 * blk + 1)
                if blk == 0:
                    pe.wait_ge(S["kf_done"], 1)
                if blk in ada_after:
                    g, pair = ada_after[blk]
                    ada_pair(g, 5 + g, pair)
            pe.wait_ge(S["vT_rdy"], 1)
            for t in range(TT):
                for c in range(CT):
                    last = pe.transpose(bank(3 + t, 128, c * 128), vT[:, c, t * P:(t + 1) * P], ident)
                last.then_inc(S["vt_ps"], 1)
            unit(12)
            pe.wait_ge(S["vt_sb"], 2)
            unit(13)
            pe.wait_ge(S["ada1_sb"], 1)
            pe.wait_ge(S["ada2_sb"], 1)
            for f in range(4):
                for t in range(TT):
                    last = mm(bank(4 + f), dft[:, t, f * P:(f + 1) * P], vtc[:, t, :],
                              start=(t == 0), stop=(t == TT - 1))
                last.then_inc(S["V_ps"], 1)
            unit(14)
            unit(15)
            pe.wait_ge(S["Y_rdy"], 2)
            pe.wait_ge(S["inv_in"], 16)
            for c in range(CT):
                for f in range(4):
                    last = mm(bank(6 + c // 2, 256, (c % 2) * 256), Y[:, f, c * P:(c + 1) * P], inv[:, f, :],
                              start=(f == 0), stop=(f == 3))
            last.then_inc(S["yT_ps"], 1)

            def scores(j):
                t, h = j // HEADS, j % HEADS
                if j >= 2:
                    pe.wait_ge(S["s_sb"], j - 1)
                for c in range(2):
                    last = mm(bank(4 + j % 2, 256, c * 256), qm[:, h, c, t * P:(t + 1) * P], kT[:, h, :],
                              start=True, stop=True)
                last.then_inc(S["s_ps"], 1)

            def weights_T(j):
                pe.wait_ge(S["a_rdy"], j + 1)
                if j >= 2:
                    pe.wait_ge(S["aT_sb"], j - 1)
                for k in range(TT):
                    last = pe.transpose(bank(3, 128, (j % 2) * 256 + k * 128), ab[j % 2][:, k * P:(k + 1) * P], ident)
                last.then_inc(S["aT_ps"], 1)

            def values(j):
                t, h = j // HEADS, j % HEADS
                pe.wait_ge(S["aT_sb"], j + 1)
                for k in range(TT):
                    last = mm(bank(6 + t, 128, h * 128), aT[j % 2][:, k, :], ve[:, k, h * P:(h + 1) * P],
                              start=(k == 0), stop=(k == TT - 1))
                last.then_inc(S["o_ps"], 1)

            pe.wait_ge(S["u_sb"], 10)
            pe.wait_ge(S["v_sb"], 2)
            scores(0)
            scores(1)
            pe.wait_ge(S["u_sb"], 14)
            pe.wait_ge(S["ada1_sb"], 1)
            ada_cols(1, 0).then_inc(S["mc_ps"], 1)
            pe.wait_ge(S["ada2_sb"], 2)
            ada_cols(2, 1).then_inc(S["mc_ps"], 1)

            pe.wait_ge(S["mc_sb"], 3)
            pe.wait_ge(S["wr_in"], 16)
            for k in range(KD):
                last = mm(bank(1, E), modc[:, 1, 2 + k // 4, k % 4:k % 4 + 1].to_broadcast([P, P]), wr[:, k, :],
                          start=(k == 0), stop=(k == KD - 1))
            last.then_inc(S["rb_ps"], 1)

            def attention_gate(i):
                m = i // 2
                if i % 2 == 0:
                    if m == 1:
                        pe.wait_ge(S["rb_sb"], 1)
                    elif m == 3:
                        pe.wait_ge(S["u_sb"], 15)
                w = front_in(("in", 8 + m // 2, 0))
                cc = i % 4
                for k in range(KD):
                    last = mm(bank(m % 3, 256, (i % 2) * 256), w[:, k, cc * P:(cc + 1) * P], hT[:, k, :],
                              start=(k == 0), stop=(k == KD - 1))
                if i % 2:
                    last.then_inc(S["u_ps"], 1)

            attention_gate(0)
            pe.wait_ge(S["yhy_rdy"], 1)
            for j in range(2 * HEADS + 1):
                if j < 2 * HEADS:
                    weights_T(j)
                    if j + 2 < 2 * HEADS:
                        scores(j + 2)
                if j >= 1:
                    values(j - 1)
                if j + 1 < KD:
                    attention_gate(j + 1)
            why, wat = front_in(("hy", 0, 0)), front_in(("att", 0, 0))

            def heads_turned(t):
                pe.wait_ge(S["on_rdy"], t + 1)
                for h in range(HEADS):
                    last = pe.transpose(bank(3, 128, h * 128), on[:, h * P:(h + 1) * P], ident)
                last.then_inc(S["oT_ps"], 1)

            def project(i, src, w, o):
                for k in range(CT):
                    last = mm(bank(pj_bank[i % 4], 256, o), w[:, k, i * P:(i + 1) * P], src[:, k, :],
                              start=(k == 0), stop=(k == CT - 1))
                return last

            pe.wait_ge(S["aT_sb"], 2 * HEADS)
            heads_turned(0)
            pe.wait_ge(S["u_sb"], 18)
            for i in range(3):
                project(i, y_hyT, why, 0)
            pe.wait_ge(S["oT_sb"], 1)
            heads_turned(1)
            project(3, y_hyT, why, 0)
            pe.wait_ge(S["oT_sb"], TT)
            for i in range(KD):
                if i >= 4:
                    pe.wait_ge(S["pj_sb"], i - 3)
                    project(i, y_hyT, why, 0)
                project(i, y_atT, wat, 256).then_inc(S["pj_ps"], 1)
            pe.wait_ge(S["pj_sb"], 6)
            mix = [front_in(("mix", i, 0)) for i in range(2)]

            def mixed(t, h, k):
                return mm(bank(2 * t + h), merged[:, k, t * P:(t + 1) * P], mix[k // 4][:, k % 4, h * 512:(h + 1) * 512],
                          start=(k == 0), stop=(k == KD - 1))

            for k in range(KD):
                if k >= 6:
                    pe.wait_ge(S["pj_sb"], k + 1)
                for h in range(2):
                    last = mixed(0, h, k)
            last.then_inc(S["mix_ps"], 1)
            for k in range(KD):
                last = mixed(1, 0, k)
            last.then_inc(S["mix_ps"], 1)

            def residual_turned(b, t, half):
                for kk in range(4):
                    k = 4 * half + kk
                    last = pe.transpose(bank(b, 128, kk * 128), x[:, t, k * P:(k + 1) * P], ident)
                return last

            pe.wait_ge(S["x1_rdy"], 2)
            residual_turned(4, 0, 0)
            residual_turned(5, 0, 1).then_inc(S["x1T_ps"], 1)
            for k in range(KD):
                last = mixed(1, 1, k)
                if k % 4 == 3:
                    last.then_inc(S["mix_ps"], 1)
            pe.wait_ge(S["x1_rdy"], 3)
            residual_turned(6, 1, 0).then_inc(S["x1T_ps"], 1)

            def router_parts(t):
                for kk in range(2):
                    for q in range(4):
                        last = mm(ps[32 * q:32 * q + 32, 4, 0:P], wr_scaled[:, 2 * q + kk, :],
                                  hT[:, 2 * q + kk, t * P:(t + 1) * P], start=(kk == 0), stop=(kk == 1))
                last.then_inc(S["part_ps"], 1)

            def router_sum(t):
                pe.wait_ge(S["part_sb"], t + 1)
                return mm(bank(5, E, E * t), part[:, t * P:(t + 1) * P], tab("quad"), start=True, stop=True)

            pe.wait_ge(S["rb_sb"], 2)
            pe.wait_ge(S["x1T_dve"], 1)
            router_parts(0)
            pe.wait_ge(S["x1_rdy"], 4)
            residual_turned(7, 1, 1).then_inc(S["x1T_ps"], 1)
            router_sum(0)
            pe.wait_ge(S["x1T_dve"], 2)
            pe.wait_ge(S["x1T_act"], 1)
            router_parts(1)
            router_sum(1).then_inc(S["log_ps"], 1)
            pe.wait_ge(S["m_rdy"], 1)
            mm(bank(5, 32, 128), tri, M[:, 0, :], start=True, stop=True)
            mm(bank(5, 32, 160), ones, M[:, 0, :], start=True, stop=False)
            mm(bank(5, 32, 160), tri, M[:, 1, :], start=False, stop=True).then_inc(S["rank_ps"], 1)
            mm(bank(2, 32, 0), ones, M[:, 0, :], start=True, stop=False)
            mm(bank(2, 32, 0), ones, M[:, 1, :], start=False, stop=True)
            for t in range(TT):
                last = mm(ps[0:32, 2, 128:256], M[:, t, :], ones, start=(t == 0), stop=(t == TT - 1))
            last.then_inc(S["cnt_ps"], 1)
            def gather(p):
                pe.wait_ge(S["sel_rdy"], p + 1)
                for half in range(2):
                    b = 7 - half
                    for kk in range(4):
                        k = 4 * half + kk
                        for t in range(TT):
                            last = mm(bank(b, 128, kk * 128), xn[:, t, k * P:(k + 1) * P], Sel[:, t, :],
                                      start=(t == 0), stop=(t == TT - 1))
                    last.then_inc(S["ga_done"], 1)

            def gate_up(p, s):
                for b in range(2):
                    for h in range(2):
                        mm(ps[64 * h:64 * h + 64, 4 + b, :], mask[:, s, :],
                           sel_bias[:, b * 1024 + h * 512:b * 1024 + (h + 1) * 512], start=True, stop=False)
                for k in range(KD):
                    if k < OWN:
                        w, landed = (odd_slot[k], s_odd[k]) if s else (gu_slot[k], s_gu[k])
                        pe.wait_ge(landed, p * 16 + 16)
                    else:
                        w = gu_slot[k]
                        pe.wait_ge(s_gu[k], p * 32 + (16 * s + 16))
                    for b in range(2):
                        for h in range(2):
                            last = mm(ps[64 * h:64 * h + 64, 4 + b, :], hTp[:, k, s * 64:(s + 1) * 64],
                                      w[:, b * 1024 + h * 512:b * 1024 + (h + 1) * 512],
                                      start=False, stop=(k == KD - 1))
                    last.then_inc(S["gu_used"], 1)

            def act_transpose():
                for j in range(4):
                    last = pe.transpose(bank(7, 128, j * 128), act_o[:, j * P:(j + 1) * P], ident)
                last.then_inc(S["tr_done"], 1)

            def down(landed, slots, count):
                for c in range(4):
                    pe.wait_ge(landed[c], count)
                    for qq in range(2):
                        q = 2 * c + qq
                        lhs = actT[:, q % 4, (q // 4) * 64:(q // 4) * 64 + 64]
                        for h in range(2):
                            last = mm(ps[64 * h:64 * h + 64, 6, :], lhs, slots[c][:, qq, h * 512:(h + 1) * 512],
                                      start=(q == 0), stop=(q == 7))
                    last.then_inc(S["dn_used"], 1)

            def scatter(stop):
                for t in range(TT):
                    for h in range(2):
                        last = mm(bank(2 * t + h), Pw[:, t, :], y[:, h * 512:(h + 1) * 512],
                                  start=False, stop=stop, skip_group_check=True)
                    if stop and t < TT - 1:
                        last.then_inc(S["sc_tile"], 1)
                last.then_inc(S["sc_done"], 1)

            def place_weights():
                for t in range(TT):
                    last = pe.transpose(bank(7, 128, t * 128), Wt[:, t, :], ident)
                last.then_inc(S["pt_done"], 1)

            pe.wait_ge(S["gub_in"], 16)
            pe.wait_ge(S["h2_rdy"], TT)
            gather(0)
            pe.wait_ge(S["cnt_sb"], 2)
            mm(bank(3, 48, 0), cntT2[0:E, :], tri[0:E, 0:48], start=True, stop=True).then_inc(S["ex_ps"], 1)
            pe.wait_ge(S["mask_rdy"], 1)
            pe.wait_ge(S["ga_sb"], 2)
            gate_up(0, 0)
            pe.wait_ge(S["g_all"], TOPK)
            for t in range(TT):
                last = pe.transpose(ps[0:32, 6, 128 * t:128 + 128 * t], G[:, t, :], ident)
            last.then_inc(S["gt_ps"], 1)
            pe.wait_ge(S["gt_sb"], 1)
            pe.wait_ge(S["bd_in"], 16)
            for t in range(TT):
                for h in range(2):
                    mm(bank(2 * t + h), GT[0:E, t * P:(t + 1) * P], b_down[0:E, h * 512:(h + 1) * 512],
                       start=True, stop=False, skip_group_check=True)
            pe.wait_ge(S["act_rdy"], 1)
            act_transpose()
            gate_up(0, 1)
            pe.wait_ge(S["actT_rdy"], 1)
            down(s_dn, dn_slot, 16)
            pe.wait_ge(S["act_rdy"], 2)
            act_transpose()
            pe.wait_ge(S["actT_rdy"], 2)
            pe.wait_ge(S["y_rdy"], 1)
            gather(1)
            pe.wait_ge(S["wt_rdy"], 1)
            pe.wait_ge(S["ga_sb"], 3)
            place_weights()
            pe.wait_ge(S["tables"], 2)
            n_pairs = pe.value_load(table_i[0:1, 48:49], min_val=E // 2, max_val=ITEMS // 2)
            with pe.Fori(1, n_pairs) as p:
                pe.wait_ge(S["mask_rdy"], p + 1)
                pe.wait_ge(S["ga_sb"], p * 2 + 2)
                gate_up(p, 0)
                pe.wait_ge(S["actT_rdy"], p * 2)
                down(s_dn, dn_slot, p * 32)
                pe.wait_ge(S["act_rdy"], p * 2 + 1)
                pe.wait_ge(S["pt_sb"], p)
                act_transpose()
                gate_up(p, 1)
                pe.wait_ge(S["y_rdy"], p * 2)
                scatter(False)
                pe.wait_ge(S["actT_rdy"], p * 2 + 1)
                down(s_dn, dn_slot, p * 32 + 16)
                pe.wait_ge(S["act_rdy"], p * 2 + 2)
                act_transpose()
                pe.wait_ge(S["actT_rdy"], p * 2 + 2)
                pe.wait_ge(S["y_rdy"], p * 2 + 1)
                gather(p + 1)
                pe.wait_ge(S["wt_rdy"], p + 1)
                pe.wait_ge(S["ga_sb"], p * 2 + 3)
                place_weights()
            pe.wait_ge(S["ga_sb"], n_pairs * 2 + 2)
            down(s_gu, last_down, n_pairs * 16 + 16)
            pe.wait_ge(S["y_rdy"], n_pairs * 2)
            pe.wait_ge(S["pt_sb"], n_pairs)
            scatter(True)

        @block.scalar
        def _(act):
            A = nc.scalar.activation
            step = Steps(act, S["act_step"])
            for dst, name in ((zT[0:17, :], a["t_z"]), (w1[0:17, :], a["filt_w1"][0]), (w2[0:64, :], a["filt_w2"][0]),
                              (w3[0:64, :], a["filt_w3"][0]), (w4[0:64, :], a["filt_w4"][0])):
                act.dma_start(dst, name).then_inc(S["filt_in"], 16)
            act.dma_start(x, a["x"][0].rearrange("(t p) d -> p t d", p=P)).then_inc(S["x_in"], 16)

            def bias_rows(g):
                for q in range(4):
                    o = g * 2048 + q * 512
                    act.dma_start(adr[g][32 * q:32 * q + 32, :], a["b_ada"][0, o:o + 512].partition_broadcast(32))\
                        .then_inc(S["ada_in"], 16)

            act.wait_ge(S["prmT_sb"], 1)
            sig(act, A(at("cs", 0, 8), prmT[:, C_C:C_C + 8], ACT.Sigmoid), "sig_c", 1)

            def sine(n):
                act.wait_ge(S[f"ang_{n}"], 1)
                A(hid[0:64, :], ang[0:64, :], ACT.Sin).then_inc(S[f"hid_{n}"], 1)

            for n in range(1, 4):
                sine(n)
            act.wait_ge(S["x_in"], 16)
            for t in range(TT):
                A(xn[:, t, :], x[:, t, :], ACT.Square, accum_out=ss[:, t:t + 1]).then_inc(S["x_sq"], 1)
            bias_rows(1)
            bias_rows(2)
            act.dma_start(at("bv"), a["b_in"][0, 2560:3072].partition_broadcast(P)).then_inc(S["bv_in"], 16)
            act.dma_start(at("br"), a["b_router"][0].partition_broadcast(P)).then_inc(S["br_in"], 16)
            act.dma_start(inv, a["t_inv"].rearrange("(f p) t -> p f t", p=P)).then_inc(S["inv_in"], 16)
            act.wait_ge(S["lam_a"], 1)
            sig(act, A(lam2, lam2, ACT.Exp), "lam_e", 1)
            act.dma_start(wr, a["w_router"][0].rearrange("(k p) e -> p k e", p=P)).then_inc(S["wr_in"], 16)
            act.wait_ge(S["kA_ps"], 1)
            step(A(kA[:, 0, :], ps[:, 6, :], ACT.Copy))
            step(A(kN, ps[:, 6, :], ACT.Copy))
            sig(act, A(kA[:, 1, :], ps[:, 7, :], ACT.Copy), "kA_sb", 1)
            act.wait_ge(S["mc_sb"], 1)
            act.wait_ge(S["xT_ps"], 1)
            for k in range(KD // 2, KD):
                last = A(hT[:, k, :], ps[:, k // 2, (k % 2) * 256:(k % 2) * 256 + 256], ACT.Identity,
                         scale=modc[:, 0, 2 + k // 4, k % 4:k % 4 + 1], bias=modc[:, 0, k // 4, k % 4:k % 4 + 1])
            last.then_inc(S["h1_act"], 1)

            def evacuate(n):
                act.wait_ge(S["u_ps"], n + 1)
                for c in range(2):
                    src = ps[:, n % 3, c * 256:(c + 1) * 256]
                    i = 2 * n + c
                    if n < 6:
                        last = A(uraw[:, i, 1:257], src, ACT.Identity, bias=col(C_BHY + i))
                    elif n < 8:
                        h = i - 12
                        for r in range(2):
                            last = A(qm[64 * r:64 * r + 64, h, r, :], src[64 * r:64 * r + 64, :], ACT.Identity,
                                     bias=col(C_BQ + h, 64 * r, 64 * r + 64))
                    elif n < 10:
                        last = A(kT[:, i - 16, :], src, ACT.Identity, bias=col(C_BK + i - 16))
                    else:
                        last = A(gate_hy[:, i - 24, :], src, ACT.Sigmoid, bias=col(C_BG + i - 24))
                last.then_inc(S["u_sb"], 1)

            act.wait_ge(S["qm_zero"], 1)
            act.wait_ge(S["pad_zero"], 2)
            for n in range(10):
                evacuate(n)
            for t in range(TT):
                act.wait_ge(S["vt_ps"], t + 1)
                A(vtc[:, t, :], ps[:, 3 + t, :], ACT.Copy).then_inc(S["vt_sb"], 1)
            for n in range(12, 16):
                evacuate(n)

            def every_partition(dst, g, q):
                for r in range(4):
                    last = A(dst[32 * r:32 * r + 32, :], adr[g][32 * q:32 * q + 32, :], ACT.Copy)
                last.then_inc(S["bc_sb"], 1)

            act.wait_ge(S["ada1_sb"], 1)
            act.wait_ge(S["V_ps"], 4)
            every_partition(gate1B[:, 0:512], 1, 0)
            every_partition(gate1B[:, 512:1024], 1, 1)
            for j in range(2 * HEADS):
                act.wait_ge(S["negm_rdy"], j + 1)
                for c in range(2):
                    last = A(sc[j % 2][:, c, :], sc[j % 2][:, c, :], ACT.Exp, scale=0.125,
                             bias=negm[:, 2 * (j % 2) + c:2 * (j % 2) + c + 1],
                             accum_out=sums[:, 2 * (j % 2) + c:2 * (j % 2) + c + 1])
                    if c == 1:
                        last.then_inc(S["exp_done"], 1)
                    else:
                        step(last)
                if j % 2:
                    m = j // 2
                    act.wait_ge(S["u_ps"], 17 + m)
                    for c in range(2):
                        last = A(gate_at[2 * m + c], ps[:, m % 3, c * 256:(c + 1) * 256], ACT.Identity,
                                 bias=col(C_BG + 8 + 2 * m + c))
                    last.then_inc(S["u_sb"], 1)
                if j in (4, 7):
                    t = j // 4 - (j == 4)
                    act.wait_ge(S["o_ps"], 4 if j == 4 else 8)
                    if t:
                        act.wait_ge(S["on_rdy"], t)
                    A(at("bv"), ps[:, 6 + t, :], ACT.Square).then_inc(S["o_sq"], 1)
            for n, g in enumerate((at("uc", 2048, 1024), at("ur", 2048, 1024))):
                act.wait_ge(S["u_sb"], 16 + 2 * n)
                A(g, g, ACT.Sigmoid).then_inc(S["gat_rdy"], 1)
            act.wait_ge(S["s_ps"], 2 * HEADS)
            act.wait_ge(S["o_ps"], 2 * HEADS)
            act.wait_ge(S["ada2_sb"], 2)
            for h in range(2):
                every_partition(shB[:, 512 * h:512 * (h + 1)], 1, 2 + h)
            for h in range(2):
                every_partition(gsB[:, 512 * h:512 * (h + 1)], 2, h)
            def row_squares(t):
                act.wait_ge(S["x1_rdy"], 2 * t + 2)
                A(xn[:, t, :], x[:, t, :], ACT.Square, accum_out=ss[:, t:t + 1]).then_inc(S["x1_sq"], 1)

            def rows_over_norm(t):
                act.wait_ge(S["rs_rdy"], t + 1)
                A(xn[:, t, :], x[:, t, :], ACT.Copy, scale=rs[:, t:t + 1]).then_inc(S["xs_rdy"], 1)

            def part_copy(t):
                act.wait_ge(S["part_ps"], t + 1)
                A(part[:, t * P:(t + 1) * P], ps[:, 4, 0:P], ACT.Copy).then_inc(S["part_sb"], 1)

            row_squares(0)
            rows_over_norm(0)
            act.wait_ge(S["x1T_ps"], 2)
            A(hT[:, 0:4, P:2 * P], ps[:, 6, :].rearrange("p (k t) -> p k t", k=4), ACT.Copy).then_inc(S["x1T_act"], 1)
            part_copy(0)
            row_squares(1)
            part_copy(1)
            rows_over_norm(1)
            act.wait_ge(S["top_rdy"], 1)
            A(gexp, gexp, ACT.Exp).then_inc(S["top_exp"], 1)

            def sigmoid(i):
                act.wait_ge(S["g_rdy"], i + 1)
                A(s_sb, g_sb, ACT.Sigmoid, scale=1.702).then_inc(S["sig_rdy"], 1)

            def act_copy(i):
                act.wait_ge(S["tr_done"], i + 1)
                A(actT.rearrange("p j s -> p (j s)"), ps[:, 7, :], ACT.Copy).then_inc(S["actT_rdy"], 1)

            def y_copy(i, s):
                act.wait_ge(S["dn_used"], i * 4 + 4)
                for h in range(2):
                    last = A(y[64 * s:64 * s + 64, 512 * h:512 * (h + 1)], ps[64 * h:64 * h + 64, 6, :], ACT.Copy)
                last.then_inc(S["y_rdy"], 1)

            act.wait_ge(S["gt_ps"], 1)
            A(GT[0:E, :], ps[0:E, 6, 0:256], ACT.Copy).then_inc(S["gt_sb"], 1)
            sigmoid(0)
            act_copy(0)
            sigmoid(1)
            y_copy(0, 0)
            act_copy(1)
            act.wait_ge(S["tables"], 2)
            n_pairs = act.value_load(table_i[0:1, 48:49], min_val=E // 2, max_val=ITEMS // 2)
            with act.Fori(1, n_pairs) as p:
                sigmoid(p * 2)
                y_copy(p * 2 - 1, 1)
                act_copy(p * 2)
                sigmoid(p * 2 + 1)
                act.wait_ge(S["sc_done"], p)
                y_copy(p * 2, 0)
                act_copy(p * 2 + 1)
            act.wait_ge(S["gu_used"], n_pairs * 16)
            for h in range(2):
                every_partition(gate2B[:, 512 * h:512 * (h + 1)], 2, 2 + h)
            y_copy(n_pairs * 2 - 1, 1)
            for t in range(TT):
                act.wait_ge(S["x2_rdy"], 2 * t + 2)
                A(fin[:, t, :], x[:, t, :], ACT.Square, accum_out=ss[:, t:t + 1]).then_inc(S["fin_sq"], 1)

        @block.vector
        def _(v):
            V = nc.vector
            step = Steps(v, S["dve_step"])

            def rstd(dst, src, n, done=None):
                w = dst.shape[1]
                m, t = nwt[:, 0:w], nwt[:, 4:4 + w]
                step(V.tensor_scalar(m, src, 1.0 / n, EPS, ALU.mult, ALU.add))
                step(V.tensor_scalar(dst.bitcast(I32), m.bitcast(I32), -0.5, float(0x5F3759DF), ALU.mult, ALU.add))
                for n in range(3):
                    step(V.scalar_tensor_tensor(t, dst, -0.5, dst, ALU.mult, ALU.mult))
                    step(V.tensor_tensor(t, t, m, ALU.mult))
                    last = V.scalar_tensor_tensor(dst, t, 1.5, dst, ALU.add, ALU.mult)
                    if n < 2 or done is None:
                        step(last)
                if done is not None:
                    last.then_inc(done, 1)

            v.wait_ge(S["prmT_ps"], 1)
            sig(v, V.tensor_copy(prmT, ps[:, 3, 0:128]), "prmT_sb", 1)

            def angle(n, src):
                step(V.tensor_scalar(ang[0:64, :], src, col(C_F + n - 1, 0, 64), col(C_F + 3, 0, 64), ALU.add, ALU.mult))
                magic = 1.5 * 2.0 ** 23
                step(V.tensor_scalar(turns[0:64, :], ang[0:64, :], 1.0 / TWO_PI, magic, ALU.mult, ALU.add))
                step(V.tensor_scalar(turns[0:64, :], turns[0:64, :], -magic, None, ALU.add))
                for part in (6.28125, 0.0019350051879882812, 3.019915981956753e-07):
                    step(V.scalar_tensor_tensor(ang[0:64, :], turns[0:64, :], -part, ang[0:64, :], ALU.mult, ALU.add))
                pi = 3.1415925
                V.tensor_scalar(ang[0:64, :], ang[0:64, :], pi, -pi, ALU.min, ALU.max).then_inc(S[f"ang_{n}"], 1)

            v.wait_ge(S["tab_in"], 16)
            step(V.tensor_copy(ef[:, 0:E], tab("item")[:, 0:E]))
            step(V.tensor_scalar(ohI[:, 0:E], ef[:, 0:E], lane, None, ALU.is_equal))
            v.wait_ge(S["f1_ps"], 1)
            angle(1, ps[0:64, 0, 0:256])
            v.wait_ge(S["sig_c"], 1)
            cb = at("on", 0, 8)
            step(V.tensor_tensor(cb, at("cs", 0, 8), prmT[:, C_C:C_C + 8], ALU.mult))
            sig(v, V.tensor_copy(cs, cb.unsqueeze(2).to_broadcast([P, KD, 32])), "silu_c", 1)
            v.wait_ge(S["hid_1"], 1)
            v.wait_ge(S["f2_ps"], 1)
            angle(2, ps[0:64, 1, 0:256])
            v.wait_ge(S["hid_2"], 1)
            v.wait_ge(S["f3_ps"], 1)
            angle(3, ps[0:64, 2, 0:256])
            v.wait_ge(S["lam_in"], 16)
            lam = at("lam").rearrange("p (a b d) -> p a b d", a=2, b=2)
            lprod = at("on", 8, 128).rearrange("p (a d) -> p a d", a=2)
            step(V.tensor_tensor(lprod, lam[:, :, 0, :], lam[:, :, 1, :], ALU.mult))
            sig(v, V.tensor_reduce(lam2, lprod, AX.X, ALU.add), "lam_a", 1)
            v.wait_ge(S["x_sq"], TT)
            rstd(rs, ss, D)
            step(V.tensor_scalar(xn[:, 0, :], x[:, 0, :], rs[:, 0:1], None, ALU.mult))
            V.tensor_scalar(xn[:, 1, :], x[:, 1, :], rs[:, 1:2], None, ALU.mult).then_inc(S["xn_rdy"], 1)
            v.wait_ge(S["f4_ps"], 4)
            v.wait_ge(S["decay_in"], 16)
            for t in range(TT):
                step(V.tensor_tensor(kminus[:, t, :], ps[:, 4 + t, :], decay[:, 0, t, :], ALU.mult))
                step(V.tensor_tensor(kback, ps[:, 6 + t, :], decay[:, 1, t, :], ALU.mult))
                step(V.tensor_tensor(kplus[:, t, :], kminus[:, t, :], kback, ALU.add))
                sig(v, V.tensor_tensor(kminus[:, t, :], kminus[:, t, :], kback, ALU.subtract), "filt_sb", t + 1)

            def ada_rows(g, b, gains):
                v.wait_ge(S["ada_used"], 4 * g + 4)
                v.wait_ge(S["gain_in" if g == 0 else "ada_in"], 16 * 8)
                sig(v, V.tensor_tensor(adr[g], ps[:, b, :], adr[g], ALU.add), f"ada{g}_sb", 1)
                if gains is not None:
                    r = slice(gains, gains + 64)
                    v.wait_ge(S["gain_in"], 16 * 8)
                    sig(v, V.scalar_tensor_tensor(adr[g][r, :], adr[g][r, :], 1.0, gain[r, :], ALU.add, ALU.mult),
                        f"ada{g}_sb", 2)

            def ada_columns(g, b):
                v.wait_ge(S["mc_ps"], g + 1)
                src = ps[:, b, :].rearrange("p (j q r) -> p q j r", j=4, q=4)[:, :, :, 0]
                sig(v, V.tensor_copy(modc[:, g, :, :], src), "mc_sb", g + 1)

            def modulated(shift, scale):
                for k in range(KD // 2):
                    last = V.tensor_scalar(hT[:, k, :], ps[:, k // 2, (k % 2) * 256:(k % 2) * 256 + 256],
                                           scale(k), shift(k), ALU.mult, ALU.add)
                return last

            ada_rows(0, 3, 64)
            ada_columns(0, 5)
            v.wait_ge(S["xT_ps"], 1)
            mc = lambda g, i: modc[:, g, i // 4, i % 4:i % 4 + 1]
            modulated(lambda k: mc(0, k), lambda k: mc(0, 8 + k)).then_inc(S["h1_sb"], 1)
            v.wait_ge(S["kA_sb"], 1)
            v.wait_ge(S["kN_ps"], 1)
            step(V.tensor_copy(kN[0:1, :], ps[0:1, 4, :]))
            v.wait_ge(S["kB_ps"], 1)
            step(V.tensor_copy(kB[:, 0, :], ps[:, 5, :]))
            step(V.memset(kB[0:1, 0, :], 0.0))
            v.wait_ge(S["kB_ps"], 2)
            sig(v, V.tensor_copy(kB[:, 1, :], ps[:, 6, :]), "kf_done", 1)
            def weigh_pair(g, pair):
                for j in (2 * pair, 2 * pair + 1):
                    n = where[("ada", g, j)]
                    v.wait_ge(s_front[n % 6], 16 * (n // 6 + 1))
                    w = block_view(("ada", g, j))
                    for kk in range(2):
                        c = cs[:, 2 * j + kk, 0:1]
                        if j % 2 == 0 and kk == 0:
                            total = w[:, 0, :]
                            ins = V.tensor_scalar(total, total, c, None, ALU.mult)
                        else:
                            ins = V.scalar_tensor_tensor(total, w[:, kk, :], c, total, ALU.mult, ALU.add)
                        if j % 2 and kk:
                            ins.then_inc(S["weighted"], 1)
                        else:
                            step(ins)

            for i in range(12):
                if i == 4:
                    weigh_pair(1, 0)
                v.wait_ge(S["u_sb"], i // 2 + 1)
                wcol = lambda j: col(C_W + 12 * j + i)
                step(V.tensor_scalar(ucv[:, i, :], uraw[:, i, 1:257], wcol(1), col(C_CB + i), ALU.mult, ALU.add))
                step(V.scalar_tensor_tensor(ucv[:, i, :], uraw[:, i, 0:256], wcol(0), ucv[:, i, :], ALU.mult, ALU.add))
                step(V.scalar_tensor_tensor(ucv[:, i, :], uraw[:, i, 2:258], wcol(2), ucv[:, i, :], ALU.mult, ALU.add))
            sig(v, V.tensor_tensor(vT, vT, x1T, ALU.mult), "vT_rdy", 1)
            weigh_pair(1, 1)
            ada_rows(1, 6, None)
            for pair in range(2):
                weigh_pair(2, pair)
            v.wait_ge(S["bv_in"], 16)
            for t in range(TT):
                v.wait_ge(S["u_ps"], 11 + t)
                V.tensor_tensor(ve[:, t, :], ps[:, (10 + t) % 3, :], at("bv"), ALU.add).then_inc(S["v_sb"], 1)
            ada_rows(2, 7, 0)
            v.wait_ge(S["V_ps"], 4)
            t0, t1 = flat
            for f in range(2):
                vr, vs = ps[:, 4 + f, :], ps[:, 6 + f, :]
                a2 = kN if f == 0 else kA[:, 1, :]
                step(V.tensor_tensor(t0, vr, kA[:, f, :], ALU.mult))
                step(V.tensor_tensor(t1, vs, kB[:, f, :], ALU.mult))
                step(V.tensor_tensor(Y[:, f, :], t0, t1, ALU.subtract))
                step(V.tensor_tensor(t0, vr, kB[:, f, :], ALU.mult))
                step(V.tensor_tensor(t1, vs, a2, ALU.mult))
                sig(v, V.tensor_tensor(Y[:, 2 + f, :], t0, t1, ALU.add), "Y_rdy", f + 1)
            v.wait_ge(S["yT_ps"], 1)
            for c in range(CT):
                step(V.scalar_tensor_tensor(vT[:, c, :], vT[:, c, :], col(C_DS + c),
                                            ps[:, 6 + c // 2, (c % 2) * 256:(c % 2) * 256 + 256], ALU.mult, ALU.add))
            sig(v, V.tensor_tensor(y_hyT, x0T, vT, ALU.mult), "yhy_rdy", 1)
            ada_columns(1, 0)
            ada_columns(2, 1)
            gs_cols = at("modc", 32, KD).unsqueeze(2).to_broadcast([P, KD, E])
            v.wait_ge(S["rb_ps"], 1)
            v.wait_ge(S["br_in"], 16)
            sig(v, V.tensor_tensor(at("br"), at("br"), ps[:, 1, 0:E], ALU.add), "rb_sb", 1)
            sig(v, V.tensor_tensor(wr_scaled, wr, gs_cols, ALU.mult), "rb_sb", 2)

            v.wait_ge(S["lam_e"], 1)
            step(V.tensor_tensor(lamcol, lam2[:, 1:2], lam2[:, 0:1], ALU.subtract))
            step(V.tensor_scalar(lamcol, lamcol, -LAM_INIT, None, ALU.add))

            def logits(j):
                t, h = j // HEADS, j % HEADS
                s = sc[j % 2]
                v.wait_ge(S["s_ps"], j + 1)
                d = dist[:, t, :].unsqueeze(1).to_broadcast([P, 2, L])
                sig(v, V.scalar_tensor_tensor(s, d, -8.0 * SLOPES[h], ps[:, 4 + j % 2, :].rearrange("p (c k) -> p c k", c=2),
                                              ALU.mult, ALU.add), "s_sb", j + 1)
                m = negm[:, 2 * (j % 2):2 * (j % 2) + 2]
                step(V.tensor_reduce(m, s, AX.X, ALU.max))
                V.tensor_scalar(m, m, -0.125, None, ALU.mult).then_inc(S["negm_rdy"], 1)

            def difference(j):
                s, o = sc[j % 2], 2 * (j % 2)
                v.wait_ge(S["exp_done"], j + 1)
                step(V.reciprocal(rinv[:, o:o + 2], sums[:, o:o + 2]))
                step(V.tensor_tensor(rlam[:, j % 2:j % 2 + 1], rinv[:, o + 1:o + 2], lamcol, ALU.mult))
                step(V.tensor_scalar(s[:, 1, :], s[:, 1, :], rlam[:, j % 2:j % 2 + 1], None, ALU.mult))
                if j >= 2:
                    v.wait_ge(S["aT_ps"], j - 1)
                sig(v, V.scalar_tensor_tensor(ab[j % 2], s[:, 0, :], rinv[:, o:o + 1], s[:, 1, :], ALU.mult, ALU.add),
                    "a_rdy", j + 1)

            def turned(j):
                v.wait_ge(S["aT_ps"], j + 1)
                if j >= 2:
                    v.wait_ge(S["o_ps"], j - 1)
                V.tensor_copy(aT[j % 2].rearrange("p k q -> p (k q)"), ps[:, 3, (j % 2) * 256:(j % 2) * 256 + 256])\
                    .then_inc(S["aT_sb"], 1)

            def head_norm(t):
                v.wait_ge(S["o_sq"], t + 1)
                step(V.tensor_reduce(oss, at("bv").rearrange("p (h e) -> p h e", h=HEADS), AX.X, ALU.add))
                rstd(ors, oss, P)
                if t:
                    v.wait_ge(S["oT_ps"], t)
                V.tensor_tensor(on.rearrange("p (h e) -> p h e", h=HEADS),
                                ps[:, 6 + t, :].rearrange("p (h e) -> p h e", h=HEADS),
                                ors.unsqueeze(2).to_broadcast([P, HEADS, P]), ALU.mult).then_inc(S["on_rdy"], 1)

            def head_turned(t):
                v.wait_ge(S["oT_ps"], t + 1)
                V.tensor_scalar(y_atT[:, :, t * P:(t + 1) * P], ps[:, 3, :].rearrange("p (h q) -> p h q", h=HEADS),
                                col(C_SG), 1.0 - LAM_INIT, ALU.mult, ALU.mult).then_inc(S["oT_sb"], 1)

            logits(0)
            for j in range(2 * HEADS):
                if j + 1 < 2 * HEADS:
                    logits(j + 1)
                difference(j)
                turned(j)
                if j == 5:
                    head_norm(0)
            head_turned(0)
            head_norm(1)
            head_turned(1)
            mt = at("ab")
            for i in range(KD):
                v.wait_ge(S["pj_ps"], i + 1)
                v.wait_ge(S["gat_rdy"], i // 4 + 1)
                b = ps[:, pj_bank[i % 4], :]
                step(V.tensor_tensor(mt[:, 0:256], b[:, 0:256], gate_hy[:, i, :], ALU.mult))
                step(V.tensor_tensor(mt[:, 256:512], b[:, 256:512], gate_at[i], ALU.mult))
                sig(v, V.tensor_tensor(merged[:, i, :], mt[:, 0:256], mt[:, 256:512], ALU.add), "pj_sb", i + 1)
            v.wait_ge(S["bc_sb"], 2)
            for t in range(TT):
                for h in range(2):
                    v.wait_ge(S["mix_ps"], 1 if t == 0 else 2 + 2 * h)
                    step(V.tensor_tensor(flat[0], ps[:, 2 * t + h, :], gate1B[:, 512 * h:512 * (h + 1)], ALU.mult))
                    xs = x[:, t, 512 * h:512 * (h + 1)]
                    sig(v, V.tensor_tensor(xs, xs, flat[0], ALU.add), "x1_rdy", 2 * t + h + 1)
                v.wait_ge(S["x1T_ps"], 2 * t + 1)
                if t == 0:
                    step(V.tensor_copy(hT[:, 0:4, 0:P], ps[:, 4, :].rearrange("p (k t) -> p k t", k=4)))
                V.tensor_copy(hT[:, 4:8, t * P:(t + 1) * P], ps[:, 5 + 2 * t, :].rearrange("p (k t) -> p k t", k=4))\
                    .then_inc(S["x1T_dve"], 1)
                v.wait_ge(S["x1_sq"], t + 1)
                rstd(rs[:, t:t + 1], ss[:, t:t + 1], D, S["rs_rdy"])
            v.wait_ge(S["log_ps"], 1)
            v.wait_ge(S["rs_rdy"], TT)
            for t in range(TT):
                step(V.scalar_tensor_tensor(log[:, t, :], ps[:, 5, E * t:E * t + E], rs[:, t:t + 1], at("br"),
                                            ALU.mult, ALU.add))
            for k in range(TOPK):
                step(V.tensor_reduce(topv[:, k, :], log, AX.X, ALU.max))
                for t in range(TT):
                    ins = V.scalar_tensor_tensor(wrk[:, t, :], log[:, t, :], topv[:, k, t:t + 1], tab("erev"),
                                                 ALU.is_ge, ALU.mult)
                    step.start(ins) if t == 0 else step(ins)
                step(V.tensor_reduce(km, wrk, AX.X, ALU.max))
                step(V.tensor_tensor(oh[:, k, :, :], wrk, km.unsqueeze(2).to_broadcast([P, TT, E]), ALU.is_equal))
                if k < TOPK - 1:
                    step(V.scalar_tensor_tensor(log, oh[:, k, :, :], -3.0e38, log, ALU.mult, ALU.add))
            sig(v, V.tensor_reduce(M, oh.rearrange("p k t e -> p t e k"), AX.X, ALU.add), "m_rdy", 1)
            sig(v, V.tensor_tensor(gexp, topv, topv[:, 0, :].unsqueeze(1).to_broadcast([P, TOPK, TT]), ALU.subtract),
                "top_rdy", 1)
            v.wait_ge(S["rank_ps"], 1)
            step(V.tensor_copy(rank, ps[:, 5, 128:192].rearrange("p (t e) -> p t e", t=TT)))
            for t in range(TT):
                for e in range(2):
                    last = V.tensor_scalar(Sel[:, t, e * SLOTS:(e + 1) * SLOTS], iota[:, 0:SLOTS],
                                           rank[:, t, e:e + 1], M[:, t, e:e + 1], ALU.is_equal, ALU.mult)
                    if (t, e) == (TT - 1, 1):
                        v.wait_ge(S["dve_step"], step.n)
                        last.then_inc(S["sel_rdy"], 1)
                    else:
                        step.start(last)

            def rows_of(p):
                src = ohI[:, bass.ds(p * 2, 2)] if not isinstance(p, int) else ohI[:, 2 * p:2 * p + 2]
                V.tensor_copy(mask, src.unsqueeze(2).to_broadcast([P, 2, SLOTS])).then_inc(S["mask_rdy"], 1)

            rows_of(0)

            def blocks_beyond(dst, cnt, tmp, signal=None):
                step(V.tensor_scalar(dst, cnt, 64.0, None, ALU.is_gt))
                for n, edge in enumerate((128.0, 192.0)):
                    step(V.tensor_scalar(tmp, cnt, edge, None, ALU.is_gt))
                    ins = V.tensor_tensor(dst, dst, tmp, ALU.add)
                    sig(v, ins, signal, n + 1) if signal else step(ins)

            v.wait_ge(S["cnt_ps"], 1)
            blocks_beyond(cntT2[0:E, :], ps[0:E, 2, 128:256], cntT[0:E, :], "cnt_sb")
            blocks_beyond(nov, ps[:, 2, 0:32], tmpe)

            def positions():
                v.wait_ge(S["ex_ps"], 1)
                step(V.tensor_copy(exc, ps[:, 3, 0:48]))
                step(V.tensor_tensor(inc, exc[:, 0:E], nov, ALU.add))
                step(V.tensor_tensor(tmpe, exc[:, 0:E], tab("item")[:, 0:E], ALU.subtract))
                step(V.tensor_scalar(tmpe, tmpe, 31.0, None, ALU.add))
                wide = lambda c: c.unsqueeze(1).to_broadcast([P, TT, E])
                step(V.tensor_scalar(wrk, rank, 64.0, None, ALU.is_ge))
                step(V.tensor_tensor(wrk, wrk, wide(tmpe), ALU.mult))
                step(V.tensor_tensor(wrk, wrk, wide(tab("item")[:, 0:E]), ALU.add))
                step(V.scalar_tensor_tensor(wrk2, wrk, 64.0, rank, ALU.mult, ALU.add))
                for k in range(TOPK):
                    step(V.tensor_tensor(pos_k[:, k, :, :], oh[:, k, :, :], wrk2, ALU.mult))
                step(V.tensor_reduce(pk, pos_k, AX.X, ALU.add))

            def activate(i, st):
                v.wait_ge(S["gu_used"], i * 8 + 8)
                sig(v, V.tensor_scalar(g_sb, ps[:, 4, :], 7.0, None, ALU.min), "g_rdy", i + 1)
                st(V.tensor_scalar(u_sb, ps[:, 5, :], 7.0, -7.0, ALU.min, ALU.max))
                st(V.scalar_tensor_tensor(t_sb, u_sb, 1.0, g_sb, ALU.add, ALU.mult))
                v.wait_ge(S["sig_rdy"], i + 1)
                V.tensor_tensor(act_o, t_sb, s_sb, ALU.mult).then_inc(S["act_rdy"], 1)

            def select(st):
                for k in range(TOPK):
                    for t in range(TT):
                        s = pk[:, k, t:t + 1]
                        if k == 0:
                            ins = V.tensor_scalar(Sel[:, t, :], iota, s, None, ALU.is_equal)
                        else:
                            ins = V.scalar_tensor_tensor(Sel[:, t, :], iota, s, Sel[:, t, :], ALU.is_equal, ALU.add)
                        if k == TOPK - 1 and t == TT - 1:
                            ins.then_inc(S["sel_rdy"], 1)
                        else:
                            st(ins)

            def weigh(st):
                for k in range(TOPK):
                    for t in range(TT):
                        dst = Wt if k == 0 else Wtmp
                        st(V.tensor_scalar(dst[:, t, :], iota, pk[:, k, t:t + 1], gk[:, k, t:t + 1],
                                           ALU.is_equal, ALU.mult))
                    if k == TOPK - 1:
                        V.tensor_tensor(Wt, Wt, Wtmp, ALU.add).then_inc(S["wt_rdy"], 1)
                    elif k:
                        st(V.tensor_tensor(Wt, Wt, Wtmp, ALU.add))

            def advance(st):
                st(V.tensor_scalar(pk, pk, -128.0, None, ALU.add))

            def gathered(p):
                for half in range(2):
                    v.wait_ge(S["ga_done"], p * 2 + (half + 1))
                    V.tensor_copy(hTp[:, 4 * half:4 * half + 4, :].rearrange("p k s -> p (k s)"), ps[:, 7 - half, :])\
                        .then_inc(S["ga_sb"], 1)

            def placed(p):
                v.wait_ge(S["pt_done"], p + 1)
                V.tensor_copy(Pw.rearrange("p t q -> p (t q)"), ps[:, 7, 0:256]).then_inc(S["pt_sb"], 1)

            gathered(0)
            positions()
            v.wait_ge(S["top_exp"], 1)
            step(V.tensor_tensor(gsum, gexp[:, 0, :], gexp[:, 1, :], ALU.add))
            step(V.tensor_tensor(gsum, gsum, gexp[:, 2, :], ALU.add))
            step(V.tensor_tensor(gsum, gsum, gexp[:, 3, :], ALU.add))
            step(V.reciprocal(gden, gsum))
            step(V.tensor_tensor(gk, gexp, gden.unsqueeze(1).to_broadcast([P, TOPK, TT]), ALU.mult))
            for k in range(TOPK):
                g2 = gk[:, k, :].unsqueeze(2).to_broadcast([P, TT, E])
                if k == 0:
                    sig(v, V.tensor_tensor(G, oh[:, 0, :, :], g2, ALU.mult), "g_all", 1)
                else:
                    step(V.tensor_tensor(wrk, oh[:, k, :, :], g2, ALU.mult))
                    sig(v, V.tensor_tensor(G, G, wrk, ALU.add), "g_all", k + 1)
            step(V.tensor_tensor(cmpI, inc.unsqueeze(1).to_broadcast([P, EXTRA, E]),
                                 tab("item")[:, 0:EXTRA].unsqueeze(2).to_broadcast([P, EXTRA, E]), ALU.is_le))
            step(V.tensor_reduce(ef[:, E:ITEMS], cmpI, AX.X, ALU.add))
            step(V.tensor_scalar(ef[:, E:ITEMS], ef[:, E:ITEMS], float(E - 1), None, ALU.min))
            step(V.memset(ohI[:, ITEMS:ITEMS + 2], 0.0))
            step(V.tensor_scalar(ohI[:, E:ITEMS], ef[:, E:ITEMS], lane, None, ALU.is_equal))
            step(V.tensor_scalar(tmpe[:, 0:8], tab("odd"), exc[:, 40:41], None, ALU.is_le))
            step(V.tensor_reduce(pairs_f[:, 0:1], tmpe[:, 0:8], AX.X, ALU.add))
            step(V.tensor_scalar(pairs_f[:, 0:1], pairs_f[:, 0:1], float(E // 2), None, ALU.add))
            sig(v, V.tensor_copy(table_i[0:1, 0:ITEMS], ef[0:1, :]), "tables", 1)
            for n in range(1, 3):
                step(V.tensor_scalar(pairs_f[:, n:n + 1], pairs_f[:, 0:1], -float(n), None, ALU.add))
            sig(v, V.tensor_copy(table_i[0:1, 48:51], pairs_f[0:1, 0:3]), "tables", 2)
            activate(0, step)
            weigh(step)
            advance(step)
            v.wait_ge(S["sel_rdy"], 1)
            select(step)
            activate(1, step)
            v.wait_ge(S["gu_used"], 16)
            rows_of(1)
            gathered(1)
            placed(0)
            v.wait_ge(S["tables"], 2)
            n_pairs = v.value_load(table_i[0:1, 48:49], min_val=E // 2, max_val=ITEMS // 2)
            PER = 2 * 2 + (TOPK * TT + TOPK - 2) + 1 + (TOPK * TT - 1)
            with v.Fori(1, n_pairs) as p:
                st = Steps(v, S["dve_loop"], p * PER - PER)
                activate(p * 2, st)
                v.wait_ge(S["pt_done"], p)
                weigh(st)
                v.wait_ge(S["wt_rdy"], p + 1)
                advance(st)
                v.wait_ge(S["ga_done"], p * 2 + 2)
                select(st)
                activate(p * 2 + 1, st)
                rows_of(p + 1)
                gathered(p + 1)
                placed(p)
                assert st.n == PER, (st.n, PER)
            v.wait_ge(S["fg_in"], 16)
            v.wait_ge(S["bc_sb"], 8)
            for t in range(TT):
                if t < TT - 1:
                    v.wait_ge(S["sc_tile"], t + 1)
                else:
                    v.wait_ge(S["sc_done"], n_pairs)
                for h in range(2):
                    step(V.tensor_tensor(u_sb, ps[:, 2 * t + h, :], gate2B[:, 512 * h:512 * (h + 1)], ALU.mult))
                    xs = x[:, t, 512 * h:512 * (h + 1)]
                    sig(v, V.tensor_tensor(xs, xs, u_sb, ALU.add), "x2_rdy", 2 * t + h + 1)
            v.wait_ge(S["fin_sq"], TT)
            rstd(rs, ss, D)
            for t in range(TT):
                V.scalar_tensor_tensor(fin[:, t, :], x[:, t, :], rs[:, t:t + 1], fgB, ALU.mult, ALU.mult)\
                    .then_inc(S["fin_rdy"], 1)


def kernel(**inputs):
    import numpy as np
    import concourse.bacc as bacc
    from concourse.bass_utils import run_bass_kernel_spmd

    nc = bacc.Bacc("TRN2", target_bir_lowering=False, num_devices=1)
    arrays, aps = {}, {}
    for name, value in list(inputs.items()) + list(host_tables().items()):
        v = np.ascontiguousarray(value)
        arrays["in_" + name] = v
        aps[name] = nc.dram_tensor("in_" + name, v.shape, mybir.dt.from_np(v.dtype), kind="ExternalInput").ap()
    out = nc.dram_tensor("out_0", (1, L, D), F32, kind="ExternalOutput").ap()
    build(nc, aps, out)
    r = run_bass_kernel_spmd(nc, [arrays], core_ids=[0])
    return r.results[0]["out_0"]
```
